# Optimizing a Trainium2 kernel written in Bass

```python
import math
import jax, jax.numpy as jnp
from jax import lax
import numpy as np

D_MODEL = 1024
BATCH = 1
SEQ = 512
DEPTH = 1

N_HEADS = 16
N_KV_HEADS = 2
GROUP = N_HEADS // N_KV_HEADS
HEAD_DIM = 64
WINDOW = 128
BLOCK = 128
ATTN_SCALE = 1.0 / math.sqrt(HEAD_DIM)
NEG_INF = -1e30
POOL_WINDOWS = (2, 4, 8, 16)
N_POOL_GROUPS = len(POOL_WINDOWS)
POOL_GROUP = 128
POOL_W = N_POOL_GROUPS * POOL_GROUP
Q_W = N_HEADS * HEAD_DIM
KV_W = N_KV_HEADS * HEAD_DIM
IN_W = Q_W + 2 * KV_W + POOL_W + 2 * D_MODEL
SPLITS = (Q_W, Q_W + KV_W, Q_W + 2 * KV_W, Q_W + 2 * KV_W + POOL_W, Q_W + 2 * KV_W + POOL_W + D_MODEL)
PEER_HEADS = 8
N_KEYS = 128
N_EXPERTS = N_KEYS * N_KEYS
D_KEY = 256
D_HALF = D_KEY // 2
PEER_TOPK = 16
PEER_CHUNK = 128
EPS = 1e-5


def rmsnorm(x, g):
    xf = x.astype(jnp.float32)
    y = xf * lax.rsqrt(jnp.mean(xf * xf, axis=-1, keepdims=True) + EPS)
    return (y * g.astype(jnp.float32)).astype(x.dtype)

def sliding_window_attention(q, k, v, sinks):
    b, s = q.shape[0], q.shape[1]
    nblk = s // BLOCK
    kp = jnp.pad(k, ((0, 0), (BLOCK, 0), (0, 0), (0, 0)))
    vp = jnp.pad(v, ((0, 0), (BLOCK, 0), (0, 0), (0, 0)))
    qb = q.reshape(b, nblk, BLOCK, N_KV_HEADS, GROUP, HEAD_DIM).swapaxes(0, 1)
    sink = sinks.astype(jnp.float32).reshape(1, N_KV_HEADS, GROUP, 1, 1)

    def one_block(args):
        i, qi = args
        start = i * BLOCK
        kb = lax.dynamic_slice_in_dim(kp, start, 2 * BLOCK, axis=1)
        vb = lax.dynamic_slice_in_dim(vp, start, 2 * BLOCK, axis=1)
        sc = jnp.einsum('bqhgd,bkhd->bhgqk', qi, kb).astype(jnp.float32) * ATTN_SCALE
        qpos = start + jnp.arange(BLOCK)
        kpos = start - BLOCK + jnp.arange(2 * BLOCK)
        rel = qpos[:, None] - kpos[None, :]
        mask = (rel >= 0) & (rel < WINDOW) & (kpos[None, :] >= 0)
        sc = jnp.where(mask, sc, NEG_INF)
        sc = jnp.concatenate([sc, jnp.broadcast_to(sink, sc.shape[:-1] + (1,))], axis=-1)
        p = jax.nn.softmax(sc, axis=-1)[..., :-1]
        return jnp.einsum('bhgqk,bkhd->bqhgd', p.astype(vb.dtype), vb)

    o = lax.map(one_block, (jnp.arange(nblk), qb))
    return o.swapaxes(0, 1).reshape(b, s, Q_W)

def multiscale_pool(p, w_grp, scale):
    b, s = p.shape[0], p.shape[1]
    pf = p.astype(jnp.float32).reshape(b, s, N_POOL_GROUPS, POOL_GROUP)
    c = jnp.cumsum(pf, axis=1)
    t1 = jnp.arange(1, s + 1, dtype=jnp.float32)
    outs = []
    for j, w in enumerate(POOL_WINDOWS):
        cj = c[:, :, j]
        lag = jnp.pad(cj, ((0, 0), (w, 0), (0, 0)))[:, :s]
        cnt = jnp.minimum(t1, float(w))[None, :, None]
        outs.append((cj - lag) / cnt - pf[:, :, j])
    pooled = jnp.stack(outs, axis=2).astype(p.dtype)
    y = jnp.einsum('bsgc,gcd->bsgd', pooled, w_grp).reshape(b, s, POOL_W)
    return y * scale

def peer(xn, w_query, sub_keys, u_tab, v_tab):
    b, s, d = xn.shape
    xt = xn.reshape((b * s) // PEER_CHUNK, PEER_CHUNK, d)

    def chunk(xc):
        c = xc.shape[0]
        q = (xc @ w_query).reshape(c, PEER_HEADS, 2, D_HALF)
        sc = jnp.einsum('chpd,hpkd->chpk', q, sub_keys).astype(jnp.float32)
        sv, si = lax.top_k(sc, PEER_TOPK)
        cand = (sv[:, :, 0, :, None] + sv[:, :, 1, None, :]).reshape(c, PEER_HEADS, PEER_TOPK * PEER_TOPK)
        cidx = (si[:, :, 0, :, None] * N_KEYS + si[:, :, 1, None, :]).reshape(c, PEER_HEADS, PEER_TOPK * PEER_TOPK)
        fv, fi = lax.top_k(cand, PEER_TOPK)
        idx = jnp.take_along_axis(cidx, fi, axis=-1)
        g = jax.nn.softmax(fv, axis=-1)
        u = u_tab[idx]
        a = jax.nn.gelu(jnp.einsum('chkd,cd->chk', u, xc).astype(jnp.float32), approximate=False)
        vv = v_tab[idx]
        return jnp.einsum('chk,chkd->cd', (g * a).astype(vv.dtype), vv)

    return lax.map(chunk, xt).reshape(b, s, d)

def first_inputs(seed: int = 0) -> dict:
    key = jax.random.key(seed)
    ks = jax.random.split(key, 16)
    f32 = jnp.float32
    L = DEPTH
    nrm = lambda k, shape, std: jax.random.normal(k, shape, f32) * std
    return {
        'x': jax.random.normal(ks[0], (BATCH, SEQ, D_MODEL), f32),
        'ln_mix_g': 1.0 + nrm(ks[1], (L, D_MODEL), 0.05),
        'w_in': nrm(ks[2], (L, D_MODEL, IN_W), D_MODEL ** -0.5),
        'b_in': nrm(ks[3], (L, IN_W), 0.02),
        'attn_sinks': nrm(ks[4], (L, N_HEADS), 0.5),
        'w_attn_up': nrm(ks[5], (L, Q_W, D_MODEL), Q_W ** -0.5),
        'w_pool_grp': nrm(ks[6], (L, N_POOL_GROUPS, POOL_GROUP, POOL_GROUP), POOL_GROUP ** -0.5),
        'pool_scale': 1.0 + nrm(ks[7], (L, POOL_W), 0.1),
        'w_pool_up': nrm(ks[8], (L, POOL_W, D_MODEL), POOL_W ** -0.5),
        'w_o': nrm(ks[9], (L, D_MODEL, D_MODEL), D_MODEL ** -0.5),
        'ln_ffn_g': 1.0 + nrm(ks[10], (L, D_MODEL), 0.05),
        'w_query': nrm(ks[11], (L, D_MODEL, PEER_HEADS * D_KEY), D_MODEL ** -0.5),
        'sub_keys': nrm(ks[12], (L, PEER_HEADS, 2, N_KEYS, D_HALF), D_HALF ** -0.5),
        'u_experts': nrm(ks[13], (L, N_EXPERTS, D_MODEL), D_MODEL ** -0.5),
        'v_experts': nrm(ks[14], (L, N_EXPERTS, D_MODEL), PEER_HEADS ** -0.5),
        'ln_final_g': 1.0 + nrm(ks[15], (D_MODEL,), 0.05),
    }

def first_block(x, ln_mix_g, w_in, b_in, attn_sinks, w_attn_up, w_pool_grp, pool_scale, w_pool_up, w_o,
              ln_ffn_g, w_query, sub_keys, u_experts, v_experts, ln_final_g):
    b, s, _ = x.shape
    h = x
    for l in range(DEPTH):
        xn = rmsnorm(h, ln_mix_g[l])
        z = xn @ w_in[l] + b_in[l]
        q, k, v, pz, ga, gp = jnp.split(z, SPLITS, axis=-1)
        q = q.reshape(b, s, N_KV_HEADS, GROUP, HEAD_DIM)
        k = k.reshape(b, s, N_KV_HEADS, HEAD_DIM)
        v = v.reshape(b, s, N_KV_HEADS, HEAD_DIM)
        y_a = sliding_window_attention(q, k, v, attn_sinks[l]) @ w_attn_up[l]
        y_p = multiscale_pool(pz, w_pool_grp[l], pool_scale[l]) @ w_pool_up[l]
        merged = jax.nn.sigmoid(ga) * y_a + jax.nn.sigmoid(gp) * y_p
        h = h + merged @ w_o[l]
        h = h + peer(rmsnorm(h, ln_ffn_g[l]), w_query[l], sub_keys[l], u_experts[l], v_experts[l])
    return rmsnorm(h, ln_final_g)


MIX_WIDTH = D_MODEL
ATTN_WIDTH = MIX_WIDTH // 2
ATTN_HEADS = ATTN_WIDTH // HEAD_DIM
SGU_WIDTH = MIX_WIDTH - ATTN_WIDTH
SGU_GROUP_DIM = 64
SGU_GROUPS = SGU_WIDTH // SGU_GROUP_DIM
SGU_CHUNK = 128
DILATED_PATTERNS = ((128, 1), (512, 4), (2048, 16))
BLOCK_Q = 128
ROPE_THETA = 500000.0
ROT_DIM = HEAD_DIM // 4
ROT_HALF = ROT_DIM // 2
D_FF = ((8 * D_MODEL // 3 + 255) // 256) * 256
IN_PROJ_WIDTH = 3 * ATTN_WIDTH + 2 * SGU_WIDTH
RMS_EPS = 1e-6
LN_EPS = 1e-5


def rms_norm(x, gain):
    xf = x.astype(jnp.float32)
    y = xf * lax.rsqrt(jnp.mean(xf * xf, axis=-1, keepdims=True) + RMS_EPS)
    return (y * gain.astype(jnp.float32)).astype(x.dtype)

def layer_norm(x, gain, bias):
    xf = x.astype(jnp.float32)
    mu = jnp.mean(xf, axis=-1, keepdims=True)
    xc = xf - mu
    y = xc * lax.rsqrt(jnp.mean(xc * xc, axis=-1, keepdims=True) + LN_EPS)
    return (y * gain.astype(jnp.float32) + bias.astype(jnp.float32)).astype(x.dtype)

def partial_rotary(x, positions):
    inv_freq = ROPE_THETA ** (-jnp.arange(0, ROT_DIM, 2, dtype=jnp.float32) / ROT_DIM)
    ang = positions.astype(jnp.float32)[:, :, None, None] * inv_freq
    cos, sin = jnp.cos(ang), jnp.sin(ang)
    xf = x.astype(jnp.float32)
    x1 = xf[..., :ROT_HALF]
    x2 = xf[..., ROT_HALF:ROT_DIM]
    out = jnp.concatenate([x1 * cos - x2 * sin, x2 * cos + x1 * sin, xf[..., ROT_DIM:]], axis=-1)
    return out.astype(x.dtype)

def dilated_window_attention(q, k, v, window, dilation):
    B, H, S, Dh = q.shape
    L = S // dilation
    W = window // dilation
    nblk = -(-L // BLOCK_Q)
    Lp = nblk * BLOCK_Q

    def strided(t):
        return t.reshape(B, H, L, dilation, Dh).transpose(0, 1, 3, 2, 4)

    qs, ks, vs = strided(q), strided(k), strided(v)
    qs = jnp.pad(qs, ((0, 0), (0, 0), (0, 0), (0, Lp - L), (0, 0)))
    kv_pad = ((0, 0), (0, 0), (0, 0), (W, Lp - L), (0, 0))
    kp = jnp.pad(ks, kv_pad)
    vp = jnp.pad(vs, kv_pad)
    blk = jnp.arange(nblk)[:, None]
    col = jnp.arange(BLOCK_Q + W)[None, :]
    idx = blk * BLOCK_Q + col
    kb = kp[:, :, :, idx]
    vb = vp[:, :, :, idx]
    qb = qs.reshape(B, H, dilation, nblk, BLOCK_Q, Dh)

    scale = 1.0 / np.sqrt(HEAD_DIM)
    s = jnp.einsum('bhrnqd,bhrnkd->bhrnqk', qb, kb,
                   preferred_element_type=jnp.float32) * scale
    row = jnp.arange(BLOCK_Q)[:, None]
    dist = row + W - jnp.arange(BLOCK_Q + W)[None, :]
    key_pos = jnp.arange(nblk)[:, None, None] * BLOCK_Q + jnp.arange(BLOCK_Q + W)[None, None, :] - W
    mask = (dist >= 0)[None] & (dist <= W)[None] & (key_pos >= 0)
    s = jnp.where(mask, s, jnp.finfo(jnp.float32).min)
    m = jnp.max(s, axis=-1, keepdims=True)
    p = jnp.exp(s - m)
    denom = jnp.sum(p, axis=-1, keepdims=True)
    o = jnp.einsum('bhrnqk,bhrnkd->bhrnqd', p, vb.astype(jnp.float32)) / denom
    lse = (m + jnp.log(denom))[..., 0]
    o = o.reshape(B, H, dilation, Lp, Dh)[:, :, :, :L]
    lse = lse.reshape(B, H, dilation, Lp)[:, :, :, :L]
    o = o.transpose(0, 1, 3, 2, 4).reshape(B, H, S, Dh)
    lse = lse.transpose(0, 1, 3, 2).reshape(B, H, S)
    return o, lse

def dilated_mixture_attention(q, k, v):
    outs, lses = [], []
    for window, dilation in DILATED_PATTERNS:
        o, lse = dilated_window_attention(q, k, v, window, dilation)
        outs.append(o)
        lses.append(lse)
    wts = jax.nn.softmax(jnp.stack(lses, axis=0), axis=0)
    o = jnp.sum(wts[..., None] * jnp.stack(outs, axis=0), axis=0)
    return o.astype(q.dtype)

def spatial_gating(u, v, ln_gain, ln_bias, w_spatial, b_spatial):
    B, S, _ = u.shape
    u = jax.nn.gelu(u, approximate=False)
    v = layer_norm(jax.nn.gelu(v, approximate=False), ln_gain, ln_bias)
    vc = v.reshape(B, S // SGU_CHUNK, SGU_CHUNK, SGU_GROUPS, SGU_GROUP_DIM)
    causal = jnp.tril(jnp.ones((SGU_CHUNK, SGU_CHUNK), dtype=bool))
    w = jnp.where(causal[None], w_spatial, 0.0).astype(v.dtype)
    mixed = jnp.einsum('gij,bnjgc->bnigc', w, vc) + b_spatial.T[:, :, None].astype(v.dtype)
    return u * mixed.reshape(B, S, SGU_WIDTH)

def second_inputs(seed: int = 0) -> dict:
    key = jax.random.key(seed)
    ks = jax.random.split(key, 20)
    f32 = jnp.float32

    def nrm(k, shape, scale):
        return jax.random.normal(k, shape, f32) * scale

    def gain(k, width):
        return 1.0 + 0.05 * jax.random.normal(k, (DEPTH, width), f32)

    x = jax.random.normal(ks[0], (BATCH, SEQ, D_MODEL), f32)
    offsets = jax.random.randint(ks[1], (BATCH, 1), 0, 4096, dtype=jnp.int32)
    positions = (jnp.arange(SEQ, dtype=jnp.int32)[None, :] + offsets).astype(jnp.int32)
    return {
        "x": x,
        "positions": positions,
        "pre_mix_norm": gain(ks[2], D_MODEL),
        "w_in": nrm(ks[3], (DEPTH, D_MODEL, IN_PROJ_WIDTH), D_MODEL ** -0.5),
        "sgu_ln_gain": gain(ks[4], SGU_WIDTH),
        "sgu_ln_bias": nrm(ks[5], (DEPTH, SGU_WIDTH), 0.02),
        "sgu_w_spatial": nrm(ks[6], (DEPTH, SGU_GROUPS, SGU_CHUNK, SGU_CHUNK), 0.5 * SGU_CHUNK ** -0.5),
        "sgu_b_spatial": 1.0 + nrm(ks[7], (DEPTH, SGU_GROUPS, SGU_CHUNK), 0.1),
        "attn_out_norm": gain(ks[8], ATTN_WIDTH),
        "sgu_out_norm": gain(ks[9], SGU_WIDTH),
        "w_out": nrm(ks[10], (DEPTH, MIX_WIDTH, D_MODEL), MIX_WIDTH ** -0.5),
        "post_mix_norm": gain(ks[11], D_MODEL),
        "pre_ffn_norm": gain(ks[12], D_MODEL),
        "w_gate": nrm(ks[13], (DEPTH, D_MODEL, D_FF), D_MODEL ** -0.5),
        "w_up": nrm(ks[14], (DEPTH, D_MODEL, D_FF), D_MODEL ** -0.5),
        "w_down": nrm(ks[15], (DEPTH, D_FF, D_MODEL), D_FF ** -0.5),
        "post_ffn_norm": gain(ks[16], D_MODEL),
    }

def second_block(x, positions, pre_mix_norm, w_in, sgu_ln_gain, sgu_ln_bias, sgu_w_spatial,
              sgu_b_spatial, attn_out_norm, sgu_out_norm, w_out, post_mix_norm,
              pre_ffn_norm, w_gate, w_up, w_down, post_ffn_norm):
    B, S, _ = x.shape
    for l in range(DEPTH):
        h = rms_norm(x, pre_mix_norm[l])
        proj = h @ w_in[l]
        q, k, v_a, u, v_s = jnp.split(
            proj, [ATTN_WIDTH, 2 * ATTN_WIDTH, 3 * ATTN_WIDTH, 3 * ATTN_WIDTH + SGU_WIDTH], axis=-1)
        q = partial_rotary(q.reshape(B, S, ATTN_HEADS, HEAD_DIM), positions).transpose(0, 2, 1, 3)
        k = partial_rotary(k.reshape(B, S, ATTN_HEADS, HEAD_DIM), positions).transpose(0, 2, 1, 3)
        v_a = v_a.reshape(B, S, ATTN_HEADS, HEAD_DIM).transpose(0, 2, 1, 3)
        attn = dilated_mixture_attention(q, k, v_a)
        attn = attn.transpose(0, 2, 1, 3).reshape(B, S, ATTN_WIDTH)
        sgu = spatial_gating(u, v_s, sgu_ln_gain[l], sgu_ln_bias[l],
                             sgu_w_spatial[l], sgu_b_spatial[l])
        mixed = jnp.concatenate([rms_norm(attn, attn_out_norm[l]),
                                 rms_norm(sgu, sgu_out_norm[l])], axis=-1)
        y = mixed @ w_out[l]
        x = x + rms_norm(y, post_mix_norm[l])
        h = rms_norm(x, pre_ffn_norm[l])
        f = (jax.nn.silu(h @ w_gate[l]) * (h @ w_up[l])) @ w_down[l]
        x = x + rms_norm(f, post_ffn_norm[l])
    return x


def setup_inputs(seed=0):
    out = dict(first_inputs(seed))
    for name, value in second_inputs(seed + 1).items():
        if name != "x":
            out[name + "_2"] = value
    return out


def reference(
    x, ln_mix_g, w_in, b_in, attn_sinks, w_attn_up, w_pool_grp, pool_scale, w_pool_up, w_o,
    ln_ffn_g, w_query, sub_keys, u_experts, v_experts, ln_final_g, positions_2, pre_mix_norm_2,
    w_in_2, sgu_ln_gain_2, sgu_ln_bias_2, sgu_w_spatial_2, sgu_b_spatial_2, attn_out_norm_2,
    sgu_out_norm_2, w_out_2, post_mix_norm_2, pre_ffn_norm_2, w_gate_2, w_up_2, w_down_2,
    post_ffn_norm_2,
):
    x = first_block(
        x, ln_mix_g, w_in, b_in, attn_sinks, w_attn_up, w_pool_grp, pool_scale, w_pool_up, w_o,
        ln_ffn_g, w_query, sub_keys, u_experts, v_experts, ln_final_g,
    )
    return second_block(
        x, positions_2, pre_mix_norm_2, w_in_2, sgu_ln_gain_2, sgu_ln_bias_2, sgu_w_spatial_2,
        sgu_b_spatial_2, attn_out_norm_2, sgu_out_norm_2, w_out_2, post_mix_norm_2,
        pre_ffn_norm_2, w_gate_2, w_up_2, w_down_2, post_ffn_norm_2,
    )


_drawn_inputs = setup_inputs


def setup_inputs(seed=0):
    import zlib

    import numpy as np

    out = dict(_drawn_inputs(seed))
    spreads = {}
    factors = {'attn_sinks': 5.386, 'sgu_ln_gain_2': 6.123, 'sgu_ln_bias_2': 33.727}
    for name, (base, spread) in spreads.items():
        noise = np.random.default_rng([zlib.crc32(name.encode()), seed]).standard_normal(out[name].shape)
        drawn = base * np.exp(spread * noise) if base else spread * noise
        out[name] = __import__('jax').numpy.asarray(drawn.astype(out[name].dtype))
    for name, factor in factors.items():
        out[name] = (out[name] * factor).astype(out[name].dtype)
    return out
```

```python
from contextlib import ExitStack

import numpy as np

import concourse.bass as bass
from concourse import mybir

F32, F32R, I32, U32 = mybir.dt.float32, mybir.dt.float32r, mybir.dt.int32, mybir.dt.uint32
ALU, ACT, AX = mybir.AluOpType, mybir.ActivationFunctionType, mybir.AxisListType

P = 128
SEQ, D = 512, 1024
TILES = SEQ // P
CHUNKS = D // P
ITEM = 2048
RAW, SPLIT = 3, 3

HEADS, KV_HEADS, DH = 16, 2, 64
Q_W, KV_W, POOL_W = HEADS * DH, KV_HEADS * DH, 512
WINDOWS = (2, 4, 8, 16)
PAD = 16
EPS1 = 1e-5
SCALE = DH ** -0.5
MASKED = -1e30

PHEADS, KEYS, TOPK = 8, 128, 16
LOWEST = -3.0e38
PAIRS = PHEADS * TOPK
J = 4
GROUPS = KEYS // J
GATE_T = 32
GATE_CHUNKS = SEQ // GATE_T
AHEAD = 3

HEADS2, W2 = 8, 512
EPS2, LN_EPS = 1e-6, 1e-5
ROT_HALF = 8
FF = 2816
FF_CHUNKS = FF // P
FF_PARTS = (12, 10)

COLUMNS = [("b_q", 8), ("b_k", 2), ("b_pool", 4), ("b_ga", 8), ("b_gp", 8), ("g_mix", 8), ("g_ffn", 8),
           ("pool_scale", 4), ("g_pre_mix", 8), ("g_out", 8), ("g_pre_ffn", 8), ("b_spatial", 8)]
TABLES = [("ident", 128), ("iota", 128), ("iota_k", 16), ("window_mask", 256), ("times", 512), ("never", 512),
          ("inv_count", 64), ("inv_freq", 8)]
ROWS = [("b_v", 128), ("sinks", 16), ("g_final", 1024), ("g_post_mix", 1024), ("ln_gain", 512), ("ln_bias", 512),
        ("g_post_ffn", 1024)]


def spans(table):
    at, out = 0, {}
    for name, width in table:
        out[name] = slice(at, at + width)
        at += width
    return out, at


class Engine:

    def __init__(self, sem):
        self.sem, self.count, self.waited, self.steps = sem, 0, {}, []

    def do(self, build, *after, tell=True):
        waits = []
        for sem, value in after:
            if self.waited.get(id(sem), 0) < value:
                self.waited[id(sem)] = value
                waits.append((sem, value))
        self.steps.append((waits, build, tell))
        if tell:
            self.count += 1
            return (self.sem, self.count)

    def start_dma(self, build, sem, total, *after):
        self.do(lambda: build().then_inc(sem, 16), *after, tell=False)
        return (sem, total)

    def run(self, eng):
        for waits, build, tell in self.steps:
            for sem, value in waits:
                eng.wait_ge(sem, value)
            ins = build() if build else None
            if tell:
                ins.then_inc(self.sem, 1)


class Slot:

    def __init__(self, ap):
        self.ap, self.free = ap, ()


class Ring:
    def __init__(self, aps):
        self.slots, self.n = [Slot(a) for a in aps], 0

    def next(self):
        self.n += 1
        return self.slots[(self.n - 1) % len(self.slots)]


def build(nc, t, out):
    col, n_col = spans(COLUMNS)
    tab, n_tab = spans(TABLES)
    row, n_row = spans(ROWS)

    with ExitStack() as ctx:
        def sem(name):
            return ctx.enter_context(nc.semaphore(name))

        base = -(-nc.sbuf_base // 32) * 32
        top = [base]

        def fixed(name, shape, dt=F32):
            size = int(np.prod(shape)) * 4
            tensor = nc.alloc_sbuf_tensor_at(name, [P] + shape, dt, offset=top[0])
            top[0] += -(-size // 32) * 32
            return tensor

        columns = fixed("columns", [n_col])
        tables = fixed("tables", [n_tab])
        v_sink_rows = fixed("v_sink_rows", [144])
        neg_sinks = fixed("neg_sinks", [HEADS])
        stats = fixed("stats", [16])
        resid = fixed("resid", [TILES, D])
        xt = (fixed("xt_high", [CHUNKS, SEQ], F32R), fixed("xt_low", [CHUNKS, SEQ], F32R))
        raw_items = [fixed(f"raw_{n}", [ITEM]) for n in range(RAW)]
        split_items = [(fixed(f"high_{n}", [ITEM], F32R), fixed(f"low_{n}", [ITEM], F32R)) for n in range(SPLIT)]
        area = top[0]
        area_size = nc.sbuf_usable_end - area

        def place(name, at, shape, dt=F32):
            assert at % 32 == 0 and at + int(np.prod(shape)) * 4 <= area_size, (name, area_size)
            return nc.alloc_sbuf_tensor_at(name, [P] + shape, dt, offset=area + at)

        def column(name, c=None):
            s = col[name]
            return columns[:, s] if c is None else columns[:, s.start + c:s.start + c + 1]

        def table(name):
            return tables[:, tab[name]]

        ident = table("ident")
        banks = Ring([ctx.enter_context(nc.psum_tensor(f"bank_{n}", [P, 512], F32))[:, :] for n in range(8)])

        pe, act, dve, pool, sp = (Engine(sem(n)) for n in ("pe_done", "act_done", "dve_done", "pool_done", "sp_done"))
        V, A, T, G, S = nc.vector, nc.scalar, nc.tensor, nc.gpsimd, nc.sync

        def mm(o, l, r, start, stop, *after, tell=False):
            return pe.do(lambda: T.matmul(o, l, r, start=start, stop=stop), *after, tell=tell)

        def mm3(o, l, r, start, stop, *after, tell=False):
            mm(o, l[0], r[0], start, False, *after)
            mm(o, l[0], r[1], False, False)
            return mm(o, l[1], r[0], False, stop, tell=tell)

        def turn(o, i, *after, tell=False):
            return pe.do(lambda: T.transpose(o, i, ident), *after, tell=tell)

        def activation(o, i, f, *after, **kw):
            return act.do(lambda: A.activation(o, i, f, **kw), *after)

        def tt_op(eng, builder, o, a, b, op, *after):
            return eng.do(lambda: builder.tensor_tensor(o, a, b, op), *after)

        def vv(o, a, b, op, *after):
            return tt_op(dve, V, o, a, b, op, *after)

        def vs(o, a, s1, op0, *after, s2=None, op1=ALU.bypass):
            return dve.do(lambda: V.tensor_scalar(o, a, s1, s2, op0, op1), *after)

        def stt(o, a, s, b, op0, op1, *after):
            return dve.do(lambda: V.scalar_tensor_tensor(out=o, in0=a, scalar=s, in1=b, op0=op0, op1=op1), *after)

        def split(high, low, x, *after, low_on=None):
            h = activation(high, x, ACT.Copy, *after)
            eng, builder = low_on or (pool, G)
            return h, tt_op(eng, builder, low, x, high.bitcast(F32), ALU.subtract, h, *after)

        small_sem, x_sem = sem("small_loaded"), [sem(f"x_loaded_{n}") for n in range(TILES)]
        for n in range(TILES):
            src = t["x"][n * P:(n + 1) * P, :]
            act.start_dma(lambda n=n, src=src: A.dma_start(resid[:, n, :], src), x_sem[n], 16)
        smalls = [(columns[:, :], t["columns"]), (tables[:, :], t["tables"]),
                  (v_sink_rows[:, :], t["rows"][0:1, 0:144].to_broadcast([P, 144]))]
        for dst, src in smalls:
            act.start_dma(lambda dst=dst, src=src: A.dma_start(dst, src), small_sem, 0)
        small = (small_sem, 16 * len(smalls))
        x_in = [(x_sem[n], 16) for n in range(TILES)]
        b_v_row, sink_row = v_sink_rows[:, 0:128], v_sink_rows[:, 128:144]

        items = []
        raw_sem = [sem(f"raw_loaded_{n}") for n in range(RAW)]
        raw_free = [()] * RAW
        split_free = [()] * SPLIT
        ready = {}
        taken = [0]

        def load_item(n):
            if n >= len(items):
                return
            r = n % RAW
            width = items[n].shape[-1]
            sp.start_dma(lambda: S.dma_start(raw_items[r][:, 0:width], items[n]), raw_sem[r], 0, *raw_free[r])

        def split_item(n):
            if n >= len(items):
                return
            r, s = n % RAW, n % SPLIT
            w = items[n].shape[-1]
            ready[n] = split(split_items[s][0][:, 0:w], split_items[s][1][:, 0:w], raw_items[r][:, 0:w],
                             (raw_sem[r], 16 * (n // RAW + 1)), *split_free[s])
            raw_free[r] = ready[n]

        def take():
            n = taken[0]
            taken[0] += 1
            s = split_items[n % SPLIT]
            return n, (s[0], s[1]), ready[n]

        def give_back(n, done):
            split_free[n % SPLIT] = (done,)
            split_item(n + SPLIT)
            load_item(n + SPLIT + RAW)

        def start_stream():
            for n in range(RAW):
                load_item(n)
            for n in range(SPLIT):
                split_item(n)
                load_item(n + RAW)

        w_all = t["weights"]
        n_w = w_all.shape[0]
        peer_at = WEIGHTS_BEFORE_PEER
        for n in range(peer_at):
            items.append(w_all[n])

        def u_items(g):
            return [t["u_tiles"][m] for m in (2 * g, 2 * g + 1)]

        v_view = t["v_experts"].rearrange("(i m e) d -> m i (e d)", i=KEYS, e=2)

        def v_items(g):
            return [v_view[m] for m in (2 * g, 2 * g + 1)]

        for g in range(AHEAD):
            items += u_items(g)
        for g in range(GROUPS):
            items += v_items(g)
            if g + AHEAD < GROUPS:
                items += u_items(g + AHEAD)
        for n in range(peer_at, n_w):
            items.append(w_all[n])
        start_stream()

        def feature_major(x, chunks, finish):
            for pair in range(chunks // 2):
                n, w, there = take()
                k = x_chunks(x)
                for e in range(2):
                    bank = banks.next()
                    for c in range(k):
                        done = mm3(bank.ap, tuple(h[:, c * 256 + e * P:c * 256 + (e + 1) * P] for h in w),
                                   tuple(h[:, c, :] for h in x), c == 0, c == k - 1,
                                   *there, *bank.free, *(x_ready if c == 0 else ()), tell=(c == k - 1))
                    if e == 1:
                        give_back(n, done)
                    bank.free = (finish(2 * pair + e, bank.ap, done),)

        def x_chunks(x):
            return x[0].shape[1]

        def token_major(x, k_items, finish, k_last=4):
            out_banks = [banks.next() for _ in range(TILES)]
            for kk in range(k_items):
                n, w, there = take()
                kc = k_last if kk == k_items - 1 else 4
                dones = []
                for tile in range(TILES):
                    b = out_banks[tile]
                    for c in range(kc):
                        first, last = kk == 0 and c == 0, kk == k_items - 1 and c == kc - 1
                        done = mm3(b.ap, tuple(h[:, 4 * kk + c, tile * P:(tile + 1) * P] for h in x),
                                   tuple(h[:, c * 512:(c + 1) * 512] for h in w), first, last,
                                   *there, *x_ready, *(b.free if first else ()), tell=(c == kc - 1))
                    dones.append(done)
                give_back(n, dones[-1])
            for tile in range(TILES):
                b = out_banks[tile]
                b.free = (finish(tile, b.ap, dones[tile]),)

        NORM_AT = area_size // 32 * 32 - 12288
        normed = Ring([place(f"normed_{n}", NORM_AT + n * 4096, [D])[:, :] for n in range(2)])
        gained = Ring([place(f"gained_{n}", NORM_AT + 8192 + n * 2048, [4, P])[:, :, :] for n in range(2)])

        def inv_rms(src, width, eps, srcs_ready, extra=(), scratch=None):
            for tile in range(TILES):
                s = (scratch or normed).next()
                last = activation(s.ap[:, 0:width], src(tile), ACT.Square, *srcs_ready(tile), *s.free, *extra,
                                  accum_out=stats[:, tile:tile + 1])
                s.free = (last,)
            a = vs(stats[:, 4:8], stats[:, 0:4], 1.0 / width, ALU.mult, last, s2=eps, op1=ALU.add)
            b = activation(stats[:, 4:8], stats[:, 4:8], ACT.Sqrt, a)
            return dve.do(lambda: V.reciprocal(stats[:, 8:12], stats[:, 4:8]), b)

        def norm_turned(src, width, eps, gain, dst, chunk0, srcs_ready, dst_free=(), extra=()):
            inv = inv_rms(src, width, eps, srcs_ready, extra)
            last = ()
            for tile in range(TILES):
                s = normed.next()
                n = vs(s.ap[:, 0:width], src(tile), stats[:, 8 + tile:9 + tile], ALU.mult, inv, *s.free)
                for half in range(width // 512):
                    bank = banks.next()
                    for c in range(4):
                        f = (half * 4 + c) * P
                        turned = turn(bank.ap[:, c * P:(c + 1) * P], s.ap[:, f:f + P], n, *bank.free, small,
                                      tell=(c == 3))
                    g = gained.next()
                    c0 = col[gain].start + chunk0 + half * 4
                    scaled = vv(g.ap, bank.ap.rearrange("p (c t) -> p c t", c=4),
                                columns[:, c0:c0 + 4].unsqueeze(2).to_broadcast([P, 4, P]), ALU.mult,
                                turned, *g.free)
                    bank.free = (scaled,)
                    where = (slice(None), slice(chunk0 + half * 4, chunk0 + half * 4 + 4),
                             slice(tile * P, (tile + 1) * P))
                    last = split(dst[0][where], dst[1][where], g.ap, scaled, *dst_free, low_on=(dve, V))
                    g.free = last
                s.free = (turned,)
            return last

        x_ready = norm_turned(lambda n: resid[:, n, :], D, EPS1, "g_mix", xt, 0, lambda n: (x_in[n],))
        ns = vs(neg_sinks[:, :], sink_row, -1.0, ALU.mult, small)

        qt = place("qt", 0, [CHUNKS, SEQ])
        ot = (place("ot_high", 16384, [CHUNKS, SEQ], F32R), place("ot_low", 32768, [CHUNKS, SEQ], F32R))
        kt = place("kt", 49152, [KV_HEADS, SEQ])
        v_tok = place("v_tok", 53248, [TILES, KV_W])
        score = Ring([place(f"score_{n}", 55296 + n * 4096, [4, 256])[:, :, :] for n in range(2)])
        prob_t = Ring([place(f"prob_t_{n}", 63488 + n * 4096, [2, 512])[:, :, :] for n in range(2)])
        head_stat = Ring([place(f"head_stat_{n}", 71680 + n * 128, [5, 4])[:, :, :] for n in range(3)])
        o_tmp = Ring([place(f"o_tmp_{n}", 72064 + n * 2048, [4, P])[:, :, :] for n in range(2)])

        made = {}

        def q_finish(c, bank, done):
            made["q", c] = activation(qt[:, c, :], bank, ACT.Identity, done, bias=column("b_q", c))
            return made["q", c]

        def k_finish(c, bank, done):
            made["k", c] = activation(kt[:, c, :], bank, ACT.Identity, done, bias=column("b_k", c))
            return made["k", c]

        feature_major(xt, 8, q_finish)
        feature_major(xt, 2, k_finish)
        n, w, there = take()
        bank = banks.next()
        for tile in range(TILES):
            for c in range(CHUNKS):
                done = mm3(bank.ap[:, tile * P:(tile + 1) * P], tuple(h[:, c, tile * P:(tile + 1) * P] for h in xt),
                           tuple(h[:, c * P:(c + 1) * P] for h in w), c == 0, c == CHUNKS - 1, *there, *bank.free,
                           tell=(c == CHUNKS - 1))
        give_back(n, done)
        v_made = vv(v_tok[:, :, :], bank.ap.rearrange("p (n f) -> p n f", n=TILES),
                    b_v_row.unsqueeze(1).to_broadcast([P, TILES, KV_W]), ALU.add, done)
        bank.free = (v_made,)

        units = [(blk, g, par) for blk in range(TILES) for g in range(KV_HEADS) for par in range(2)]
        state = {}

        def attend_scores(u):
            blk, g, par = units[u]
            rows = slice(par * DH, (par + 1) * DH)
            keys = slice(max(blk - 1, 0) * P, (blk + 1) * P)
            n = keys.stop - keys.start
            s, st = score.next(), head_stat.next()
            mask = table("window_mask")[:, 256 - n:256].unsqueeze(1).to_broadcast([P, 2, n])
            for b in range(2):
                bank = banks.next()
                for e in range(2):
                    c = 4 * g + 2 * b + e
                    done = mm(bank.ap[:, e * 256:e * 256 + n], qt[rows, c, blk * P:(blk + 1) * P], kt[rows, g, keys],
                              True, True, *bank.free, made["q", c], made["k", g], tell=True)
                masked = stt(s.ap[:, 2 * b:2 * b + 2, 0:n],
                             bank.ap.rearrange("p (h k) -> p h k", h=2)[:, :, 0:n], SCALE, mask,
                             ALU.mult, ALU.add, done, *s.free)
                bank.free = (masked,)
            neg_max, total, sink_e, inv = (st.ap[:, k, :] for k in range(4))
            m = dve.do(lambda: V.tensor_reduce(neg_max, s.ap[:, :, 0:n], AX.X, ALU.max, negate=True), masked, *st.free)
            own = slice(8 * g + par, 8 * g + 8, 2)
            m = vv(neg_max, neg_max, neg_sinks[:, own], ALU.min, m, ns)
            d = vv(sink_e, neg_max, sink_row[:, own], ALU.add, m)
            for h in range(4):
                e = activation(s.ap[:, h, 0:n], s.ap[:, h, 0:n], ACT.Exp, m, bias=neg_max[:, h:h + 1],
                               accum_out=total[:, h:h + 1])
            e = activation(sink_e, sink_e, ACT.Exp, d)
            state[u] = dict(s=s, st=st, n=n, e=e)

        def attend_turn(u):
            x = state[u]
            s, st, n = x["s"], x["st"], x["n"]
            total, sink_e, inv = (st.ap[:, k, :] for k in (1, 2, 3))
            a = vv(total, total, sink_e, ALU.add, x["e"])
            a = dve.do(lambda: V.reciprocal(inv, total), a)
            for h in range(4):
                p = vs(s.ap[:, h, 0:n], s.ap[:, h, 0:n], inv[:, h:h + 1], ALU.mult, a)
            st.free = (p,)
            pt = prob_t.next()
            for kb in range(n // P):
                bank = banks.next()
                for h in range(4):
                    done = turn(bank.ap[:, h * P:(h + 1) * P], s.ap[:, h, kb * P:(kb + 1) * P], p, *bank.free,
                                tell=(h == 3))
                c = activation(pt.ap[:, kb, :], bank.ap, ACT.Copy, done, *pt.free)
                bank.free = (c,)
            s.free = (done,)
            x.update(pt=pt, c=c)

        def attend_values(u):
            x = state.pop(u)
            blk, g, par = units[u]
            rows = slice(par * DH, (par + 1) * DH)
            nb = x["n"] // P
            bank = banks.next()
            for kb in range(nb):
                done = mm(bank.ap[rows, :], v_tok[:, blk - nb + 1 + kb, g * DH:(g + 1) * DH], x["pt"].ap[:, kb, :],
                          kb == 0, kb == nb - 1, x["c"], v_made, *bank.free, tell=(kb == nb - 1))
            x["pt"].free = (done,)
            o = o_tmp.next()
            c = dve.do(lambda: V.tensor_copy(o.ap[rows], bank.ap[rows, :].rearrange("p (c t) -> p c t", c=4)),
                       done, *o.free)
            bank.free = (c,)
            where = (rows, slice(4 * g, 4 * g + 4), slice(blk * P, (blk + 1) * P))
            o.free = split(ot[0][where], ot[1][where], o.ap[rows], c, low_on=(dve, V))
            return o.free

        for step in range(len(units) + 2):
            if step < len(units):
                attend_scores(step)
            if 0 <= step - 1 < len(units):
                attend_turn(step - 1)
            if step >= 2:
                o_ready = attend_values(step - 2)
        attended = (pe.sem, pe.count)

        ya = place("ya", 0, [CHUNKS, SEQ])
        x_ready_norm, x_ready = x_ready, o_ready

        def ya_finish(c, bank, done):
            made["ya", c] = activation(ya[:, c, :], bank, ACT.Copy, done, attended)
            return made["ya", c]

        feature_major(ot, 8, ya_finish)
        ot_read = (pe.sem, pe.count)

        POOL_AT = 49152
        padded = Ring([place(f"padded_{n}", POOL_AT + n * 2112, [PAD + SEQ])[:, :] for n in range(2)])
        sums = [place(f"sums_{n}", POOL_AT + 4224 + n * 2112, [PAD + SEQ]) for n in range(2)]
        pooled = Ring([place(f"pooled_{n}", POOL_AT + 8448 + n * 2048, [SEQ])[:, :] for n in range(2)])
        w_group = place("w_group", POOL_AT + 12544, [4, P])
        ypt = (place("ypt_high", POOL_AT + 14592, [4, SEQ], F32R), place("ypt_low", POOL_AT + 22784, [4, SEQ], F32R))
        group_sem = sem("group_matrices_loaded")
        w_group_in = act.start_dma(lambda: A.dma_start(w_group[:, :, :], t["w_pool_grp"]), group_sem, 16, attended,
                                   *o_ready)
        zeroed = [pool.do(lambda s=s: G.memset(s.ap[:, 0:PAD], 0.0), attended, *o_ready) for s in padded.slots]
        sums_free = [()]
        y_group = place("y_group", 16384 + 0, [2, SEQ])
        y_groups = Ring([y_group[:, n, :] for n in range(2)])

        def pool_finish(g, bank, done):
            if g:
                group_matrix(g - 1)
            p = padded.next()
            a = activation(p.ap[:, PAD:], bank, ACT.Identity, done, *zeroed, *p.free, bias=column("b_pool", g))
            src, reach, last = p.ap, 1, a
            for k in range(g + 1):
                dst = sums[k % 2][:, :]
                lo = 2 * reach - 1
                last = tt_op(pool, G, dst[:, lo:], src[:, lo:], src[:, lo - reach:PAD + SEQ - reach], ALU.add,
                             last, *sums_free[0])
                src, reach = dst, 2 * reach
            o = pooled.next()
            inv = table("inv_count").rearrange("p (g k) -> p g k", g=4)[:, g, :]
            b = stt(o.ap[:, PAD:], src[:, 2 * PAD:], 1.0 / WINDOWS[g], p.ap[:, 2 * PAD:], ALU.mult, ALU.subtract,
                    last, *o.free)
            b = vv(o.ap[:, 0:PAD], src[:, PAD:2 * PAD], inv, ALU.mult, b)
            b = vv(o.ap[:, 0:PAD], o.ap[:, 0:PAD], p.ap[:, PAD:2 * PAD], ALU.subtract, b)
            p.free, sums_free[0] = (b,), (b,)
            made["pooled", g] = (o, b)
            return a

        def group_matrix(g):
            o, b = made["pooled", g]
            bank = banks.next()
            done = mm(bank.ap, w_group[:, g, :], o.ap, True, True, b, w_group_in, *bank.free, tell=True)
            o.free = (done,)
            y = y_groups.next()
            a = vs(y.ap, bank.ap, column("pool_scale", g), ALU.mult, done, *y.free, ot_read)
            bank.free = (a,)
            y.free = split(ypt[0][:, g, :], ypt[1][:, g, :], y.ap, a, low_on=(dve, V))
            return done, y.free

        x_ready = x_ready_norm
        feature_major(xt, 4, pool_finish)
        done, y_ready = group_matrix(3)

        merged = (place("merged_high", 16384, [CHUNKS, SEQ], F32R), place("merged_low", 32768, [CHUNKS, SEQ], F32R))
        gate = Ring([place(f"gate_{n}", POOL_AT + n * 2048, [SEQ])[:, :] for n in range(4)])
        for s in gate.slots:
            s.free = (*y_ready, done)

        for pair in range(4):
            a_items = take()
            halves = {}
            for kind, bias in (("a", "b_ga"), ("p", "b_gp")):
                n, w, there = a_items if kind == "a" else take()
                for e in range(2):
                    c = 2 * pair + e
                    bank = banks.next()
                    for k in range(CHUNKS):
                        done = mm3(bank.ap, tuple(h[:, k * 256 + e * P:k * 256 + (e + 1) * P] for h in w),
                                   tuple(h[:, k, :] for h in xt), k == 0, k == CHUNKS - 1, *there, *bank.free,
                                   tell=(k == CHUNKS - 1))
                    gt = gate.next()
                    s = activation(gt.ap, bank.ap, ACT.Sigmoid, done, *gt.free, bias=column(bias, c))
                    bank.free = (s,)
                    halves[kind, e] = (gt, s)
                give_back(n, done)
            n, w, there = take()
            for e in range(2):
                c = 2 * pair + e
                bank = banks.next()
                for k in range(4):
                    done = mm3(bank.ap, tuple(h[:, k * 256 + e * P:k * 256 + (e + 1) * P] for h in w),
                               tuple(h[:, k, :] for h in ypt), k == 0, k == 3, *there, *y_ready, *bank.free,
                               tell=(k == 3))
                (ga, sa), (gp, sg) = halves["a", e], halves["p", e]
                m1 = vv(ga.ap, ga.ap, ya[:, c, :], ALU.mult, sa, made["ya", c])
                m2 = vv(gp.ap, gp.ap, bank.ap, ALU.mult, sg, done)
                bank.free = (m2,)
                m3 = vv(ga.ap, ga.ap, gp.ap, ALU.add, m1, m2)
                gp.free = (m3,)
                ga.free = split(merged[0][:, c, :], merged[1][:, c, :], ga.ap, m3, ot_read, *y_ready)
            give_back(n, done)
        x_ready = ga.free

        added = {}

        def residual_add(half):
            def finish(tile, bank, done):
                r = resid[:, tile, half * 512:(half + 1) * 512]
                added[tile] = vv(r, r, bank, ALU.add, done)
                return added[tile]
            return finish

        for half in range(2):
            token_major(merged, 2, residual_add(half))
        mixed_in = (pe.sem, pe.count)

        x_ready = norm_turned(lambda n: resid[:, n, :], D, EPS1, "g_ffn", xt, 0, lambda n: (added[n],),
                              dst_free=(mixed_in,), extra=(mixed_in,))

        hidden = Ring([place(f"hidden_{n}", n * 8192, [J, SEQ])[:, :, :] for n in range(AHEAD)])
        sub_keys = place("sub_keys", 24576, [2 * PHEADS, KEYS])
        query = Ring([place(f"query_{n}", 32768 + n * 2048, [SEQ])[:, :] for n in range(2)])
        key_score = Ring([place(f"key_score_{n}", 36864 + n * 2048, [TILES, KEYS])[:, :, :] for n in range(2)])
        top_v = place("top_v", 40960, [TILES, 2 * PHEADS, TOPK])
        top_i = place("top_i", 45056, [TILES, 2 * PHEADS, TOPK], U32)
        top_f = place("top_f", 49152, [TILES, 2 * PHEADS, TOPK])
        cand = place("cand", 53248, [PHEADS, TOPK * TOPK])
        same = place("same", 32768, [PAIRS, TOPK])
        names = ["best", "pos", "pos_a", "pos_b", "a_f", "b_f", "first", "second", "gate_w", "shifted"]
        small_at = {n: place(n, 61440 + 512 * k, [PHEADS, TOPK], U32 if n in ("pos", "pos_a", "pos_b") else F32)
                    for k, n in enumerate(names)}
        gate_sum = place("gate_sum", 61440 + 512 * len(names), [2, PHEADS])
        pair_t = place("pair_t", 67584, [3, SEQ])

        keys_sem = sem("sub_keys_loaded")
        keys_in = act.start_dma(lambda: A.dma_start(sub_keys[:, :, :], t["sub_keys"]), keys_sem, 16, mixed_in, *ga.free)

        def query_finish(c, bank, done):
            q = query.next()
            a = activation(q.ap, bank, ACT.Copy, done, *q.free)
            made["query"] = (q, a)
            return a

        def best_keys(c):
            q, a = made["query"]
            bank = banks.next()
            for tile in range(TILES):
                done = mm(bank.ap[:, tile * P:(tile + 1) * P], q.ap[:, tile * P:(tile + 1) * P], sub_keys[:, c, :],
                          True, True, a, keys_in, *bank.free, tell=(tile == TILES - 1))
            q.free = (done,)
            s = key_score.next()
            b = activation(s.ap, bank.ap.rearrange("p (n k) -> p n k", n=TILES), ACT.Copy, done, *s.free)
            bank.free = (b,)
            last = b
            for tile in range(TILES):
                v, i, x = top_v[:, tile, c, :], top_i[:, tile, c, :], s.ap[:, tile, :]
                last = top16(v, i, x, last)
            s.free = (last,)
            return last

        def top16(v, i, x, *after):
            a = dve.do(lambda: V.max(v[:, 0:8], x), *after)
            dve.do(lambda: V.max_index(i[:, 0:8], v[:, 0:8], x), a)
            b = dve.do(lambda: V.match_replace(x, v[:, 0:8], x, LOWEST), (dve.sem, dve.count))
            c = dve.do(lambda: V.max(v[:, 8:16], x), b)
            return dve.do(lambda: V.max_index(i[:, 8:16], v[:, 8:16], x), c)

        for pair in range(PHEADS):
            n, w, there = take()
            for e in range(2):
                bank = banks.next()
                for k in range(CHUNKS):
                    done = mm3(bank.ap, tuple(h[:, k * 256 + e * P:k * 256 + (e + 1) * P] for h in w),
                               tuple(h[:, k, :] for h in xt), k == 0, k == CHUNKS - 1, *there, *x_ready, *bank.free,
                               tell=(k == CHUNKS - 1))
                if e == 1:
                    give_back(n, done)
                bank.free = (query_finish(2 * pair + e, bank.ap, done),)
                keys_done = best_keys(2 * pair + e)

        def expert_hidden(g):
            slot = hidden.next()
            for half in range(2):
                n, w, there = take()
                for e in range(2):
                    bank = banks.next()
                    for k in range(CHUNKS):
                        at = (e * CHUNKS + k) * P
                        done = mm3(bank.ap, tuple(h[:, at:at + P] for h in w), tuple(h[:, k, :] for h in xt),
                                   k == 0, k == CHUNKS - 1, *there, *bank.free, tell=(k == CHUNKS - 1))
                    if e == 1:
                        give_back(n, done)
                    a = activation(slot.ap[:, 2 * half + e, :], bank.ap, ACT.Gelu, done, *slot.free, mixed_in)
                    bank.free = (a,)
            made["hidden", g] = (slot, a)

        for g in range(AHEAD):
            expert_hidden(g)

        as_float = dve.do(lambda: V.tensor_copy(top_f[:, :, :, :], top_i[:, :, :, :]), keys_done)
        free_small = ()
        for tile in range(TILES):
            def half(x, which):
                return x[:, tile, :, :].rearrange("p (h two) k -> p two h k", two=2)[:, which, :, :]
            a = vv(cand[:, :, :].rearrange("p h (a b) -> p h a b", a=TOPK),
                   half(top_v, 0).unsqueeze(3).to_broadcast([P, PHEADS, TOPK, TOPK]),
                   half(top_v, 1).unsqueeze(2).to_broadcast([P, PHEADS, TOPK, TOPK]), ALU.add, keys_done,
                   (dve.sem, dve.count))
            best, pos, pos_a, pos_b, a_f, b_f, first, second, gate_w, shifted = (small_at[n][:, :, :] for n in names)
            last = a
            for h in range(PHEADS):
                last = top16(best[:, h, :], pos[:, h, :], cand[:, h, :], last, *free_small)
            ua = dve.do(lambda: V.tensor_scalar(pos_a, pos, 4, None, ALU.logical_shift_right), last)
            ub = dve.do(lambda: V.tensor_scalar(pos_b, pos, 15, None, ALU.bitwise_and), last)
            fa = dve.do(lambda: V.tensor_copy(a_f, pos_a), ua)
            fb = dve.do(lambda: V.tensor_copy(b_f, pos_b), ub)
            d = vv(shifted, best, best[:, :, 0:1].to_broadcast([P, PHEADS, TOPK]), ALU.subtract, last)
            ex = activation(shifted, shifted, ACT.Exp, d)
            iota_k = table("iota_k").unsqueeze(1).to_broadcast([P, PAIRS, TOPK])
            for which, at, dst, f in ((0, a_f, first, fa), (1, b_f, second, fb)):
                flat = at.rearrange("p h k -> p (h k)")
                x = vv(same[:, :, :], iota_k, flat.unsqueeze(2).to_broadcast([P, PAIRS, TOPK]), ALU.is_equal, f,
                       as_float, (dve.sem, dve.count))
                s4 = same[:, :, :].rearrange("p (h k) a -> p h k a", h=PHEADS)
                x = vv(s4, s4, half(top_f, which).unsqueeze(2).to_broadcast([P, PHEADS, TOPK, TOPK]), ALU.mult, x)
                looked = dve.do(lambda dst=dst: V.tensor_reduce(dst.rearrange("p h k -> p (h k)"), same[:, :, :], AX.X,
                                                                ALU.add), x, *free_small)
            y = dve.do(lambda: V.tensor_reduce(gate_sum[:, 0, :], shifted, AX.X, ALU.add), ex)
            y = dve.do(lambda: V.reciprocal(gate_sum[:, 1, :], gate_sum[:, 0, :]), y)
            y = vv(gate_w, shifted, gate_sum[:, 1, :].unsqueeze(2).to_broadcast([P, PHEADS, TOPK]), ALU.mult, y)
            bank = banks.next()
            for k, src in enumerate((first, second, gate_w)):
                done = turn(bank.ap[:, k * P:(k + 1) * P], src.rearrange("p h k -> p (h k)"), looked, y, *bank.free,
                            tell=(k == 2))
            free_small = (done,)
            pairs_ready = activation(pair_t[:, :, tile * P:(tile + 1) * P],
                                     bank.ap[:, 0:3 * P].rearrange("p (k t) -> p k t", k=3), ACT.Copy, done)
            bank.free = (pairs_ready,)
        chosen = (dve.sem, dve.count)

        gates = nc.dram_tensor("expert_gates", [GATE_CHUNKS, KEYS, KEYS, GATE_T], F32, kind="Internal").ap()
        staged = Ring([place(f"staged_{n}", 24576 + n * 16384, [KEYS, GATE_T])[:, :, :] for n in range(2)])
        hot_i = Ring([place(f"hot_i_{n}", 57344 + n * 512, [KEYS])[:, :] for n in range(8)])
        hot_j = Ring([place(f"hot_j_{n}", 61440 + n * 512, [KEYS])[:, :] for n in range(8)])
        stored_sem = [sem(f"gates_stored_{n}") for n in range(2)]
        for s in hot_i.slots + hot_j.slots + staged.slots:
            s.free = (chosen, pairs_ready, done)
        for tok in range(0, SEQ, 4):
            bank = banks.next()
            chunk = tok // GATE_T
            if tok % GATE_T == 0:
                stage = staged.next()
            for k in range(4):
                hi_, hj_ = hot_i.next(), hot_j.next()
                at = tok + k
                if at % 2:
                    a = pool.do(lambda o=hi_.ap, at=at: G.tensor_scalar(o, table("iota"), pair_t[:, 0, at:at + 1],
                                                                        None, ALU.is_equal),
                                pairs_ready, *hi_.free)
                else:
                    a = vs(hi_.ap, table("iota"), pair_t[:, 0, at:at + 1], ALU.is_equal, pairs_ready, *hi_.free)
                b = vs(hj_.ap, table("iota"), pair_t[:, 1, at:at + 1], ALU.is_equal, pairs_ready, *hj_.free,
                       s2=pair_t[:, 2, at:at + 1], op1=ALU.mult)
                done = mm(bank.ap[:, k * P:(k + 1) * P], hi_.ap, hj_.ap, True, True, a, b, *bank.free, tell=True)
                hi_.free = hj_.free = (done,)
            t0 = tok % GATE_T
            e = activation(stage.ap[:, :, t0:t0 + 4].rearrange("p j t -> p t j"),
                           bank.ap.rearrange("p (t j) -> p t j", t=4), ACT.Copy, done, *stage.free)
            bank.free = (e,)
            if tok % GATE_T == GATE_T - 4:
                total = 16 * (chunk // 2 + 1)
                st = act.start_dma(lambda stage=stage, chunk=chunk: A.dma_start(gates[chunk], stage.ap),
                                   stored_sem[chunk % 2], total, e)
                stage.free = (st,)
        all_stored = [s.free[0] for s in staged.slots]
        gates_built = (pe.sem, pe.count)

        gate_in = Ring([place(f"gate_in_{n}", 24576 + n * 8192, [GATE_CHUNKS, J * GATE_T])[:, :, :] for n in range(2)])
        weight = Ring([(place(f"weight_high_{n}", 40960 + n * 16384, [J, SEQ], F32R),
                        place(f"weight_low_{n}", 40960 + n * 16384 + 8192, [J, SEQ], F32R)) for n in range(2)])
        gate_sem = [sem(f"gates_loaded_{n}") for n in range(2)]
        for s in weight.slots:
            s.free = (gates_built, *all_stored)
        gate_there = {}

        def load_gates(g):
            if g >= GROUPS:
                return
            s = gate_in.next()
            src = gates[:, :, g * J:(g + 1) * J, :].rearrange("c i j t -> i c (j t)")
            gate_there[g] = (s, act.start_dma(lambda: A.dma_start(s.ap, src), gate_sem[g % 2], 16 * (g // 2 + 1),
                                              *all_stored, *s.free))

        def weigh(g):
            if g >= GROUPS:
                return
            slot, a = made["hidden", g]
            gs, there = gate_there[g]
            w = weight.next()
            h = slot.ap.rearrange("p j (c t) -> p j c t", t=GATE_T)
            m = vv(h, h, gs.ap.rearrange("p c (j t) -> p j c t", j=J), ALU.mult, a, there)
            gs.free = (m,)
            load_gates(g + 2)
            done = split(w.ap[0][:, :, :], w.ap[1][:, :, :], slot.ap, m, *w.free, low_on=(dve, V))
            slot.free = done
            made["weight", g] = (w, done)

        load_gates(0)
        load_gates(1)
        weigh(0)
        for g in range(GROUPS):
            weigh(g + 1)
            w, w_ready = made["weight", g]
            pair = [take() for _ in range(2)]
            for tile in range(TILES):
                for half in range(2):
                    bank = banks.next()
                    for j in range(J):
                        n, v, there = pair[j // 2]
                        at = (j % 2) * D + half * 512
                        done = mm3(bank.ap, tuple(h[:, j, tile * P:(tile + 1) * P] for h in w.ap),
                                   tuple(h[:, at:at + 512] for h in v), j == 0, j == J - 1,
                                   *there, *w_ready, *bank.free, tell=(j == J - 1 or (tile == TILES - 1 and half == 1 and j == 1)))
                        if tile == TILES - 1 and half == 1 and j % 2 == 1:
                            give_back(n, done)
                    r = resid[:, tile, half * 512:(half + 1) * 512]
                    added[tile] = vv(r, r, bank.ap, ALU.add, done)
                    bank.free = (added[tile],)
            w.free = (done,)
            if g + AHEAD < GROUPS:
                expert_hidden(g + AHEAD)
        experts_done = (pe.sem, pe.count)

        row_sem = [sem(f"row_loaded_{n}") for n in range(4)]

        def load_row(name, first, last, at, k, *after):
            width = row[last].stop - row[first].start
            dst = place(name, at, [width])
            src = t["rows"][0:1, row[first].start:row[last].stop].to_broadcast([P, width])
            return dst, act.start_dma(lambda: A.dma_start(dst[:, :], src), row_sem[k], 16, *after)

        last_weigh = made["weight", GROUPS - 1][1]
        g_final, g_final_in = load_row("g_final_row", "g_final", "g_final", 0, 0, experts_done, *last_weigh)
        inv = inv_rms(lambda n: resid[:, n, :], D, EPS1, lambda n: (added[n],), (experts_done, *last_weigh))
        for tile in range(TILES):
            r = resid[:, tile, :]
            added[tile] = stt(r, r, stats[:, 8 + tile:9 + tile], g_final[:, :], ALU.mult, ALU.mult, inv, g_final_in)
        scaled_all = added[TILES - 1]
        x_ready = norm_turned(lambda n: resid[:, n, :], D, EPS2, "g_pre_mix", xt, 0, lambda n: (added[n],),
                              dst_free=(experts_done,))

        pos_i = place("pos_i", 65536, [TILES], I32)
        pos_f = place("pos_f", 65568, [TILES])
        angle = place("angle", 65600, [TILES, ROT_HALF])
        turns_i = place("turns_i", 65728, [TILES, ROT_HALF], I32)
        turns = place("turns", 65856, [TILES, ROT_HALF])
        over = place("over", 65984, [TILES, ROT_HALF])
        sin_a = place("sin_a", 66112, [TILES, ROT_HALF])
        cos_a = place("cos_a", 66240, [TILES, ROT_HALF])
        rot = place("rot", 66368, [4, 2 * HEADS2 * ROT_HALF])
        pos_sem = sem("positions_loaded")
        pos_in = act.start_dma(lambda: A.dma_start(pos_i[:, :], t["positions"]), pos_sem, 16, experts_done, *last_weigh)
        TWO_PI = 2 * np.pi
        part1 = 6.28125
        part2 = float(np.float32(np.round((TWO_PI - part1) * 2 ** 21) / 2 ** 21))
        part3 = float(np.float32(TWO_PI - part1 - part2))
        PI_IN = float(np.nextafter(np.float32(np.pi), np.float32(0)))
        a = dve.do(lambda: V.tensor_copy(pos_f[:, :], pos_i[:, :]), pos_in)
        a = vv(angle[:, :, :], pos_f[:, :].unsqueeze(2).to_broadcast([P, TILES, ROT_HALF]),
               table("inv_freq").unsqueeze(1).to_broadcast([P, TILES, ROT_HALF]), ALU.mult, a, small)
        a = vs(turns[:, :, :], angle[:, :, :], 1 / TWO_PI, ALU.mult, a)
        a = dve.do(lambda: V.tensor_copy(turns_i[:, :, :], turns[:, :, :]), a)
        a = dve.do(lambda: V.tensor_copy(turns[:, :, :], turns_i[:, :, :]), a)
        for part in (part1, part2, part3):
            a = stt(angle[:, :, :], turns[:, :, :], -part, angle[:, :, :], ALU.mult, ALU.add, a)

        def wrap(x, a):
            for limit, op, step in ((float(np.pi), ALU.is_gt, -TWO_PI), (-float(np.pi), ALU.is_lt, TWO_PI)):
                a = vs(over[:, :, :], x, limit, op, a, s2=step, op1=ALU.mult)
                a = vv(x, x, over[:, :, :], ALU.add, a)
            return vs(x, x, PI_IN, ALU.min, a, s2=-PI_IN, op1=ALU.max)

        a = vs(cos_a[:, :, :], angle[:, :, :], float(np.pi / 2), ALU.add, a)
        a = wrap(angle[:, :, :], a)
        b = activation(sin_a[:, :, :], angle[:, :, :], ACT.Sin, a)
        a = wrap(cos_a[:, :, :], a)
        rope_ready = activation(cos_a[:, :, :], cos_a[:, :, :], ACT.Sin, a)

        qk = place("qk", 0, [2, TILES, W2])
        v2 = place("v2", 16384, [TILES, W2])
        u_gate = place("u_gate", 24576, [TILES, W2])
        v_gate = place("v_gate", 32768, [TILES, W2])
        q2t = place("q2t", 40960, [4, SEQ])
        k2t = place("k2t", 49152, [4, SEQ])

        def qk_finish(which):
            def finish(tile, bank, done):
                made["qk", which, tile] = activation(qk[:, which, tile, :], bank, ACT.Copy, done, scaled_all)
                return made["qk", which, tile]
            return finish

        def v_finish(tile, bank, done):
            made["v2", tile] = activation(v2[:, tile, :], bank, ACT.Copy, done, *x_ready)
            return made["v2", tile]

        def gelu_finish(dst, sums):
            def finish(tile, bank, done):
                kw = dict(accum_out=sums[:, tile:tile + 1]) if sums is not None else {}
                made[id(dst), tile] = activation(dst[:, tile, :], bank, ACT.Gelu, done, *x_ready, **kw)
                return made[id(dst), tile]
            return finish

        token_major(xt, 2, qk_finish(0))
        token_major(xt, 2, qk_finish(1))
        for tile in range(TILES):
            x = qk[:, :, tile, :].rearrange("p w (h f) -> p w h f", h=HEADS2)
            x1, x2 = x[:, :, :, 0:ROT_HALF], x[:, :, :, ROT_HALF:2 * ROT_HALF]
            cs, sn = (z[:, tile, :].unsqueeze(1).unsqueeze(1).to_broadcast([P, 2, HEADS2, ROT_HALF])
                      for z in (cos_a, sin_a))
            r = [rot[:, k, :].rearrange("p (w h f) -> p w h f", w=2, h=HEADS2) for k in range(4)]
            after = (made["qk", 0, tile], made["qk", 1, tile], rope_ready, (dve.sem, dve.count))
            m = [vv(r[k], y, z, ALU.mult, *after) for k, (y, z) in enumerate(((x1, cs), (x2, sn), (x2, cs), (x1, sn)))]
            vv(x1, r[0], r[1], ALU.subtract, *m)
            made["rot", tile] = vv(x2, r[2], r[3], ALU.add, *m)
        token_major(xt, 2, v_finish)
        for which, dst in ((0, q2t), (1, k2t)):
            for tile in range(TILES):
                bank = banks.next()
                for c in range(4):
                    done = turn(bank.ap[:, c * P:(c + 1) * P], qk[:, which, tile, c * P:(c + 1) * P],
                                made["rot", tile], *bank.free, tell=(c == 3))
                made["t", which, tile] = activation(dst[:, :, tile * P:(tile + 1) * P],
                                                    bank.ap.rearrange("p (c t) -> p c t", c=4), ACT.Copy, done)
                bank.free = (made["t", which, tile],)
        qk_turned = done
        v_mean = stats[:, 12:16]
        token_major(xt, 2, gelu_finish(u_gate, None))
        token_major(xt, 2, gelu_finish(v_gate, v_mean))
        projected = (pe.sem, pe.count)

        score2 = Ring([place(f"score2_{n}", 57344 + n * 4096, [2, SEQ])[:, :, :] for n in range(2)])
        prob2 = Ring([place(f"prob2_{n}", 68416 + n * 4096, [2, SEQ])[:, :, :] for n in range(2)])
        stat2 = Ring([place(f"stat2_{n}", 76608 + n * 32, [3, 2])[:, :, :] for n in range(3)])
        o2 = place("o2", 0, [TILES, W2])
        units2 = [(tile, c) for tile in range(TILES) for c in range(4)]
        for s in score2.slots + prob2.slots:
            s.free = (*x_ready, rope_ready, made["rot", TILES - 1])

        def dilated_scores(u):
            tile, c = units2[u]
            n = (tile + 1) * P
            s, st = score2.next(), stat2.next()
            for par in range(2):
                rows = slice(par * DH, (par + 1) * DH)
                bank = banks.next()
                done = mm(bank.ap[:, 0:n], q2t[rows, c, tile * P:(tile + 1) * P], k2t[rows, c, 0:n], True, True,
                          made["t", 0, tile], *(made["t", 1, k] for k in range(tile + 1)), *bank.free, tell=True)
                masked = stt(s.ap[:, par, 0:n], bank.ap[:, 0:n], SCALE, table("never")[:, SEQ - n:], ALU.mult, ALU.add,
                             done, *s.free)
                bank.free = (masked,)
            neg_max = st.ap[:, 0, :]
            m = dve.do(lambda: V.tensor_reduce(neg_max, s.ap[:, :, 0:n], AX.X, ALU.max, negate=True), masked, *st.free)
            for par in range(2):
                e = activation(s.ap[:, par, 0:n], s.ap[:, par, 0:n], ACT.Exp, m, bias=neg_max[:, par:par + 1])
            state[u] = dict(s=s, st=st, n=n, e=e)

        def dilated_turn(u):
            x = state[u]
            s, st, n = x["s"], x["st"], x["n"]
            for par in range(2):
                p = dve.do(lambda par=par: V.tensor_tensor_reduce(
                    out=s.ap[:, par, 0:n], in0=s.ap[:, par, 0:n], in1=table("times")[:, SEQ - n:], scale=1.0,
                    scalar=0.0, op0=ALU.mult, op1=ALU.add, accum_out=st.ap[:, 1, par:par + 1]), x["e"])
            inv = dve.do(lambda: V.reciprocal(st.ap[:, 2, :], st.ap[:, 1, :]), p)
            pt = prob2.next()
            for par in range(2):
                bank = banks.next()
                for kt_ in range(n // P):
                    done = turn(bank.ap[:, kt_ * P:(kt_ + 1) * P], s.ap[:, par, kt_ * P:(kt_ + 1) * P], p, *bank.free,
                                tell=(kt_ == n // P - 1))
                c = activation(pt.ap[:, par, 0:n], bank.ap[:, 0:n], ACT.Copy, done, *pt.free)
                bank.free = (c,)
            s.free = (done,)
            x.update(pt=pt, c=c, inv=inv)

        def dilated_values(u):
            x = state.pop(u)
            tile, cc = units2[u]
            bank = banks.next()
            for par in range(2):
                head = 2 * cc + par
                for kt_ in range(tile + 1):
                    done = mm(bank.ap[:, par * DH:(par + 1) * DH], x["pt"].ap[:, par, kt_ * P:(kt_ + 1) * P],
                              v2[:, kt_, head * DH:(head + 1) * DH], kt_ == 0, kt_ == tile, x["c"],
                              made["v2", kt_], *bank.free, tell=(kt_ == tile))
            x["pt"].free = (done,)
            o = vv(o2[:, tile, cc * P:(cc + 1) * P].rearrange("p (h f) -> p h f", h=2),
                   bank.ap[:, 0:P].rearrange("p (h f) -> p h f", h=2),
                   x["st"].ap[:, 2, :].unsqueeze(2).to_broadcast([P, 2, DH]), ALU.mult, done, x["inv"], qk_turned)
            bank.free = (o,)
            x["st"].free = (o,)
            made["o2", tile] = o

        for step in range(len(units2) + 2):
            if step < len(units2):
                dilated_scores(step)
            if 0 <= step - 1 < len(units2):
                dilated_turn(step - 1)
            if step >= 2:
                dilated_values(step - 2)
        attended2 = (pe.sem, pe.count)
        attended2_d = (dve.sem, dve.count)

        ln_rows, ln_rows_in = load_row("ln_rows", "ln_gain", "ln_bias", 57344, 1, attended2, attended2_d,
                                       (act.sem, act.count))
        w_sp = place("w_sp", 8192, [8, P])
        sp_sem = sem("spatial_loaded")
        w_sp_in = act.start_dma(lambda: A.dma_start(w_sp[:, :, :], t["w_spatial"]), sp_sem, 16, qk_turned)
        causal = pool.do(lambda: G.affine_select(out=w_sp[:, :, :], in_=w_sp[:, :, :], compare_op=ALU.is_ge, fill=0.0,
                                                 base=0, pattern=[[0, 8], [1, P]], channel_multiplier=-1), w_sp_in)
        mean = vs(v_mean, v_mean, -1.0 / W2, ALU.mult, made[id(v_gate), TILES - 1])
        for tile in range(TILES):
            v = v_gate[:, tile, :]
            a = vs(v, v, v_mean[:, tile:tile + 1], ALU.add, mean, made[id(v_gate), tile])
            s = normed.next()
            a = activation(s.ap[:, 0:W2], v, ACT.Square, a, *s.free, attended2, accum_out=stats[:, tile:tile + 1])
            s.free = (a,)
        a = vs(stats[:, 4:8], stats[:, 0:4], 1.0 / W2, ALU.mult, a, s2=LN_EPS, op1=ALU.add)
        a = activation(stats[:, 4:8], stats[:, 4:8], ACT.Sqrt, a)
        a = dve.do(lambda: V.reciprocal(stats[:, 8:12], stats[:, 4:8]), a)
        for tile in range(TILES):
            v = v_gate[:, tile, :]
            b = stt(v, v, stats[:, 8 + tile:9 + tile], ln_rows[:, 0:W2], ALU.mult, ALU.mult, a, ln_rows_in)
            b = vv(v, v, ln_rows[:, W2:2 * W2], ALU.add, b)
        for g in range(8):
            bank = banks.next()
            done = mm(bank.ap[:, 0:256], w_sp[:, g, :], v_gate[:, :, g * DH:(g + 1) * DH], True, True, b, causal,
                      *bank.free, tell=True)
            u = u_gate[:, :, g * DH:(g + 1) * DH]
            gated = stt(u, bank.ap[:, 0:256].rearrange("p (n f) -> p n f", n=TILES), column("b_spatial", g), u,
                        ALU.add, ALU.mult, done, *(made[id(u_gate), k] for k in range(TILES)))
            bank.free = (gated,)

        norm_turned(lambda n: o2[:, n, :], W2, EPS2, "g_out", xt, 0, lambda n: (made["o2", n],),
                    dst_free=(projected,), extra=(attended2,))
        x_ready = norm_turned(lambda n: u_gate[:, n, :], W2, EPS2, "g_out", xt, 4, lambda n: (gated,),
                              dst_free=(projected,))
        y2 = place("y2", 0, [TILES, D])
        turned_all = (pe.sem, pe.count)
        g_pm, g_pm_in = load_row("g_post_mix_row", "g_post_mix", "g_post_mix", 61440, 2, attended2, attended2_d,
                                 turned_all)

        def y_finish(half):
            def finish(tile, bank, done):
                added[tile] = activation(y2[:, tile, half * 512:(half + 1) * 512], bank, ACT.Copy, done)
                return added[tile]
            return finish

        for half in range(2):
            token_major(xt, 2, y_finish(half))
        out_done = (pe.sem, pe.count)

        def add_normed(y, gain, gain_in, tile, inv):
            a = stt(y, y, stats[:, 8 + tile:9 + tile], gain[:, :], ALU.mult, ALU.mult, inv, gain_in)
            return vv(resid[:, tile, :], resid[:, tile, :], y, ALU.add, a)

        inv = inv_rms(lambda n: y2[:, n, :], D, EPS2, lambda n: (added[n],))
        for tile in range(TILES):
            added[tile] = add_normed(y2[:, tile, :], g_pm, g_pm_in, tile, inv)

        x_ready = norm_turned(lambda n: resid[:, n, :], D, EPS2, "g_pre_ffn", xt, 0, lambda n: (added[n],),
                              dst_free=(out_done,))
        ff = (place("ff_high", 0, [FF_PARTS[0], SEQ], F32R), place("ff_low", 24576, [FF_PARTS[0], SEQ], F32R))
        down = place("down", 49152, [TILES, D])
        act_g = Ring([place(f"act_g_{n}", 65536 + n * 2048, [SEQ])[:, :] for n in range(4)])
        normed_done = (*x_ready, (pe.sem, pe.count), (dve.sem, dve.count))
        g_pf, g_pf_in = load_row("g_post_ffn_row", "g_post_ffn", "g_post_ffn", 73728, 3, *normed_done)
        for s in act_g.slots:
            s.free = normed_done
        ff_free = normed_done
        for part, chunks in enumerate(FF_PARTS):
            for pair in range(chunks // 2):
                silu = []
                for kind in range(2):
                    n, w, there = take()
                    for e in range(2):
                        bank = banks.next()
                        for k in range(CHUNKS):
                            done = mm3(bank.ap, tuple(h[:, k * 256 + e * P:k * 256 + (e + 1) * P] for h in w),
                                       tuple(h[:, k, :] for h in xt), k == 0, k == CHUNKS - 1, *there, *x_ready,
                                       *bank.free, tell=(k == CHUNKS - 1))
                        if e == 1:
                            give_back(n, done)
                        if kind == 0:
                            s = act_g.next()
                            a = activation(s.ap, bank.ap, ACT.Silu, done, *s.free)
                            bank.free = (a,)
                            silu.append((s, a))
                        else:
                            s, a = silu[e]
                            m = vv(s.ap, s.ap, bank.ap, ALU.mult, a, done)
                            bank.free = (m,)
                            c = 2 * pair + e
                            s.free = ff_ready = split(ff[0][:, c, :], ff[1][:, c, :], s.ap, m, *ff_free)
            keep_x = x_ready
            x_ready = ff_ready

            def down_finish(half, part=part):
                def finish(tile, bank, done):
                    d = down[:, tile, half * 512:(half + 1) * 512]
                    if part == 0:
                        added[tile] = activation(d, bank, ACT.Copy, done)
                    else:
                        added[tile] = vv(d, d, bank, ALU.add, done, added[tile])
                    return added[tile]
                return finish

            for half in range(2):
                token_major(ff, -(-chunks // 4), down_finish(half), k_last=(chunks - 1) % 4 + 1)
            ff_free = ((pe.sem, pe.count),)
            x_ready = keep_x

        squares = Ring([place(f"square_{n}", n * 4096, [D])[:, :] for n in range(2)])
        for s in squares.slots:
            s.free = ff_free
        inv = inv_rms(lambda n: down[:, n, :], D, EPS2, lambda n: (added[n],), scratch=squares)
        out_sem = sem("out_stored")
        for tile in range(TILES):
            a = add_normed(down[:, tile, :], g_pf, g_pf_in, tile, inv)
            sp.start_dma(lambda tile=tile: S.dma_start(out[tile * P:(tile + 1) * P, :], resid[:, tile, :]), out_sem, 0, a)
        sp.do(None, (out_sem, 16 * TILES), *all_stored, tell=False)
        assert taken[0] == len(items), (taken[0], len(items))

        block = ctx.enter_context(nc.Block())

        @block.sync
        def _(e):
            sp.run(e)

        @block.scalar
        def _(e):
            act.run(e)

        @block.vector
        def _(e):
            dve.run(e)

        @block.gpsimd
        def _(e):
            pool.run(e)

        @block.tensor
        def _(e):
            pe.run(e)


WEIGHTS_BEFORE_PEER = 4 + 1 + 1 + 4 + 2 + 12 + 4 + 8


def column_items(w, c0, c1, k=CHUNKS):
    return [w[:, c:c + 256].reshape(k, P, 256).transpose(1, 0, 2).reshape(P, k * 256) for c in range(c0, c1, 256)]


def row_items(w, c0, c1):
    out = []
    for c in range(c0, c1, 512):
        for r in range(0, w.shape[0], 4 * P):
            x = w[r:r + 4 * P, c:c + 512]
            out.append(x.reshape(-1, P, 512).transpose(1, 0, 2).reshape(P, -1))
    return out


def lay_out(i):
    w_in = i["w_in"][0]
    k0, v0 = Q_W, Q_W + KV_W
    p0 = v0 + KV_W
    ga0 = p0 + POOL_W
    gp0 = ga0 + D
    kk = [w_in[:, k0 + g * DH:k0 + (g + 1) * DH] for g in (0, 0, 1, 1)]
    items = column_items(w_in, 0, Q_W)
    items += column_items(np.concatenate(kk, axis=1), 0, 256)
    items.append(w_in[:, v0:v0 + KV_W].reshape(CHUNKS, P, KV_W).transpose(1, 0, 2).reshape(P, -1))
    items += column_items(i["w_attn_up"][0], 0, D)
    items += column_items(w_in, p0, ga0)
    ga, gp, up = column_items(w_in, ga0, gp0), column_items(w_in, gp0, gp0 + D), column_items(i["w_pool_up"][0], 0, D, 4)
    for c in range(4):
        items += [ga[c], gp[c], up[c]]
    items += row_items(i["w_o"][0], 0, D)
    items += column_items(i["w_query"][0], 0, 2048)
    assert len(items) == WEIGHTS_BEFORE_PEER
    items += row_items(i["w_in_2"][0], 0, 5 * W2)
    items += row_items(i["w_out_2"][0], 0, D)
    gate, up = column_items(i["w_gate_2"][0], 0, FF), column_items(i["w_up_2"][0], 0, FF)
    at = 0
    for chunks in FF_PARTS:
        for c in range(at // 2, (at + chunks) // 2):
            items += [gate[c], up[c]]
        items += row_items(i["w_down_2"][0][at * P:(at + chunks) * P], 0, D)
        at += chunks
    weights = np.zeros((len(items), P, ITEM), np.float32)
    for n, x in enumerate(items):
        weights[n, :, :x.shape[1]] = x

    def cols(v):
        return v.reshape(-1, P).T

    b = i["b_in"][0]
    bk = [b[k0 + g * DH:k0 + (g + 1) * DH] for g in (0, 0, 1, 1)]
    columns = [cols(b[:Q_W]), cols(np.concatenate(bk)), cols(b[p0:ga0]), cols(b[ga0:gp0]), cols(b[gp0:]),
               cols(i["ln_mix_g"][0]), cols(i["ln_ffn_g"][0]), cols(i["pool_scale"][0]), cols(i["pre_mix_norm_2"][0]),
               cols(i["attn_out_norm_2"][0]), cols(i["sgu_out_norm_2"][0]), cols(i["pre_ffn_norm_2"][0]),
               i["sgu_b_spatial_2"][0].T]
    rows = [b[v0:p0], i["attn_sinks"][0], i["ln_final_g"], i["post_mix_norm_2"][0], i["sgu_ln_gain_2"][0],
            i["sgu_ln_bias_2"][0], i["post_ffn_norm_2"][0]]
    u = i["u_experts"][0].reshape(KEYS, KEYS // 2, 2, CHUNKS, P)
    return {
        "x": i["x"][0],
        "positions": np.ascontiguousarray(i["positions_2"][0].reshape(TILES, P).T),
        "weights": weights,
        "u_tiles": np.ascontiguousarray(u.transpose(1, 4, 2, 3, 0)).reshape(KEYS // 2, P, ITEM),
        "v_experts": i["v_experts"][0],
        "columns": np.ascontiguousarray(np.concatenate(columns, axis=1)),
        "rows": np.ascontiguousarray(np.concatenate(rows)[None]),
        "tables": shape_tables(),
        "w_pool_grp": np.ascontiguousarray(i["w_pool_grp"][0].transpose(1, 0, 2)),
        "sub_keys": np.ascontiguousarray(i["sub_keys"][0].reshape(2 * PHEADS, KEYS, P).transpose(2, 0, 1)),
        "w_spatial": np.ascontiguousarray(i["sgu_w_spatial_2"][0].transpose(2, 0, 1)),
    }


def shape_tables():
    q, k = np.arange(P)[:, None], np.arange(2 * P)[None, :] - P
    near = (q - k >= 0) & (q - k < P)
    dist = q - (np.arange(SEQ)[None, :] - (SEQ - P))
    times = ((dist >= 0) & (dist <= 128)) * 1.0 + ((dist >= 0) & (dist % 4 == 0)) + ((dist >= 0) & (dist % 16 == 0))
    count = np.minimum(np.arange(1, PAD + 1)[None, :], np.array(WINDOWS)[:, None]).astype(np.float32)
    freq = np.float32(500000.0) ** (-np.arange(0, 16, 2, dtype=np.float32) / np.float32(16))
    every = lambda r: np.broadcast_to(np.asarray(r, np.float32).reshape(1, -1), (P, np.size(r)))
    parts = [np.eye(P), every(np.arange(P)), every(np.arange(TOPK)), np.where(near, 0.0, MASKED), times,
             np.where(times > 0, 0.0, MASKED), every(1 / count), every(freq)]
    return np.ascontiguousarray(np.concatenate(parts, axis=1).astype(np.float32))


def kernel(**inputs):
    import concourse.bacc as bacc
    from concourse.bass_utils import run_bass_kernel_spmd as run

    nc = bacc.Bacc("TRN2", target_bir_lowering=False, num_devices=1)
    arrays, t = {}, {}
    for name, a in lay_out({k: np.asarray(v) for k, v in inputs.items()}).items():
        arrays[f"in_{name}"] = a
        t[name] = nc.dram_tensor(f"in_{name}", a.shape, mybir.dt.from_np(a.dtype), kind="ExternalInput").ap()
    out = nc.dram_tensor("out_x", (SEQ, D), F32, kind="ExternalOutput").ap()
    build(nc, t, out)
    r = run(nc, [arrays], core_ids=[0])
    return r.results[0]["out_x"].reshape(1, SEQ, D)
```

```python
from contextlib import ExitStack

import numpy as np

import concourse.bass as bass
from concourse import mybir

BF16, F32, F32R, I32, U32 = mybir.dt.bfloat16, mybir.dt.float32, mybir.dt.float32r, mybir.dt.int32, mybir.dt.uint32
ALU, ACT, AX = mybir.AluOpType, mybir.ActivationFunctionType, mybir.AxisListType

P = 128
SEQ, D = 512, 1024
TILES = SEQ // P
CHUNKS = D // P
ITEM = 2048
RAW, SPLIT = 3, 3

HEADS, KV_HEADS, DH = 16, 2, 64
Q_W, KV_W, POOL_W = HEADS * DH, KV_HEADS * DH, 512
WINDOWS = (2, 4, 8, 16)
PAD = 16
EPS1 = 1e-5
SCALE = DH ** -0.5
MASKED = -1e30

PHEADS, KEYS, TOPK = 8, 128, 16
LOWEST = -3.0e38
CAND_BANKS = 8
PAIRS = PHEADS * TOPK
J = 4
GROUPS = KEYS // J
GATE_T = 32
GATE_CHUNKS = SEQ // GATE_T
AHEAD = 3
EARLY = 18
SPILLED = EARLY - AHEAD

HEADS2, W2 = 8, 512
EPS2, LN_EPS = 1e-6, 1e-5
ROT_HALF = 8
FF = 2816
FF_CHUNKS = FF // P
FF_PARTS = (12, 10)



def value_order():
    late, spilled = list(range(EARLY, GROUPS)), list(range(SPILLED))
    order = list(range(SPILLED, EARLY))
    while late or spilled:
        if late:
            order.append(late.pop(0))
        if spilled and len(spilled) >= len(late):
            order.append(spilled.pop(0))
    return order


ORDER = value_order()
COLUMNS = [("b_q", 8), ("b_k", 2), ("b_pool", 4), ("b_ga", 8), ("b_gp", 8), ("g_mix", 8), ("g_ffn", 8),
           ("pool_scale", 4), ("g_pre_mix", 8), ("g_out", 8), ("g_pre_ffn", 8), ("b_spatial", 8)]
TABLES = [("ident", 128), ("iota", 128), ("iota_k", 16), ("window_mask", 256), ("inv_count", 64), ("inv_freq", 8)]
ROWS = [("b_v", 128), ("sinks", 16), ("g_final", 1024), ("g_post_mix", 1024), ("ln_gain", 512), ("ln_bias", 512),
        ("g_post_ffn", 1024)]


def spans(table):
    at, out = 0, {}
    for name, width in table:
        out[name] = slice(at, at + width)
        at += width
    return out, at


class Engine:

    def __init__(self, sem):
        self.sem, self.count, self.waited, self.steps = sem, 0, {}, []

    def do(self, build, *after, tell=True):
        waits = []
        for sem, value in after:
            if self.waited.get(id(sem), 0) < value:
                self.waited[id(sem)] = value
                waits.append((sem, value))
        self.steps.append((waits, build, tell))
        if tell:
            self.count += 1
            return (self.sem, self.count)

    def start_dma(self, build, sem, total, *after):
        self.do(lambda: build().then_inc(sem, 16), *after, tell=False)
        return (sem, total)

    def run(self, eng):
        for waits, build, tell in self.steps:
            for sem, value in waits:
                eng.wait_ge(sem, value)
            ins = build() if build else None
            if tell:
                ins.then_inc(self.sem, 1)


class Slot:

    def __init__(self, ap):
        self.ap, self.free = ap, ()


class Ring:
    def __init__(self, aps):
        self.slots, self.n = [Slot(a) for a in aps], 0

    def next(self):
        self.n += 1
        return self.slots[(self.n - 1) % len(self.slots)]


def build(nc, t, out):
    col, n_col = spans(COLUMNS)
    tab, n_tab = spans(TABLES)
    row, n_row = spans(ROWS)

    with ExitStack() as ctx:
        def sem(name):
            return ctx.enter_context(nc.semaphore(name))

        base = -(-nc.sbuf_base // 32) * 32
        top = [base]

        def fixed(name, shape, dt=F32):
            size = int(np.prod(shape)) * 4
            tensor = nc.alloc_sbuf_tensor_at(name, [P] + shape, dt, offset=top[0])
            top[0] += -(-size // 32) * 32
            return tensor

        columns = fixed("columns", [n_col])
        tables = fixed("tables", [n_tab])
        v_sink_rows = fixed("v_sink_rows", [144])
        neg_sinks = fixed("neg_sinks", [HEADS])
        stats = fixed("stats", [16])
        resid = fixed("resid", [TILES, D])
        xt = (fixed("xt_high", [CHUNKS, SEQ], F32R), fixed("xt_low", [CHUNKS, SEQ], F32R))
        raw_items = [fixed(f"raw_{n}", [ITEM]) for n in range(RAW)]
        split_items = [(fixed(f"high_{n}", [ITEM], F32R), fixed(f"low_{n}", [ITEM], F32R)) for n in range(SPLIT)]
        area = top[0]
        area_size = nc.sbuf_usable_end - area

        def place(name, at, shape, dt=F32):
            assert at % 32 == 0 and at + int(np.prod(shape)) * 4 <= area_size, (name, area_size)
            return nc.alloc_sbuf_tensor_at(name, [P] + shape, dt, offset=area + at)

        def column(name, c=None):
            s = col[name]
            return columns[:, s] if c is None else columns[:, s.start + c:s.start + c + 1]

        def table(name):
            return tables[:, tab[name]]

        ident = table("ident")
        banks = Ring([ctx.enter_context(nc.psum_tensor(f"bank_{n}", [P, 512], F32))[:, :] for n in range(8)])

        pe, act, dve, pool, sp = (Engine(sem(n)) for n in ("pe_done", "act_done", "dve_done", "pool_done", "sp_done"))
        V, A, T, G, S = nc.vector, nc.scalar, nc.tensor, nc.gpsimd, nc.sync

        def mm(o, l, r, start, stop, *after, tell=False):
            return pe.do(lambda: T.matmul(o, l, r, start=start, stop=stop), *after, tell=tell)

        def mm3(o, l, r, start, stop, *after, tell=False):
            mm(o, l[0], r[0], start, False, *after)
            mm(o, l[0], r[1], False, False)
            return mm(o, l[1], r[0], False, stop, tell=tell)

        def turn(o, i, *after, tell=False):
            return pe.do(lambda: T.transpose(o, i, ident), *after, tell=tell)

        def activation(o, i, f, *after, **kw):
            return act.do(lambda: A.activation(o, i, f, **kw), *after)

        def tt_op(eng, builder, o, a, b, op, *after):
            return eng.do(lambda: builder.tensor_tensor(o, a, b, op), *after)

        def vv(o, a, b, op, *after):
            return tt_op(dve, V, o, a, b, op, *after)

        def vs(o, a, s1, op0, *after, s2=None, op1=ALU.bypass):
            return dve.do(lambda: V.tensor_scalar(o, a, s1, s2, op0, op1), *after)

        def stt(o, a, s, b, op0, op1, *after):
            return dve.do(lambda: V.scalar_tensor_tensor(out=o, in0=a, scalar=s, in1=b, op0=op0, op1=op1), *after)

        def split(high, low, x, *after, low_on=None):
            h = activation(high, x, ACT.Copy, *after)
            eng, builder = low_on or (pool, G)
            return h, tt_op(eng, builder, low, x, high.bitcast(F32), ALU.subtract, h, *after)

        small_sem, x_sem = sem("small_loaded"), [sem(f"x_loaded_{n}") for n in range(TILES)]
        for n in range(TILES):
            src = t["x"][n * P:(n + 1) * P, :]
            sp.start_dma(lambda n=n, src=src: S.dma_start(resid[:, n, :], src), x_sem[n], 16)
        smalls = [(columns[:, :], t["columns"]), (tables[:, :], t["tables"]),
                  (v_sink_rows[:, :], t["rows"][0:1, 0:144].to_broadcast([P, 144]))]
        for dst, src in smalls:
            act.start_dma(lambda dst=dst, src=src: A.dma_start(dst, src), small_sem, 0)
        small = (small_sem, 16 * len(smalls))
        x_in = [(x_sem[n], 16) for n in range(TILES)]
        b_v_row, sink_row = v_sink_rows[:, 0:128], v_sink_rows[:, 128:144]

        items = []
        raw_sem = [sem(f"raw_loaded_{n}") for n in range(RAW)]
        raw_free = [()] * RAW
        split_free = [()] * SPLIT
        ready = {}
        taken = [0]

        def load_item(n):
            if n >= len(items):
                return
            r = n % RAW
            width = items[n].shape[-1]
            sp.start_dma(lambda: S.dma_start(raw_items[r][:, 0:width], items[n]), raw_sem[r], 0, *raw_free[r])

        def split_item(n):
            if n >= len(items):
                return
            r, s = n % RAW, n % SPLIT
            w = items[n].shape[-1]
            there = (raw_sem[r], 16 * (n // RAW + 1))
            ready[n] = ()
            for part, low_on in ((slice(0, w // 2), (pool, G)), (slice(w // 2, w), (dve, V))):
                ready[n] += split(split_items[s][0][:, part], split_items[s][1][:, part], raw_items[r][:, part],
                                  there, *split_free[s], low_on=low_on)
            raw_free[r] = ready[n]

        def take():
            n = taken[0]
            taken[0] += 1
            s = split_items[n % SPLIT]
            return n, (s[0], s[1]), ready[n]

        def give_back(n, done):
            split_free[n % SPLIT] = (done,)
            split_item(n + SPLIT)
            load_item(n + SPLIT + RAW)

        def start_stream():
            for n in range(RAW):
                load_item(n)
            for n in range(SPLIT):
                split_item(n)
                load_item(n + RAW)

        w_all = t["weights"]
        n_w = w_all.shape[0]
        peer_at = WEIGHTS_BEFORE_PEER
        for n in range(peer_at):
            items.append(w_all[n])

        def u_items(g):
            return [t["u_tiles"][m] for m in (2 * g, 2 * g + 1)]

        v_view = t["v_experts"].rearrange("(i m e) d -> m i (e d)", i=KEYS, e=2)

        def v_items(g):
            return [v_view[m] for m in (2 * g, 2 * g + 1)]

        for g in range(EARLY):
            items += u_items(g)
        for at, g in enumerate(ORDER):
            items += v_items(g)
            if at + AHEAD < GROUPS and ORDER[at + AHEAD] >= EARLY:
                items += u_items(ORDER[at + AHEAD])
        for n in range(peer_at, n_w):
            items.append(w_all[n])
        start_stream()

        def feature_major(x, chunks, finish):
            for pair in range(chunks // 2):
                n, w, there = take()
                k = x_chunks(x)
                for e in range(2):
                    bank = banks.next()
                    for c in range(k):
                        done = mm3(bank.ap, tuple(h[:, c * 256 + e * P:c * 256 + (e + 1) * P] for h in w),
                                   tuple(h[:, c, :] for h in x), c == 0, c == k - 1,
                                   *there, *bank.free, *(x_ready if c == 0 else ()), tell=(c == k - 1))
                    if e == 1:
                        give_back(n, done)
                    bank.free = (finish(2 * pair + e, bank.ap, done),)

        def x_chunks(x):
            return x[0].shape[1]

        def token_major(x, k_items, finish, k_last=4, by_tile=False):
            chunks = [4] * (k_items - 1) + [k_last]

            def products(bank, kk, tile, w, there):
                for c in range(chunks[kk]):
                    first, last = kk == 0 and c == 0, kk == k_items - 1 and c == chunks[kk] - 1
                    done = mm3(bank.ap, tuple(h[:, 4 * kk + c, tile * P:(tile + 1) * P] for h in x),
                               tuple(h[:, c * 512:(c + 1) * 512] for h in w), first, last,
                               *there, *x_ready, *(bank.free if first else ()), tell=(c == chunks[kk] - 1))
                return done

            if by_tile:
                held = [take() for _ in range(k_items)]
                for tile in range(TILES):
                    bank = banks.next()
                    for kk, (n, w, there) in enumerate(held):
                        done = products(bank, kk, tile, w, there)
                        if tile == TILES - 1:
                            give_back(n, done)
                    bank.free = (finish(tile, bank.ap, done),)
                return
            out_banks = [banks.next() for _ in range(TILES)]
            for kk in range(k_items):
                n, w, there = take()
                dones = [products(out_banks[tile], kk, tile, w, there) for tile in range(TILES)]
                give_back(n, dones[-1])
            for tile, bank in enumerate(out_banks):
                bank.free = (finish(tile, bank.ap, dones[tile]),)

        NORM_AT = area_size // 32 * 32 - 16384
        normed = Ring([place(f"normed_{n}", NORM_AT + n * 4096, [D])[:, :] for n in range(2)])
        squared = Ring([place(f"squared_{n}", NORM_AT + 12288 + n * 2048, [D // 2]).bitcast(BF16)[:, :]
                        for n in range(2)])
        gained = Ring([place(f"gained_{n}", NORM_AT + 8192 + n * 2048, [4, P])[:, :, :] for n in range(2)])

        def in_turn(stages, count=TILES):
            for step in range(count + len(stages) - 1):
                for k in reversed(range(len(stages))):
                    if 0 <= step - k < count:
                        stages[k](step - k)

        def rms_stages(src, width, eps, srcs_ready, extra=(), on_scalar=False):
            def square(tile):
                s = squared.next()
                if on_scalar:
                    a = activation(s.ap[:, 0:width], src(tile), ACT.Square, *srcs_ready(tile), *s.free, *extra,
                                   accum_out=stats[:, tile:tile + 1])
                else:
                    a = dve.do(lambda: V.tensor_tensor_reduce(
                        out=s.ap[:, 0:width], in0=src(tile), in1=src(tile), scale=1.0, scalar=0.0, op0=ALU.mult,
                        op1=ALU.add, accum_out=stats[:, tile:tile + 1]), *srcs_ready(tile), *s.free, *extra)
                s.free = (a,)
                made["var"] = vs(stats[:, 4 + tile:5 + tile], stats[:, tile:tile + 1], 1.0 / width, ALU.mult, a,
                                 s2=eps, op1=ALU.add)

            def root(tile, var):
                b = activation(stats[:, 4 + tile:5 + tile], stats[:, 4 + tile:5 + tile], ACT.Sqrt, var)
                return dve.do(lambda: V.reciprocal(stats[:, 8 + tile:9 + tile], stats[:, 4 + tile:5 + tile]), b)

            return square, root

        def norm_stages(src, width, eps, gain, dst, chunk0, srcs_ready, dst_free=(), extra=()):
            square, root = rms_stages(src, width, eps, srcs_ready, extra)
            var, on_way = {}, {}

            def stats_of(tile):
                square(tile)
                var[tile] = made["var"]

            def scale(tile):
                inv = root(tile, var[tile])
                s = normed.next()
                on_way[tile] = s, activation(s.ap[:, 0:width], src(tile), ACT.Copy, inv, *s.free,
                                             scale=stats[:, 8 + tile:9 + tile])

            def turned(tile):
                s, n = on_way[tile]
                for half in range(width // 512):
                    bank = banks.next()
                    for c in range(4):
                        f = (half * 4 + c) * P
                        done = turn(bank.ap[:, c * P:(c + 1) * P], s.ap[:, f:f + P], n, *bank.free, small,
                                    tell=(c == 3))
                    g = gained.next()
                    c0 = col[gain].start + chunk0 + half * 4
                    scaled = vv(g.ap, bank.ap.rearrange("p (c t) -> p c t", c=4),
                                columns[:, c0:c0 + 4].unsqueeze(2).to_broadcast([P, 4, P]), ALU.mult,
                                done, *g.free)
                    bank.free = (scaled,)
                    where = (slice(None), slice(chunk0 + half * 4, chunk0 + half * 4 + 4),
                             slice(tile * P, (tile + 1) * P))
                    g.free = split(dst[0][where], dst[1][where], g.ap, scaled, *dst_free)
                s.free = (done,)
                made["normed"] = g.free

            return [stats_of, scale, turned]

        made = {}

        in_turn(norm_stages(lambda n: resid[:, n, :], D, EPS1, "g_mix", xt, 0, lambda n: (x_in[n],)))
        x_ready = made["normed"]
        ns = vs(neg_sinks[:, :], sink_row, -1.0, ALU.mult, small)

        qt = place("qt", 0, [CHUNKS, SEQ])
        ot = (place("ot_high", 16384, [CHUNKS, SEQ], F32R), place("ot_low", 32768, [CHUNKS, SEQ], F32R))
        kt = place("kt", 49152, [KV_HEADS, SEQ])
        v_tok = place("v_tok", 53248, [TILES, KV_W])
        score = Ring([place(f"score_{n}", 55296 + n * 4096, [4, 256])[:, :, :] for n in range(3)])
        prob_t = Ring([place(f"prob_t_{n}", 67584 + n * 4096, [2, 512])[:, :, :] for n in range(2)])
        head_stat = Ring([place(f"head_stat_{n}", 75776 + n * 128, [5, 4])[:, :, :] for n in range(4)])
        o_tmp = Ring([place(f"o_tmp_{n}", 76288 + n * 2048, [4, P])[:, :, :] for n in range(2)])

        def q_finish(c, bank, done):
            made["q", c] = activation(qt[:, c, :], bank, ACT.Identity, done, bias=column("b_q", c))
            return made["q", c]

        def k_finish(c, bank, done):
            made["k", c] = activation(kt[:, c, :], bank, ACT.Identity, done, bias=column("b_k", c))
            return made["k", c]

        feature_major(xt, 8, q_finish)
        feature_major(xt, 2, k_finish)
        n, w, there = take()
        bank = banks.next()
        for tile in range(TILES):
            for c in range(CHUNKS):
                done = mm3(bank.ap[:, tile * P:(tile + 1) * P], tuple(h[:, c, tile * P:(tile + 1) * P] for h in xt),
                           tuple(h[:, c * P:(c + 1) * P] for h in w), c == 0, c == CHUNKS - 1, *there, *bank.free,
                           tell=(c == CHUNKS - 1))
        give_back(n, done)
        v_made = vv(v_tok[:, :, :], bank.ap.rearrange("p (n f) -> p n f", n=TILES),
                    b_v_row.unsqueeze(1).to_broadcast([P, TILES, KV_W]), ALU.add, done)
        bank.free = (v_made,)

        units = [(blk, g, par) for blk in range(TILES) for g in range(KV_HEADS) for par in range(2)]
        state = {}

        def scores(u):
            blk, g, par = units[u]
            rows = slice(par * DH, (par + 1) * DH)
            keys = slice(max(blk - 1, 0) * P, (blk + 1) * P)
            n = keys.stop - keys.start
            pair_banks = []
            for b in range(2):
                bank = banks.next()
                for e in range(2):
                    c = 4 * g + 2 * b + e
                    done = mm(bank.ap[:, e * 256:e * 256 + n], qt[rows, c, blk * P:(blk + 1) * P], kt[rows, g, keys],
                              True, True, *bank.free, made["q", c], made["k", g], tell=(e == 1))
                pair_banks.append((bank, done))
            state[u] = dict(s=score.next(), st=head_stat.next(), n=n, banks=pair_banks)

        def maximum(u):
            x = state[u]
            blk, g, par = units[u]
            s, st, n = x["s"], x["st"], x["n"]
            mask = table("window_mask")[:, 256 - n:256].unsqueeze(1).to_broadcast([P, 2, n])
            for b, (bank, done) in enumerate(x["banks"]):
                masked = stt(s.ap[:, 2 * b:2 * b + 2, 0:n],
                             bank.ap.rearrange("p (h k) -> p h k", h=2)[:, :, 0:n], SCALE, mask,
                             ALU.mult, ALU.add, done, *s.free)
                bank.free = (masked,)
            neg_max, sink_e = st.ap[:, 0, :], st.ap[:, 2, :]
            m = dve.do(lambda: V.tensor_reduce(neg_max, s.ap[:, :, 0:n], AX.X, ALU.max, negate=True), masked, *st.free)
            own = slice(8 * g + par, 8 * g + 8, 2)
            x["m"] = vv(neg_max, neg_max, neg_sinks[:, own], ALU.min, m, ns)
            x["d"] = vv(sink_e, neg_max, sink_row[:, own], ALU.add, x["m"])

        def exponents(u):
            x = state[u]
            s, st, n = x["s"], x["st"], x["n"]
            neg_max, total, sink_e = (st.ap[:, k, :] for k in range(3))
            for h in range(4):
                activation(s.ap[:, h, 0:n], s.ap[:, h, 0:n], ACT.Exp, x["m"], bias=neg_max[:, h:h + 1],
                           accum_out=total[:, h:h + 1])
            x["e"] = activation(sink_e, sink_e, ACT.Exp, x["d"])

        def probabilities(u):
            x = state[u]
            s, st, n = x["s"], x["st"], x["n"]
            total, sink_e, inv = (st.ap[:, k, :] for k in (1, 2, 3))
            a = vv(total, total, sink_e, ALU.add, x["e"])
            a = dve.do(lambda: V.reciprocal(inv, total), a)
            for h in range(4):
                p = vs(s.ap[:, h, 0:n], s.ap[:, h, 0:n], inv[:, h:h + 1], ALU.mult, a)
            st.free = (p,)
            x["p"] = p

        def turn_probabilities(u):
            x = state[u]
            s, n = x["s"], x["n"]
            pt = x["pt"] = prob_t.next()
            for kb in range(n // P):
                bank = banks.next()
                for h in range(4):
                    done = turn(bank.ap[:, h * P:(h + 1) * P], s.ap[:, h, kb * P:(kb + 1) * P], x["p"], *bank.free,
                                tell=(h == 3))
                x["c"] = activation(pt.ap[:, kb, :], bank.ap, ACT.Copy, done, *pt.free)
                bank.free = (x["c"],)
            s.free = (done,)

        def values(u):
            x = state.pop(u)
            blk, g, par = units[u]
            rows = slice(par * DH, (par + 1) * DH)
            nb = x["n"] // P
            bank = banks.next()
            for kb in range(nb):
                done = mm(bank.ap[rows, :], v_tok[:, blk - nb + 1 + kb, g * DH:(g + 1) * DH], x["pt"].ap[:, kb, :],
                          kb == 0, kb == nb - 1, x["c"], v_made, *bank.free, tell=(kb == nb - 1))
            x["pt"].free = (done,)
            o = o_tmp.next()
            c = dve.do(lambda: V.tensor_copy(o.ap[rows], bank.ap[rows, :].rearrange("p (c t) -> p c t", c=4)),
                       done, *o.free)
            bank.free = (c,)
            where = (rows, slice(4 * g, 4 * g + 4), slice(blk * P, (blk + 1) * P))
            o.free = split(ot[0][where], ot[1][where], o.ap[rows], c, low_on=(dve, V))
            return o.free

        def attend(count, scores, maximum, exponents, probabilities, turn_probabilities, values, between=None):
            for s in range(count + 3):
                if s < count:
                    scores(s)
                if 0 <= s - 1 < count:
                    exponents(s - 1)
                if 0 <= s - 2 < count:
                    probabilities(s - 2)
                    turn_probabilities(s - 2)
                if s < count:
                    maximum(s)
                if s >= 3:
                    last = values(s - 3)
                if between:
                    between(s)
            return last

        o_ready = attend(len(units), scores, maximum, exponents, probabilities, turn_probabilities, values)
        attended = (pe.sem, pe.count)

        POOL_AT = 49152
        padded = Ring([place(f"padded_{n}", POOL_AT + n * 2112, [PAD + SEQ])[:, :] for n in range(2)])
        sums = [place(f"sums_{n}", POOL_AT + 4224 + n * 2112, [PAD + SEQ]) for n in range(2)]
        pooled = [place(f"pooled_{n}", POOL_AT + 8448 + n * 2048, [SEQ]) for n in range(4)]
        w_group = place("w_group", POOL_AT + 16640, [4, P])
        ypt = (place("ypt_high", POOL_AT + 18688, [4, SEQ], F32R), place("ypt_low", POOL_AT + 26880, [4, SEQ], F32R))
        y_groups = Ring([place(f"y_group_{n}", POOL_AT + n * 2048, [SEQ])[:, :] for n in range(2)])
        group_sem = sem("group_matrices_loaded")
        w_group_in = act.start_dma(lambda: A.dma_start(w_group[:, :, :], t["w_pool_grp"]), group_sem, 16, attended,
                                   *o_ready)
        zeroed = [dve.do(lambda s=s: V.memset(s.ap[:, 0:PAD], 0.0), attended, *o_ready) for s in padded.slots]

        def pool_finish(g, bank, done):
            p = padded.next()
            a = activation(p.ap[:, PAD:], bank, ACT.Identity, done, *zeroed, *p.free, bias=column("b_pool", g))
            src, reach, last = p.ap, 1, a
            for k in range(g + 1):
                dst = sums[k % 2][:, :]
                lo = 2 * reach - 1
                last = vv(dst[:, lo:], src[:, lo:], src[:, lo - reach:PAD + SEQ - reach], ALU.add, last, *zeroed)
                src, reach = dst, 2 * reach
            o = pooled[g][:, :]
            inv = table("inv_count").rearrange("p (g k) -> p g k", g=4)[:, g, :]
            b = stt(o[:, PAD:], src[:, 2 * PAD:], 1.0 / WINDOWS[g], p.ap[:, 2 * PAD:], ALU.mult, ALU.subtract, last)
            b = vv(o[:, 0:PAD], src[:, PAD:2 * PAD], inv, ALU.mult, b)
            b = vv(o[:, 0:PAD], o[:, 0:PAD], p.ap[:, PAD:2 * PAD], ALU.subtract, b)
            p.free = (b,)
            made["pooled"] = b
            return a

        feature_major(xt, 4, pool_finish)

        ya = place("ya", 0, [CHUNKS, SEQ])
        x_ready_norm, x_ready = x_ready, o_ready

        def ya_finish(c, bank, done):
            made["ya", c] = activation(ya[:, c, :], bank, ACT.Copy, done, attended)
            return made["ya", c]

        feature_major(ot, 8, ya_finish)
        ot_read = (pe.sem, pe.count)
        x_ready = x_ready_norm
        for g in range(4):
            bank = banks.next()
            done = mm(bank.ap, w_group[:, g, :], pooled[g][:, :], True, True, made["pooled"], w_group_in, *bank.free,
                      tell=True)
            y = y_groups.next()
            a = vs(y.ap, bank.ap, column("pool_scale", g), ALU.mult, done, *y.free, made["pooled"])
            bank.free = (a,)
            y.free = split(ypt[0][:, g, :], ypt[1][:, g, :], y.ap, a, low_on=(dve, V))
        y_ready = y.free

        merged = (place("merged_high", 16384, [CHUNKS, SEQ], F32R), place("merged_low", 32768, [CHUNKS, SEQ], F32R))
        gate = Ring([place(f"gate_{n}", POOL_AT + n * 2048, [SEQ])[:, :] for n in range(4)])
        for s in gate.slots:
            s.free = (*y_ready, done)

        for pair in range(4):
            a_items = take()
            halves = {}
            for kind, bias in (("a", "b_ga"), ("p", "b_gp")):
                n, w, there = a_items if kind == "a" else take()
                for e in range(2):
                    c = 2 * pair + e
                    bank = banks.next()
                    for k in range(CHUNKS):
                        done = mm3(bank.ap, tuple(h[:, k * 256 + e * P:k * 256 + (e + 1) * P] for h in w),
                                   tuple(h[:, k, :] for h in xt), k == 0, k == CHUNKS - 1, *there, *bank.free,
                                   tell=(k == CHUNKS - 1))
                    gt = gate.next()
                    s = activation(gt.ap, bank.ap, ACT.Sigmoid, done, *gt.free, bias=column(bias, c))
                    bank.free = (s,)
                    halves[kind, e] = (gt, s)
                give_back(n, done)
            n, w, there = take()
            for e in range(2):
                c = 2 * pair + e
                bank = banks.next()
                for k in range(4):
                    done = mm3(bank.ap, tuple(h[:, k * 256 + e * P:k * 256 + (e + 1) * P] for h in w),
                               tuple(h[:, k, :] for h in ypt), k == 0, k == 3, *there, *y_ready, *bank.free,
                               tell=(k == 3))
                (ga, sa), (gp, sg) = halves["a", e], halves["p", e]
                m1 = vv(ga.ap, ga.ap, ya[:, c, :], ALU.mult, sa, made["ya", c])
                m2 = vv(gp.ap, gp.ap, bank.ap, ALU.mult, sg, done)
                bank.free = (m2,)
                m3 = vv(ga.ap, ga.ap, gp.ap, ALU.add, m1, m2)
                gp.free = (m3,)
                ga.free = split(merged[0][:, c, :], merged[1][:, c, :], ga.ap, m3, ot_read, *y_ready)
            give_back(n, done)
        x_ready = ga.free

        added = {}

        def residual_add(half):
            def finish(tile, bank, done):
                r = resid[:, tile, half * 512:(half + 1) * 512]
                added[tile] = vv(r, r, bank, ALU.add, done)
                return added[tile]
            return finish

        for half in range(2):
            token_major(merged, 2, residual_add(half), by_tile=(half == 1))
        mixed_in = (pe.sem, pe.count)

        in_turn(norm_stages(lambda n: resid[:, n, :], D, EPS1, "g_ffn", xt, 0, lambda n: (added[n],),
                            extra=(*y_ready, *x_ready)))
        x_ready = made["normed"]

        hidden = Ring([place(f"hidden_{n}", n * 8192, [J, SEQ])[:, :, :] for n in range(AHEAD)])
        sub_keys = place("sub_keys", 24576, [2 * PHEADS, KEYS])
        query = Ring([place(f"query_{n}", 32768 + n * 2048, [SEQ])[:, :] for n in range(2)])
        key_score = Ring([place(f"key_score_{n}", 36864 + n * 2048, [TILES, KEYS])[:, :, :] for n in range(2)])
        top_v = place("top_v", 40960, [TILES, 2 * PHEADS, TOPK])
        top_i = place("top_i", 45056, [TILES, 2 * PHEADS, TOPK], U32)
        top_f = place("top_f", 49152, [TILES, 2 * PHEADS, TOPK])
        cand = place("cand", 53248, [PHEADS, TOPK * TOPK])
        same = place("same", 32768, [PAIRS, TOPK])
        names = ["best", "pos", "pos_a", "pos_b", "a_f", "b_f", "first", "second", "gate_w", "shifted"]
        small_at = {n: place(n, 61440 + 512 * k, [PHEADS, TOPK], U32 if n in ("pos", "pos_a", "pos_b") else F32)
                    for k, n in enumerate(names)}
        gate_sum = place("gate_sum", 61440 + 512 * len(names), [2, PHEADS])
        pair_t = place("pair_t", 79424, [3, SEQ])

        keys_sem = sem("sub_keys_loaded")
        keys_in = act.start_dma(lambda: A.dma_start(sub_keys[:, :, :], t["sub_keys"]), keys_sem, 16, mixed_in, *ga.free)

        def query_finish(c, bank, done):
            q = query.next()
            a = activation(q.ap, bank, ACT.Copy, done, *q.free)
            made["query"] = (q, a)
            return a

        def best_keys(c):
            q, a = made["query"]
            bank = banks.next()
            for tile in range(TILES):
                done = mm(bank.ap[:, tile * P:(tile + 1) * P], q.ap[:, tile * P:(tile + 1) * P], sub_keys[:, c, :],
                          True, True, a, keys_in, *bank.free, tell=(tile == TILES - 1))
            q.free = (done,)
            s = key_score.next()
            b = activation(s.ap, bank.ap.rearrange("p (n k) -> p n k", n=TILES), ACT.Copy, done, *s.free)
            bank.free = (b,)
            last = b
            for tile in range(TILES):
                v, i, x = top_v[:, tile, c, :], top_i[:, tile, c, :], s.ap[:, tile, :]
                last = top16(v, i, x, last)
            s.free = (last,)
            return last

        def top16(v, i, x, *after):
            a = dve.do(lambda: V.max(v[:, 0:8], x), *after)
            dve.do(lambda: V.max_index(i[:, 0:8], v[:, 0:8], x), a)
            b = dve.do(lambda: V.match_replace(x, v[:, 0:8], x, LOWEST), (dve.sem, dve.count))
            c = dve.do(lambda: V.max(v[:, 8:16], x), b)
            return dve.do(lambda: V.max_index(i[:, 8:16], v[:, 8:16], x), c)

        def chunk_of(n, w, there, e):
            bank = banks.next()
            for k in range(CHUNKS):
                done = mm3(bank.ap, tuple(h[:, k * 256 + e * P:k * 256 + (e + 1) * P] for h in w),
                           tuple(h[:, k, :] for h in xt), k == 0, k == CHUNKS - 1, *there, *x_ready, *bank.free,
                           tell=(k == CHUNKS - 1))
            if e == 1:
                give_back(n, done)
            return bank, done

        for c in range(2 * PHEADS):
            if c % 2 == 0:
                item = take()
            bank, done = chunk_of(*item, c % 2)
            if c:
                best_keys(c - 1)
            bank.free = (query_finish(c, bank.ap, done),)
        keys_done = best_keys(2 * PHEADS - 1)

        spill = nc.dram_tensor("spilled_hidden", [SPILLED, P, J * SEQ], F32, kind="Internal").ap()
        spill_sem = [sem(f"hidden_stored_{n}") for n in range(AHEAD)]
        reload_sem = [sem(f"hidden_loaded_{n}") for n in range(AHEAD)]
        spills, reloads = [0] * AHEAD, [0] * AHEAD
        held = {}

        def hidden_steps(g, j, ring):
            if j == 0:
                held["slot"] = hidden.next()
            if j % 2 == 0:
                held["item"] = take()
            slot, (n, w, there) = held["slot"], held["item"]
            bank = ring.next()
            for k in range(CHUNKS):
                at = (j % 2 * CHUNKS + k) * P
                done = mm3(bank.ap, tuple(h[:, at:at + P] for h in w), tuple(h[:, k, :] for h in xt),
                           k == 0, k == CHUNKS - 1, *there, *bank.free, tell=(k == CHUNKS - 1))
                if k < CHUNKS - 1:
                    yield
            if j % 2 == 1:
                give_back(n, done)
            a = activation(slot.ap[:, j, :], bank.ap, ACT.Gelu, done, *slot.free, *x_ready)
            bank.free = (a,)
            made["hidden", g] = (slot, (a,))
            if j == J - 1 and g < SPILLED:
                k = g % AHEAD
                spills[k] += 16
                src = slot.ap.rearrange("p j t -> p (j t)")
                st = act.start_dma(lambda: A.dma_start(spill[g], src), spill_sem[k], spills[k], a)
                slot.free = (st,)
                made["spilled", g] = st

        def expert_hidden(g, j):
            for _ in hidden_steps(g, j, banks):
                pass

        def reload_hidden(g):
            slot = hidden.next()
            k = (hidden.n - 1) % AHEAD
            reloads[k] += 16
            dst = slot.ap.rearrange("p j t -> p (j t)")
            there = act.start_dma(lambda: A.dma_start(dst, spill[g]), reload_sem[k], reloads[k], *slot.free,
                                  made["spilled", g])
            made["hidden", g] = (slot, (there,))

        early = [(g, j) for g in range(EARLY) for j in range(J)]

        as_float = dve.do(lambda: V.tensor_copy(top_f[:, :, :, :], top_i[:, :, :, :]), keys_done)
        free_small = ()
        for tile in range(TILES):
            def half(x, which):
                return x[:, tile, :, :].rearrange("p (h two) k -> p two h k", two=2)[:, which, :, :]
            a = vv(cand[:, :, :].rearrange("p h (a b) -> p h a b", a=TOPK),
                   half(top_v, 0).unsqueeze(3).to_broadcast([P, PHEADS, TOPK, TOPK]),
                   half(top_v, 1).unsqueeze(2).to_broadcast([P, PHEADS, TOPK, TOPK]), ALU.add, keys_done,
                   (dve.sem, dve.count))
            best, pos, pos_a, pos_b, a_f, b_f, first, second, gate_w, shifted = (small_at[n][:, :, :] for n in names)
            last = a
            for h in range(PHEADS):
                last = top16(best[:, h, :], pos[:, h, :], cand[:, h, :], last, *free_small)
            ua = dve.do(lambda: V.tensor_scalar(pos_a, pos, 4, None, ALU.logical_shift_right), last)
            ub = dve.do(lambda: V.tensor_scalar(pos_b, pos, 15, None, ALU.bitwise_and), last)
            fa = dve.do(lambda: V.tensor_copy(a_f, pos_a), ua)
            fb = dve.do(lambda: V.tensor_copy(b_f, pos_b), ub)
            d = vv(shifted, best, best[:, :, 0:1].to_broadcast([P, PHEADS, TOPK]), ALU.subtract, last)
            iota_k = table("iota_k").unsqueeze(1).to_broadcast([P, PAIRS, TOPK])
            for which, at, dst, f in ((0, a_f, first, fa), (1, b_f, second, fb)):
                flat = at.rearrange("p h k -> p (h k)")
                x = vv(same[:, :, :], iota_k, flat.unsqueeze(2).to_broadcast([P, PAIRS, TOPK]), ALU.is_equal, f,
                       as_float, (dve.sem, dve.count))
                s4 = same[:, :, :].rearrange("p (h k) a -> p h k a", h=PHEADS)
                x = vv(s4, s4, half(top_f, which).unsqueeze(2).to_broadcast([P, PHEADS, TOPK, TOPK]), ALU.mult, x)
                looked = dve.do(lambda dst=dst: V.tensor_reduce(dst.rearrange("p h k -> p (h k)"), same[:, :, :], AX.X,
                                                                ALU.add), x, *free_small)
            for _ in range(CAND_BANKS):
                expert_hidden(*early.pop(0))
            ex = activation(shifted, shifted, ACT.Exp, d)
            y = dve.do(lambda: V.tensor_reduce(gate_sum[:, 0, :], shifted, AX.X, ALU.add), ex)
            y = dve.do(lambda: V.reciprocal(gate_sum[:, 1, :], gate_sum[:, 0, :]), y)
            y = vv(gate_w, shifted, gate_sum[:, 1, :].unsqueeze(2).to_broadcast([P, PHEADS, TOPK]), ALU.mult, y)
            bank = banks.next()
            for k, src in enumerate((first, second, gate_w)):
                done = turn(bank.ap[:, k * P:(k + 1) * P], src.rearrange("p h k -> p (h k)"), looked, y, *bank.free,
                            tell=(k == 2))
            free_small = (done,)
            pairs_ready = activation(pair_t[:, :, tile * P:(tile + 1) * P],
                                     bank.ap[:, 0:3 * P].rearrange("p (k t) -> p k t", k=3), ACT.Copy, done)
            bank.free = (pairs_ready,)
        chosen = (dve.sem, dve.count)

        gates = nc.dram_tensor("expert_gates", [GATE_CHUNKS, KEYS, KEYS, GATE_T], F32, kind="Internal").ap()
        staged = Ring([place(f"staged_{n}", 24576 + n * 16384, [KEYS, GATE_T])[:, :, :] for n in range(2)])
        hot_i, hot_high, hot_low = (
            Ring([place(f"{name}_{n}", 57344 + (at + n) * 2048, [4, KEYS], F32R)[:, :, :] for n in range(depth)])
            for name, at, depth in (("hot_i", 0, 4), ("hot_j_high", 4, 3), ("hot_j_low", 7, 3)))
        stored_sem = [sem(f"gates_stored_{n}") for n in range(2)]
        for s in hot_i.slots + hot_high.slots + hot_low.slots + staged.slots:
            s.free = (chosen, pairs_ready, done)
        quads = SEQ // 4
        hot_banks, out_banks, hidden_banks = Ring([]), Ring([]), Ring([])
        hot_banks.slots, out_banks.slots, hidden_banks.slots = banks.slots[0:3], banks.slots[3:6], banks.slots[6:8]
        hot = {}

        def one_hots(quad):
            if quad >= quads:
                return
            tok = 4 * quad
            hi_, hj_ = hot_i.next(), hot_banks.next()
            for k in range(4):
                o, i = hi_.ap[:, k, :], pair_t[:, 0, tok + k:tok + k + 1]
                if k < 3:
                    a1 = pool.do(lambda o=o, i=i: G.tensor_scalar(o, table("iota"), i, None, ALU.is_equal),
                                 pairs_ready, *hi_.free)
                else:
                    a2 = vs(o, table("iota"), i, ALU.is_equal, pairs_ready, *hi_.free)
            for k in range(4):
                b = vs(hj_.ap[:, k * P:(k + 1) * P], table("iota"), pair_t[:, 1, tok + k:tok + k + 1], ALU.is_equal,
                       pairs_ready, *hj_.free, s2=pair_t[:, 2, tok + k:tok + k + 1], op1=ALU.mult)
            hot[quad] = hi_, hj_, (a1, a2), b

        def split_hots(quad):
            if quad >= quads:
                return
            hi_, hj_, i_ready, j_ready = hot.pop(quad)
            hh_, hl_ = hot_high.next(), hot_low.next()
            hj_.free = split(hh_.ap, hl_.ap, hj_.ap.rearrange("p (t j) -> p t j", t=4), j_ready, *hh_.free, *hl_.free, low_on=(dve, V))
            hots[quad] = hi_, hh_, hl_, (*i_ready, *hj_.free)

        hots = {}
        def early_steps():
            for g, j in early:
                yield from hidden_steps(g, j, hidden_banks)
                yield

        steps, between = early_steps(), len(early) * CHUNKS
        one_hots(0)
        one_hots(1)
        split_hots(0)
        one_hots(2)
        split_hots(1)
        for quad in range(quads):
            one_hots(quad + 3)
            split_hots(quad + 2)
            tok = 4 * quad
            chunk = tok // GATE_T
            if tok % GATE_T == 0:
                stage = staged.next()
            hi_, hh_, hl_, there = hots.pop(quad)
            bank = out_banks.next()
            for k in range(4):
                o = bank.ap[:, k * P:(k + 1) * P]
                mm(o, hi_.ap[:, k, :], hh_.ap[:, k, :], True, False, *there, *bank.free)
                done = mm(o, hi_.ap[:, k, :], hl_.ap[:, k, :], False, True, tell=(k == 3))
            hi_.free = hh_.free = hl_.free = (done,)
            t0 = tok % GATE_T
            e = activation(stage.ap[:, :, t0:t0 + 4].rearrange("p j t -> p t j"),
                           bank.ap.rearrange("p (t j) -> p t j", t=4), ACT.Copy, done, *stage.free)
            bank.free = (e,)
            if t0 == GATE_T - 4:
                total = 16 * (chunk // 2 + 1)
                st = act.start_dma(lambda stage=stage, chunk=chunk: A.dma_start(gates[chunk], stage.ap),
                                   stored_sem[chunk % 2], total, e)
                stage.free = (st,)
            for _ in range((quad + 1) * between // quads - quad * between // quads):
                next(steps)
        all_stored = [s.free[0] for s in staged.slots]
        gates_built = (pe.sem, pe.count)

        gate_in = Ring([place(f"gate_in_{n}", 24576 + n * 8192, [GATE_CHUNKS, J * GATE_T])[:, :, :] for n in range(2)])
        weight = Ring([(place(f"weight_high_{n}", 40960 + n * 16384, [J, SEQ], F32R),
                        place(f"weight_low_{n}", 40960 + n * 16384 + 8192, [J, SEQ], F32R)) for n in range(2)])
        gate_sem = [sem(f"gates_loaded_{n}") for n in range(2)]
        for s in weight.slots:
            s.free = (gates_built, *all_stored)
        gate_there = {}

        def load_gates(at):
            if at >= GROUPS:
                return
            g = ORDER[at]
            s = gate_in.next()
            src = gates[:, :, g * J:(g + 1) * J, :].rearrange("c i j t -> i c (j t)")
            gate_there[g] = (s, act.start_dma(lambda: A.dma_start(s.ap, src), gate_sem[at % 2], 16 * (at // 2 + 1),
                                              *all_stored, *s.free))

        def weigh(at):
            if at >= GROUPS:
                return
            g = ORDER[at]
            slot, a = made["hidden", g]
            gs, there = gate_there[g]
            w = weight.next()
            h = slot.ap.rearrange("p j (c t) -> p j c t", t=GATE_T)
            m = vv(h, h, gs.ap.rearrange("p c (j t) -> p j c t", j=J), ALU.mult, *a, there)
            gs.free = (m,)
            load_gates(at + 2)
            done = split(w.ap[0][:, :, :], w.ap[1][:, :, :], slot.ap, m, *w.free, low_on=(dve, V))
            slot.free = done
            made["weight", g] = (w, done)

        load_gates(0)
        load_gates(1)
        weigh(0)
        for at_group, g in enumerate(ORDER):
            weigh(at_group + 1)
            w, w_ready = made["weight", g]
            pair = [take() for _ in range(2)]
            for two in range(0, TILES, 2):
                outs = [(tile, half, banks.next()) for tile in (two, two + 1) for half in range(2)]
                for e, (n, v, there) in enumerate(pair):
                    for tile, half, bank in outs:
                        for j in (2 * e, 2 * e + 1):
                            at = (j % 2) * D + half * 512
                            done = mm3(bank.ap, tuple(h[:, j, tile * P:(tile + 1) * P] for h in w.ap),
                                       tuple(h[:, at:at + 512] for h in v), j == 0, j == J - 1,
                                       *there, *w_ready, *bank.free, tell=(j % 2 == 1))
                        if e == 1:
                            r = resid[:, tile, half * 512:(half + 1) * 512]
                            added[tile] = vv(r, r, bank.ap, ALU.add, done)
                            bank.free = (added[tile],)
                    if two == TILES - 2:
                        give_back(n, done)
            w.free = (done,)
            if at_group + AHEAD < GROUPS:
                then = ORDER[at_group + AHEAD]
                if then < SPILLED:
                    reload_hidden(then)
                else:
                    for j in range(J):
                        expert_hidden(then, j)
        experts_done = (pe.sem, pe.count)

        row_sem = [sem(f"row_loaded_{n}") for n in range(4)]

        def load_row(name, first, last, at, k, *after):
            width = row[last].stop - row[first].start
            dst = place(name, at, [width])
            src = t["rows"][0:1, row[first].start:row[last].stop].to_broadcast([P, width])
            return dst, act.start_dma(lambda: A.dma_start(dst[:, :], src), row_sem[k], 16, *after)

        last_weigh = made["weight", ORDER[-1]][1]
        g_final, g_final_in = load_row("g_final_row", "g_final", "g_final", 0, 0, experts_done, *last_weigh)
        square, root = rms_stages(lambda n: resid[:, n, :], D, EPS1, lambda n: (added[n],), (experts_done, *last_weigh))
        var = {}

        def final_square(tile):
            square(tile)
            var[tile] = made["var"]

        def final_scale(tile):
            r = resid[:, tile, :]
            added[tile] = stt(r, r, stats[:, 8 + tile:9 + tile], g_final[:, :], ALU.mult, ALU.mult,
                              root(tile, var[tile]), g_final_in)

        in_turn([final_square, final_scale] + norm_stages(lambda n: resid[:, n, :], D, EPS2, "g_pre_mix", xt, 0,
                                                          lambda n: (added[n],)))
        x_ready = made["normed"]
        scaled_all = added[TILES - 1]

        pos_i = place("pos_i", 65536, [TILES], I32)
        pos_f = place("pos_f", 65568, [TILES])
        angle = place("angle", 65600, [TILES, ROT_HALF])
        turns_i = place("turns_i", 65728, [TILES, ROT_HALF], I32)
        turns = place("turns", 65856, [TILES, ROT_HALF])
        over = place("over", 65984, [TILES, ROT_HALF])
        sin_a = place("sin_a", 66112, [TILES, ROT_HALF])
        cos_a = place("cos_a", 66240, [TILES, ROT_HALF])
        rot = place("rot", 66368, [4, 2 * HEADS2 * ROT_HALF])
        pos_sem = sem("positions_loaded")
        pos_in = act.start_dma(lambda: A.dma_start(pos_i[:, :], t["positions"]), pos_sem, 16, experts_done, *last_weigh)
        times_never = place("times_never", 77952, [2 * SEQ])
        masks_sem = sem("dilated_masks_loaded")
        masks_in = act.start_dma(lambda: A.dma_start(times_never[:, :], t["dilated_masks"]), masks_sem, 16, *x_ready)
        times, never = times_never[:, 0:SEQ], times_never[:, SEQ:2 * SEQ]
        TWO_PI = 2 * np.pi
        part1 = 6.28125
        part2 = float(np.float32(np.round((TWO_PI - part1) * 2 ** 21) / 2 ** 21))
        part3 = float(np.float32(TWO_PI - part1 - part2))
        PI_IN = float(np.nextafter(np.float32(np.pi), np.float32(0)))
        a = dve.do(lambda: V.tensor_copy(pos_f[:, :], pos_i[:, :]), pos_in)
        a = vv(angle[:, :, :], pos_f[:, :].unsqueeze(2).to_broadcast([P, TILES, ROT_HALF]),
               table("inv_freq").unsqueeze(1).to_broadcast([P, TILES, ROT_HALF]), ALU.mult, a, small)
        a = vs(turns[:, :, :], angle[:, :, :], 1 / TWO_PI, ALU.mult, a)
        a = dve.do(lambda: V.tensor_copy(turns_i[:, :, :], turns[:, :, :]), a)
        a = dve.do(lambda: V.tensor_copy(turns[:, :, :], turns_i[:, :, :]), a)
        for part in (part1, part2, part3):
            a = stt(angle[:, :, :], turns[:, :, :], -part, angle[:, :, :], ALU.mult, ALU.add, a)

        def wrap(x, a):
            for limit, op, step in ((float(np.pi), ALU.is_gt, -TWO_PI), (-float(np.pi), ALU.is_lt, TWO_PI)):
                a = vs(over[:, :, :], x, limit, op, a, s2=step, op1=ALU.mult)
                a = vv(x, x, over[:, :, :], ALU.add, a)
            return vs(x, x, PI_IN, ALU.min, a, s2=-PI_IN, op1=ALU.max)

        a = vs(cos_a[:, :, :], angle[:, :, :], float(np.pi / 2), ALU.add, a)
        a = wrap(angle[:, :, :], a)
        b = activation(sin_a[:, :, :], angle[:, :, :], ACT.Sin, a)
        a = wrap(cos_a[:, :, :], a)
        rope_ready = activation(cos_a[:, :, :], cos_a[:, :, :], ACT.Sin, a)

        qk = place("qk", 0, [2, TILES, W2])
        v2 = place("v2", 16384, [TILES, W2])
        u_gate = place("u_gate", 24576, [TILES, W2])
        v_gate = place("v_gate", 32768, [TILES, W2])
        q2t = place("q2t", 40960, [4, SEQ])
        k2t = place("k2t", 49152, [4, SEQ])

        def qk_finish(which):
            def finish(tile, bank, done):
                made["qk", which, tile] = activation(qk[:, which, tile, :], bank, ACT.Copy, done, scaled_all)
                return made["qk", which, tile]
            return finish

        def v_finish(tile, bank, done):
            made["v2", tile] = activation(v2[:, tile, :], bank, ACT.Copy, done, *x_ready)
            return made["v2", tile]

        def gelu_finish(dst, sums):
            def finish(tile, bank, done):
                kw = dict(accum_out=sums[:, tile:tile + 1]) if sums is not None else {}
                made[id(dst), tile] = activation(dst[:, tile, :], bank, ACT.Gelu, done, *x_ready, **kw)
                return made[id(dst), tile]
            return finish

        token_major(xt, 2, qk_finish(0))
        token_major(xt, 2, qk_finish(1))
        for tile in range(TILES):
            x = qk[:, :, tile, :].rearrange("p w (h f) -> p w h f", h=HEADS2)
            x1, x2 = x[:, :, :, 0:ROT_HALF], x[:, :, :, ROT_HALF:2 * ROT_HALF]
            cs, sn = (z[:, tile, :].unsqueeze(1).unsqueeze(1).to_broadcast([P, 2, HEADS2, ROT_HALF])
                      for z in (cos_a, sin_a))
            r = [rot[:, k, :].rearrange("p (w h f) -> p w h f", w=2, h=HEADS2) for k in range(4)]
            after = (made["qk", 0, tile], made["qk", 1, tile], rope_ready, (dve.sem, dve.count))
            m = [vv(r[k], y, z, ALU.mult, *after) for k, (y, z) in enumerate(((x1, cs), (x2, sn), (x2, cs), (x1, sn)))]
            vv(x1, r[0], r[1], ALU.subtract, *m)
            made["rot", tile] = vv(x2, r[2], r[3], ALU.add, *m)
        token_major(xt, 2, v_finish)
        for which, dst in ((0, q2t), (1, k2t)):
            for tile in range(TILES):
                bank = banks.next()
                for c in range(4):
                    done = turn(bank.ap[:, c * P:(c + 1) * P], qk[:, which, tile, c * P:(c + 1) * P],
                                made["rot", tile], *bank.free, tell=(c == 3))
                made["t", which, tile] = activation(dst[:, :, tile * P:(tile + 1) * P],
                                                    bank.ap.rearrange("p (c t) -> p c t", c=4), ACT.Copy, done)
                bank.free = (made["t", which, tile],)
        qk_turned = done
        v_mean = stats[:, 12:16]
        token_major(xt, 2, gelu_finish(u_gate, None))
        token_major(xt, 2, gelu_finish(v_gate, v_mean))
        projected = (pe.sem, pe.count)

        score2 = Ring([place(f"score2_{n}", 57344 + n * 4096, [2, SEQ])[:, :, :] for n in range(3)])
        prob2 = Ring([place(f"prob2_{n}", 69632 + n * 4096, [2, SEQ])[:, :, :] for n in range(2)])
        stat2 = Ring([place(f"stat2_{n}", 77824 + n * 32, [3, 2])[:, :, :] for n in range(4)])
        o2 = place("o2", 0, [TILES, W2])
        units2 = [(tile, c) for tile in range(TILES) for c in range(4)]
        for s in score2.slots + prob2.slots:
            s.free = (*x_ready, rope_ready, made["rot", TILES - 1])

        def scores2(u):
            tile, c = units2[u]
            n = (tile + 1) * P
            two = []
            for par in range(2):
                rows = slice(par * DH, (par + 1) * DH)
                bank = banks.next()
                done = mm(bank.ap[:, 0:n], q2t[rows, c, tile * P:(tile + 1) * P], k2t[rows, c, 0:n], True, True,
                          made["t", 0, tile], *(made["t", 1, k] for k in range(tile + 1)), *bank.free, tell=True)
                two.append((bank, done))
            state[u] = dict(s=score2.next(), st=stat2.next(), n=n, banks=two)

        def maximum2(u):
            x = state[u]
            s, st, n = x["s"], x["st"], x["n"]
            for par, (bank, done) in enumerate(x["banks"]):
                masked = stt(s.ap[:, par, 0:n], bank.ap[:, 0:n], SCALE, never[:, SEQ - n:], ALU.mult, ALU.add,
                             done, masks_in, *s.free)
                bank.free = (masked,)
            x["m"] = dve.do(lambda: V.tensor_reduce(st.ap[:, 0, :], s.ap[:, :, 0:n], AX.X, ALU.max, negate=True),
                            masked, *st.free)

        def exponents2(u):
            x = state[u]
            s, n = x["s"], x["n"]
            for par in range(2):
                x["e"] = activation(s.ap[:, par, 0:n], s.ap[:, par, 0:n], ACT.Exp, x["m"],
                                    bias=x["st"].ap[:, 0, par:par + 1])

        def probabilities2(u):
            x = state[u]
            s, st, n = x["s"], x["st"], x["n"]
            for par in range(2):
                p = dve.do(lambda par=par: V.tensor_tensor_reduce(
                    out=s.ap[:, par, 0:n], in0=s.ap[:, par, 0:n], in1=times[:, SEQ - n:], scale=1.0,
                    scalar=0.0, op0=ALU.mult, op1=ALU.add, accum_out=st.ap[:, 1, par:par + 1]), x["e"])
            x["p"] = p
            x["inv"] = dve.do(lambda: V.reciprocal(st.ap[:, 2, :], st.ap[:, 1, :]), p)

        def turn_probabilities2(u):
            x = state[u]
            s, n = x["s"], x["n"]
            pt = x["pt"] = prob2.next()
            for par in range(2):
                bank = banks.next()
                for kb in range(n // P):
                    done = turn(bank.ap[:, kb * P:(kb + 1) * P], s.ap[:, par, kb * P:(kb + 1) * P], x["p"],
                                *bank.free, tell=(kb == n // P - 1))
                x["c"] = activation(pt.ap[:, par, 0:n], bank.ap[:, 0:n], ACT.Copy, done, *pt.free)
                bank.free = (x["c"],)
            s.free = (done,)

        def values2(u):
            x = state.pop(u)
            tile, cc = units2[u]
            bank = banks.next()
            for par in range(2):
                head = 2 * cc + par
                for kb in range(tile + 1):
                    done = mm(bank.ap[:, par * DH:(par + 1) * DH], x["pt"].ap[:, par, kb * P:(kb + 1) * P],
                              v2[:, kb, head * DH:(head + 1) * DH], kb == 0, kb == tile, x["c"],
                              made["v2", kb], *bank.free, tell=(kb == tile))
            x["pt"].free = (done,)
            o = vv(o2[:, tile, cc * P:(cc + 1) * P].rearrange("p (h f) -> p h f", h=2),
                   bank.ap[:, 0:P].rearrange("p (h f) -> p h f", h=2),
                   x["st"].ap[:, 2, :].unsqueeze(2).to_broadcast([P, 2, DH]), ALU.mult, done, x["inv"], qk_turned)
            bank.free = x["st"].free = (o,)
            made["o2", tile] = o

        ln_rows, ln_rows_in = load_row("ln_rows", "ln_gain", "ln_bias", 12288, 1, qk_turned)
        w_sp = place("w_sp", 8192, [8, P])
        sp_sem = sem("spatial_loaded")
        w_sp_in = act.start_dma(lambda: A.dma_start(w_sp[:, :, :], t["w_spatial"]), sp_sem, 16, qk_turned)
        causal = pool.do(lambda: G.affine_select(out=w_sp[:, :, :], in_=w_sp[:, :, :], compare_op=ALU.is_ge, fill=0.0,
                                                 base=0, pattern=[[0, 8], [1, P]], channel_multiplier=-1), w_sp_in)
        square_v = Ring([place(f"square_v_{n}", 82048 + n * 1024, [W2 // 2]).bitcast(BF16)[:, :] for n in range(2)])

        def centre(tile):
            if tile == 0:
                made["mean"] = vs(v_mean, v_mean, -1.0 / W2, ALU.mult, made[id(v_gate), TILES - 1])
            v, s = v_gate[:, tile, :], square_v.next()
            a = vs(v, v, v_mean[:, tile:tile + 1], ALU.add, made["mean"], made[id(v_gate), tile])
            a = dve.do(lambda: V.tensor_tensor_reduce(out=s.ap, in0=v, in1=v, scale=1.0, scalar=0.0, op0=ALU.mult,
                                                      op1=ALU.add, accum_out=stats[:, tile:tile + 1]), a, *s.free)
            s.free = (a,)
            made["squares"] = a

        def deviation():
            a = vs(stats[:, 4:8], stats[:, 0:4], 1.0 / W2, ALU.mult, made["squares"], s2=LN_EPS, op1=ALU.add)
            a = activation(stats[:, 4:8], stats[:, 4:8], ACT.Sqrt, a)
            made["deviation"] = dve.do(lambda: V.reciprocal(stats[:, 8:12], stats[:, 4:8]), a)

        def gain(tile):
            v = v_gate[:, tile, :]
            b = stt(v, v, stats[:, 8 + tile:9 + tile], ln_rows[:, 0:W2], ALU.mult, ALU.mult, made["deviation"],
                    ln_rows_in)
            made["v_normed"] = vv(v, v, ln_rows[:, W2:2 * W2], ALU.add, b)

        def mix(g):
            bank = banks.next()
            done = mm(bank.ap[:, 0:256], w_sp[:, g, :], v_gate[:, :, g * DH:(g + 1) * DH], True, True,
                      made["v_normed"], causal, *bank.free, tell=True)
            u = u_gate[:, :, g * DH:(g + 1) * DH]
            made["gated"] = stt(u, bank.ap[:, 0:256].rearrange("p (n f) -> p n f", n=TILES), column("b_spatial", g), u,
                                ALU.add, ALU.mult, done, *(made[id(u_gate), k] for k in range(TILES)))
            bank.free = (made["gated"],)

        gating = [lambda: centre(0), lambda: centre(1), lambda: centre(2), lambda: centre(3), deviation,
                  lambda: gain(0), lambda: gain(1), lambda: gain(2), lambda: gain(3),
                  *((lambda g=g: (mix(g), mix(g + 1))) for g in range(0, 8, 2))]

        attend(len(units2), scores2, maximum2, exponents2, probabilities2, turn_probabilities2, values2,
               between=lambda s: gating[s]() if s < len(gating) else None)
        gated = made["gated"]
        attended2 = (pe.sem, pe.count)
        attended2_d = (dve.sem, dve.count)

        gate_norm = norm_stages(lambda n: u_gate[:, n, :], W2, EPS2, "g_out", xt, 4, lambda n: (gated,),
                                dst_free=(projected,), extra=(attended2,))
        attn_norm = norm_stages(lambda n: o2[:, n, :], W2, EPS2, "g_out", xt, 0, lambda n: (made["o2", n],),
                                dst_free=(projected,), extra=(attended2,))
        in_turn([lambda n, f=f, g=g: (f if n < TILES else g)(n % TILES) for f, g in zip(gate_norm, attn_norm)],
                2 * TILES)
        x_ready = made["normed"]
        y2 = place("y2", 0, [TILES, D])
        turned_all = (pe.sem, pe.count)
        g_pm, g_pm_in = load_row("g_post_mix_row", "g_post_mix", "g_post_mix", 61440, 2, attended2, attended2_d,
                                 turned_all)

        def y_finish(half):
            def finish(tile, bank, done):
                added[tile] = activation(y2[:, tile, half * 512:(half + 1) * 512], bank, ACT.Copy, done)
                return added[tile]
            return finish

        for half in range(2):
            token_major(xt, 2, y_finish(half), by_tile=(half == 1))
        out_done = (pe.sem, pe.count)

        def add_normed(y, gain, gain_in, tile, inv):
            a = stt(y, y, stats[:, 8 + tile:9 + tile], gain[:, :], ALU.mult, ALU.mult, inv, gain_in)
            return vv(resid[:, tile, :], resid[:, tile, :], y, ALU.add, a)

        def add_stages(y, gain, gain_in, srcs_ready):
            square, root = rms_stages(y, D, EPS2, srcs_ready, on_scalar=True)
            var = {}

            def stats_of(tile):
                square(tile)
                var[tile] = made["var"]

            def add(tile):
                added[tile] = add_normed(y(tile), gain, gain_in, tile, root(tile, var[tile]))

            return [stats_of, add]

        y_in = dict(added)

        in_turn(add_stages(lambda n: y2[:, n, :], g_pm, g_pm_in, lambda n: (y_in[n],))
                + norm_stages(lambda n: resid[:, n, :], D, EPS2, "g_pre_ffn", xt, 0, lambda n: (added[n],),
                              dst_free=(out_done,)))
        x_ready = made["normed"]
        ff = (place("ff_high", 0, [FF_PARTS[0], SEQ], F32R), place("ff_low", 24576, [FF_PARTS[0], SEQ], F32R))
        down = place("down", 49152, [TILES, D])
        act_g = Ring([place(f"act_g_{n}", 65536 + n * 2048, [SEQ])[:, :] for n in range(4)])
        normed_done = (*x_ready, (pe.sem, pe.count), (dve.sem, dve.count))
        g_pf, g_pf_in = load_row("g_post_ffn_row", "g_post_ffn", "g_post_ffn", 73728, 3, *normed_done)
        for s in act_g.slots:
            s.free = normed_done
        ff_free = normed_done
        for part, chunks in enumerate(FF_PARTS):
            for pair in range(chunks // 2):
                silu = []
                for kind in range(2):
                    n, w, there = take()
                    for e in range(2):
                        bank = banks.next()
                        for k in range(CHUNKS):
                            done = mm3(bank.ap, tuple(h[:, k * 256 + e * P:k * 256 + (e + 1) * P] for h in w),
                                       tuple(h[:, k, :] for h in xt), k == 0, k == CHUNKS - 1, *there, *x_ready,
                                       *bank.free, tell=(k == CHUNKS - 1))
                        if e == 1:
                            give_back(n, done)
                        if kind == 0:
                            s = act_g.next()
                            a = activation(s.ap, bank.ap, ACT.Silu, done, *s.free)
                            bank.free = (a,)
                            silu.append((s, a))
                        else:
                            s, a = silu[e]
                            m = vv(s.ap, s.ap, bank.ap, ALU.mult, a, done)
                            bank.free = (m,)
                            c = 2 * pair + e
                            s.free = ff_ready = split(ff[0][:, c, :], ff[1][:, c, :], s.ap, m, *ff_free,
                                                      low_on=(dve, V))
            keep_x = x_ready
            x_ready = ff_ready

            def down_finish(half, part=part):
                def finish(tile, bank, done):
                    d = down[:, tile, half * 512:(half + 1) * 512]
                    if part == 0:
                        added[tile] = activation(d, bank, ACT.Copy, done)
                    else:
                        added[tile] = vv(d, d, bank, ALU.add, done, added[tile])
                    return added[tile]
                return finish

            for half in range(2):
                token_major(ff, -(-chunks // 4), down_finish(half), k_last=(chunks - 1) % 4 + 1,
                            by_tile=(part == half == 1))
            ff_free = ((pe.sem, pe.count),)
            x_ready = keep_x

        out_sem = sem("out_stored")
        down_in = dict(added)

        def store(tile):
            sp.start_dma(lambda: S.dma_start(out[tile * P:(tile + 1) * P, :], resid[:, tile, :]), out_sem, 0,
                         added[tile])

        in_turn(add_stages(lambda n: down[:, n, :], g_pf, g_pf_in, lambda n: (down_in[n],)) + [store])
        sp.do(None, (out_sem, 16 * TILES), *all_stored, *(made["spilled", g] for g in range(SPILLED)), tell=False)
        assert taken[0] == len(items), (taken[0], len(items))

        block = ctx.enter_context(nc.Block())

        @block.sync
        def _(e):
            sp.run(e)

        @block.scalar
        def _(e):
            act.run(e)

        @block.vector
        def _(e):
            dve.run(e)

        @block.gpsimd
        def _(e):
            pool.run(e)

        @block.tensor
        def _(e):
            pe.run(e)


WEIGHTS_BEFORE_PEER = 4 + 1 + 1 + 4 + 2 + 12 + 4 + 8


def column_items(w, c0, c1, k=CHUNKS):
    return [w[:, c:c + 256].reshape(k, P, 256).transpose(1, 0, 2).reshape(P, k * 256) for c in range(c0, c1, 256)]


def row_items(w, c0, c1):
    out = []
    for c in range(c0, c1, 512):
        for r in range(0, w.shape[0], 4 * P):
            x = w[r:r + 4 * P, c:c + 512]
            out.append(x.reshape(-1, P, 512).transpose(1, 0, 2).reshape(P, -1))
    return out


def lay_out(i):
    w_in = i["w_in"][0]
    k0, v0 = Q_W, Q_W + KV_W
    p0 = v0 + KV_W
    ga0 = p0 + POOL_W
    gp0 = ga0 + D
    kk = [w_in[:, k0 + g * DH:k0 + (g + 1) * DH] for g in (0, 0, 1, 1)]
    items = column_items(w_in, 0, Q_W)
    items += column_items(np.concatenate(kk, axis=1), 0, 256)
    items.append(w_in[:, v0:v0 + KV_W].reshape(CHUNKS, P, KV_W).transpose(1, 0, 2).reshape(P, -1))
    items += column_items(w_in, p0, ga0)
    items += column_items(i["w_attn_up"][0], 0, D)
    ga, gp, up = column_items(w_in, ga0, gp0), column_items(w_in, gp0, gp0 + D), column_items(i["w_pool_up"][0], 0, D, 4)
    for c in range(4):
        items += [ga[c], gp[c], up[c]]
    items += row_items(i["w_o"][0], 0, D)
    items += column_items(i["w_query"][0], 0, 2048)
    assert len(items) == WEIGHTS_BEFORE_PEER
    items += row_items(i["w_in_2"][0], 0, 5 * W2)
    items += row_items(i["w_out_2"][0], 0, D)
    gate, up = column_items(i["w_gate_2"][0], 0, FF), column_items(i["w_up_2"][0], 0, FF)
    at = 0
    for chunks in FF_PARTS:
        for c in range(at // 2, (at + chunks) // 2):
            items += [gate[c], up[c]]
        items += row_items(i["w_down_2"][0][at * P:(at + chunks) * P], 0, D)
        at += chunks
    weights = np.zeros((len(items), P, ITEM), np.float32)
    for n, x in enumerate(items):
        weights[n, :, :x.shape[1]] = x

    def cols(v):
        return v.reshape(-1, P).T

    b = i["b_in"][0]
    bk = [b[k0 + g * DH:k0 + (g + 1) * DH] for g in (0, 0, 1, 1)]
    columns = [cols(b[:Q_W]), cols(np.concatenate(bk)), cols(b[p0:ga0]), cols(b[ga0:gp0]), cols(b[gp0:]),
               cols(i["ln_mix_g"][0]), cols(i["ln_ffn_g"][0]), cols(i["pool_scale"][0]), cols(i["pre_mix_norm_2"][0]),
               cols(i["attn_out_norm_2"][0]), cols(i["sgu_out_norm_2"][0]), cols(i["pre_ffn_norm_2"][0]),
               i["sgu_b_spatial_2"][0].T]
    rows = [b[v0:p0], i["attn_sinks"][0], i["ln_final_g"], i["post_mix_norm_2"][0], i["sgu_ln_gain_2"][0],
            i["sgu_ln_bias_2"][0], i["post_ffn_norm_2"][0]]
    u = i["u_experts"][0].reshape(KEYS, KEYS // 2, 2, CHUNKS, P)
    return {
        "x": i["x"][0],
        "positions": np.ascontiguousarray(i["positions_2"][0].reshape(TILES, P).T),
        "weights": weights,
        "u_tiles": np.ascontiguousarray(u.transpose(1, 4, 2, 3, 0)).reshape(KEYS // 2, P, ITEM),
        "v_experts": i["v_experts"][0],
        "columns": np.ascontiguousarray(np.concatenate(columns, axis=1)),
        "rows": np.ascontiguousarray(np.concatenate(rows)[None]),
        "tables": shape_tables()[0],
        "dilated_masks": shape_tables()[1],
        "w_pool_grp": np.ascontiguousarray(i["w_pool_grp"][0].transpose(1, 0, 2)),
        "sub_keys": np.ascontiguousarray(i["sub_keys"][0].reshape(2 * PHEADS, KEYS, P).transpose(2, 0, 1)),
        "w_spatial": np.ascontiguousarray(i["sgu_w_spatial_2"][0].transpose(2, 0, 1)),
    }


def shape_tables():
    q, k = np.arange(P)[:, None], np.arange(2 * P)[None, :] - P
    near = (q - k >= 0) & (q - k < P)
    dist = q - (np.arange(SEQ)[None, :] - (SEQ - P))
    times = ((dist >= 0) & (dist <= 128)) * 1.0 + ((dist >= 0) & (dist % 4 == 0)) + ((dist >= 0) & (dist % 16 == 0))
    count = np.minimum(np.arange(1, PAD + 1)[None, :], np.array(WINDOWS)[:, None]).astype(np.float32)
    freq = np.float32(500000.0) ** (-np.arange(0, 16, 2, dtype=np.float32) / np.float32(16))
    every = lambda r: np.broadcast_to(np.asarray(r, np.float32).reshape(1, -1), (P, np.size(r)))
    parts = [np.eye(P), every(np.arange(P)), every(np.arange(TOPK)), np.where(near, 0.0, MASKED), every(1 / count),
             every(freq)]
    masks = [times, np.where(times > 0, 0.0, MASKED)]
    return tuple(np.ascontiguousarray(np.concatenate(x, axis=1).astype(np.float32)) for x in (parts, masks))


def kernel(**inputs):
    import concourse.bacc as bacc
    from concourse.bass_utils import run_bass_kernel_spmd as run

    nc = bacc.Bacc("TRN2", target_bir_lowering=False, num_devices=1)
    arrays, t = {}, {}
    for name, a in lay_out({k: np.asarray(v) for k, v in inputs.items()}).items():
        arrays[f"in_{name}"] = a
        t[name] = nc.dram_tensor(f"in_{name}", a.shape, mybir.dt.from_np(a.dtype), kind="ExternalInput").ap()
    out = nc.dram_tensor("out_x", (SEQ, D), F32, kind="ExternalOutput").ap()
    build(nc, t, out)
    r = run(nc, [arrays], core_ids=[0])
    return r.results[0]["out_x"].reshape(1, SEQ, D)
```

```python
from contextlib import ExitStack

import numpy as np

import concourse.bass as bass
from concourse import mybir

BF16, F32, F32R, I32, U32 = mybir.dt.bfloat16, mybir.dt.float32, mybir.dt.float32r, mybir.dt.int32, mybir.dt.uint32
ALU, ACT, AX = mybir.AluOpType, mybir.ActivationFunctionType, mybir.AxisListType

P = 128
SEQ, D = 512, 1024
TILES = SEQ // P
CHUNKS = D // P
ITEM = 2048
RAW, SPLIT = 3, 3

HEADS, KV_HEADS, DH = 16, 2, 64
Q_W, KV_W, POOL_W = HEADS * DH, KV_HEADS * DH, 512
WINDOWS = (2, 4, 8, 16)
PAD = 16
EPS1 = 1e-5
SCALE = DH ** -0.5
MASKED = -1e30

PHEADS, KEYS, TOPK = 8, 128, 16
LOWEST = -3.0e38
CAND_BANKS = 9
LATE_BANKS = 2
PAIRS = PHEADS * TOPK
J = 4
GROUPS = KEYS // J
GATE_T = 32
GATE_CHUNKS = SEQ // GATE_T
AHEAD = 3
EARLY = 20
SPILLED = EARLY - AHEAD

HEADS2, W2 = 8, 512
EPS2, LN_EPS = 1e-6, 1e-5
ROT_HALF = 8
FF = 2816
FF_CHUNKS = FF // P
FF_PARTS = (12, 10)



def value_order():
    late, spilled = list(range(EARLY, GROUPS)), list(range(SPILLED))
    order = list(range(SPILLED, EARLY))
    while late or spilled:
        if late:
            order.append(late.pop(0))
        if spilled and len(spilled) >= len(late):
            order.append(spilled.pop(0))
    return order


ORDER = value_order()
COLUMNS = [("b_q", 8), ("b_k", 1), ("b_pool", 4), ("b_ga", 8), ("b_gp", 8), ("g_mix", 8), ("g_ffn", 8),
           ("pool_scale", 4), ("g_pre_mix", 8), ("g_out", 8), ("g_pre_ffn", 8), ("b_spatial", 8)]
TABLES = [("ident", 128), ("iota", 128), ("iota_k", 16), ("window_mask", 256), ("inv_count", 64), ("inv_freq", 8)]
ROWS = [("b_v", 128), ("sinks", 16), ("g_final", 1024), ("g_post_mix", 1024), ("ln_gain", 512), ("ln_bias", 512),
        ("g_post_ffn", 1024)]


def spans(table):
    at, out = 0, {}
    for name, width in table:
        out[name] = slice(at, at + width)
        at += width
    return out, at


class Engine:

    def __init__(self, sem):
        self.sem, self.count, self.waited, self.steps = sem, 0, {}, []

    def do(self, build, *after, tell=True):
        waits = []
        for sem, value in after:
            if self.waited.get(id(sem), 0) < value:
                self.waited[id(sem)] = value
                waits.append((sem, value))
        self.steps.append((waits, build, tell))
        if tell:
            self.count += 1
            return (self.sem, self.count)

    def start_dma(self, build, sem, total, *after):
        self.do(lambda: build().then_inc(sem, 16), *after, tell=False)
        return (sem, total)

    def run(self, eng):
        for waits, build, tell in self.steps:
            for sem, value in waits:
                eng.wait_ge(sem, value)
            ins = build() if build else None
            if tell:
                ins.then_inc(self.sem, 1)


class Slot:

    def __init__(self, ap):
        self.ap, self.free = ap, ()


class Ring:
    def __init__(self, aps):
        self.slots, self.n = [Slot(a) for a in aps], 0

    def part(self, first, last):
        ring = Ring([])
        ring.slots = self.slots[first:last]
        return ring

    def next(self):
        self.n += 1
        return self.slots[(self.n - 1) % len(self.slots)]


def build(nc, t, out):
    col, n_col = spans(COLUMNS)
    tab, n_tab = spans(TABLES)
    row, n_row = spans(ROWS)

    with ExitStack() as ctx:
        def sem(name):
            return ctx.enter_context(nc.semaphore(name))

        base = -(-nc.sbuf_base // 32) * 32
        top = [base]

        def fixed(name, shape, dt=F32):
            size = int(np.prod(shape)) * 4
            tensor = nc.alloc_sbuf_tensor_at(name, [P] + shape, dt, offset=top[0])
            top[0] += -(-size // 32) * 32
            return tensor

        columns = fixed("columns", [n_col])
        tables = fixed("tables", [n_tab])
        v_sink_rows = fixed("v_sink_rows", [144])
        neg_sinks = fixed("neg_sinks", [HEADS])
        stats = fixed("stats", [16])
        resid = fixed("resid", [TILES, D])
        xt_low_at = top[0]
        xt_low, xt_high = fixed("xt_low", [CHUNKS, SEQ], F32R), fixed("xt_high", [CHUNKS, SEQ], F32R)
        xt = (xt_high, xt_low)
        xt_gained = nc.alloc_sbuf_tensor_at("xt_gained", [P, CHUNKS, SEQ], F32, offset=xt_low_at)
        raw_items = [fixed(f"raw_{n}", [ITEM]) for n in range(RAW)]
        split_items = [(fixed(f"high_{n}", [ITEM], F32R), fixed(f"low_{n}", [ITEM], F32R)) for n in range(SPLIT)]
        area = top[0]
        area_size = nc.sbuf_usable_end - area

        def place(name, at, shape, dt=F32):
            assert at % 32 == 0 and at + int(np.prod(shape)) * 4 <= area_size, (name, area_size)
            return nc.alloc_sbuf_tensor_at(name, [P] + shape, dt, offset=area + at)

        def column(name, c=None):
            s = col[name]
            return columns[:, s] if c is None else columns[:, s.start + c:s.start + c + 1]

        def table(name):
            return tables[:, tab[name]]

        ident = table("ident")
        banks = Ring([ctx.enter_context(nc.psum_tensor(f"bank_{n}", [P, 512], F32))[:, :] for n in range(8)])

        attn_banks, fill_banks = banks.part(0, 6), banks.part(6, 8)

        pe, act, dve, pool, sp = (Engine(sem(n)) for n in ("pe_done", "act_done", "dve_done", "pool_done", "sp_done"))
        V, A, T, G, S = nc.vector, nc.scalar, nc.tensor, nc.gpsimd, nc.sync

        def mm(o, l, r, start, stop, *after, tell=False):
            return pe.do(lambda: T.matmul(o, l, r, start=start, stop=stop), *after, tell=tell)

        def mm3(o, l, r, start, stop, *after, tell=False):
            mm(o, l[0], r[0], start, False, *after)
            mm(o, l[0], r[1], False, False)
            return mm(o, l[1], r[0], False, stop, tell=tell)

        def turn(o, i, *after, tell=False):
            return pe.do(lambda: T.transpose(o, i, ident), *after, tell=tell)

        def activation(o, i, f, *after, **kw):
            return act.do(lambda: A.activation(o, i, f, **kw), *after)

        def tt_op(eng, builder, o, a, b, op, *after):
            return eng.do(lambda: builder.tensor_tensor(o, a, b, op), *after)

        def vv(o, a, b, op, *after):
            return tt_op(dve, V, o, a, b, op, *after)

        def vs(o, a, s1, op0, *after, s2=None, op1=ALU.bypass):
            return dve.do(lambda: V.tensor_scalar(o, a, s1, s2, op0, op1), *after)

        def stt(o, a, s, b, op0, op1, *after):
            return dve.do(lambda: V.scalar_tensor_tensor(out=o, in0=a, scalar=s, in1=b, op0=op0, op1=op1), *after)

        def split(high, low, x, *after, low_on=None):
            h = activation(high, x, ACT.Copy, *after)
            eng, builder = low_on or (pool, G)
            return h, tt_op(eng, builder, low, x, high.bitcast(F32), ALU.subtract, h, *after)

        small_sem, x_sem = sem("small_loaded"), [sem(f"x_loaded_{n}") for n in range(TILES)]
        for n in range(TILES):
            src = t["x"][n * P:(n + 1) * P, :]
            sp.start_dma(lambda n=n, src=src: S.dma_start(resid[:, n, :], src), x_sem[n], 16)
        smalls = [(columns[:, :], t["columns"]), (tables[:, :], t["tables"]),
                  (v_sink_rows[:, :], t["rows"][0:1, 0:144].to_broadcast([P, 144]))]
        for dst, src in smalls:
            act.start_dma(lambda dst=dst, src=src: A.dma_start(dst, src), small_sem, 0)
        small = (small_sem, 16 * len(smalls))
        x_in = [(x_sem[n], 16) for n in range(TILES)]
        b_v_row, sink_row = v_sink_rows[:, 0:128], v_sink_rows[:, 128:144]

        items = []
        raw_sem = [sem(f"raw_loaded_{n}") for n in range(RAW)]
        raw_free = [()] * RAW
        split_free = [()] * SPLIT
        ready = {}
        taken = [0]

        def load_item(n):
            if n >= len(items):
                return
            r = n % RAW
            width = items[n].shape[-1]
            sp.start_dma(lambda: S.dma_start(raw_items[r][:, 0:width], items[n]), raw_sem[r], 0, *raw_free[r])

        dve_busy = [False]

        def low_halves(w):
            if dve_busy[0]:
                return [(slice(0, w), (pool, G))]
            return [(slice(0, w // 2), (pool, G)), (slice(w // 2, w), (dve, V))]

        def split_item(n):
            if n >= len(items):
                return
            r, s = n % RAW, n % SPLIT
            w = items[n].shape[-1]
            there = (raw_sem[r], 16 * (n // RAW + 1))
            ready[n] = ()
            for part, low_on in low_halves(w):
                ready[n] += split(split_items[s][0][:, part], split_items[s][1][:, part], raw_items[r][:, part],
                                  there, *split_free[s], low_on=low_on)
            raw_free[r] = ready[n]

        def take():
            n = taken[0]
            taken[0] += 1
            s = split_items[n % SPLIT]
            return n, (s[0], s[1]), ready[n]

        def give_back(n, done):
            split_free[n % SPLIT] = (done,)
            split_item(n + SPLIT)
            load_item(n + SPLIT + RAW)

        def first_split(n):
            split_item(n)
            load_item(n + RAW)

        w_all = t["weights"]
        n_w = w_all.shape[0]
        peer_at = WEIGHTS_BEFORE_PEER
        for n in range(peer_at):
            items.append(w_all[n])

        def u_items(g):
            return [t["u_tiles"][m] for m in (2 * g, 2 * g + 1)]

        v_view = t["v_experts"].rearrange("(i m e) d -> m i (e d)", i=KEYS, e=2)

        def v_items(g):
            return [v_view[m] for m in (2 * g, 2 * g + 1)]

        for g in range(EARLY):
            items += u_items(g)
        for at, g in enumerate(ORDER):
            items += v_items(g)
            if at + AHEAD < GROUPS and ORDER[at + AHEAD] >= EARLY:
                items += u_items(ORDER[at + AHEAD])
        for n in range(peer_at, n_w):
            items.append(w_all[n])
        for n in range(RAW):
            load_item(n)

        def feature_major(*args):
            for _ in feature_steps(*args, banks):
                pass

        def feature_steps(x, chunks, finish, ring):
            for pair in range(chunks // 2):
                n, w, there = take()
                k = x_chunks(x)
                for e in range(2):
                    bank = ring.next()
                    for c in range(k):
                        done = mm3(bank.ap, tuple(h[:, c * 256 + e * P:c * 256 + (e + 1) * P] for h in w),
                                   tuple(h[:, c, :] for h in x), c == 0, c == k - 1,
                                   *there, *bank.free, *(x_ready if c == 0 else ()), tell=(c == k - 1))
                        if c < k - 1:
                            yield
                    if e == 1:
                        give_back(n, done)
                    bank.free = (finish(2 * pair + e, bank.ap, done),)
                    yield

        def x_chunks(x):
            return x[0].shape[1]

        def token_major(x, k_items, finish, k_last=4, by_tile=False, ready=None, steps=None):
            ready = ready or (lambda chunk, tile: x_ready)
            chunks = [4] * (k_items - 1) + [k_last]

            def products(bank, kk, tile, w, there):
                for c in range(chunks[kk]):
                    first, last = kk == 0 and c == 0, kk == k_items - 1 and c == chunks[kk] - 1
                    done = mm3(bank.ap, tuple(h[:, 4 * kk + c, tile * P:(tile + 1) * P] for h in x),
                               tuple(h[:, c * 512:(c + 1) * 512] for h in w), first, last,
                               *there, *ready(4 * kk + c, tile), *(bank.free if first else ()),
                               tell=(c == chunks[kk] - 1))
                return done

            if by_tile:
                held = [take() for _ in range(k_items)]
                last_read = {}
                for tile in range(TILES):
                    bank = banks.next()
                    for kk, (n, w, there) in enumerate(held):
                        last_read[n] = done = products(bank, kk, tile, w, there)
                    bank.free = (finish(tile, bank.ap, done),)
                    if steps:
                        next(steps)
                        next(steps)
                for _ in steps or ():
                    pass
                for n, done in last_read.items():
                    give_back(n, done)
                return
            out_banks = [banks.next() for _ in range(TILES)]
            for kk in range(k_items):
                n, w, there = take()
                dones = [products(out_banks[tile], kk, tile, w, there) for tile in range(TILES)]
                give_back(n, dones[-1])
            for tile, bank in enumerate(out_banks):
                bank.free = (finish(tile, bank.ap, dones[tile]),)

        def norm_buffers(name, at):
            return (Ring([place(f"{name}_normed_{n}", at + n * 4096, [D])[:, :] for n in range(2)]),
                    Ring([place(f"{name}_squared_{n}", at + 8192 + n * 2048, [D // 2]).bitcast(BF16)[:, :]
                          for n in range(2)]))

        NORM_AT = area_size // 32 * 32 - 12288
        usual_buffers = norm_buffers("tile", NORM_AT)
        normed, squared = usual_buffers

        def tile_steps(stages, count=TILES, apart=2):
            for step in range(apart * (count - 1) + len(stages)):
                for k in reversed(range(len(stages))):
                    tile, off = divmod(step - k, apart)
                    if off == 0 and 0 <= tile < count:
                        stages[k](tile)
                yield

        def in_turn(stages, count=TILES):
            for _ in tile_steps(stages, count, 1):
                pass

        def rms_stages(src, width, eps, srcs_ready, extra=(), on_scalar=False):
            def square(tile):
                s = squared.next()
                if on_scalar:
                    a = activation(s.ap[:, 0:width], src(tile), ACT.Square, *srcs_ready(tile), *s.free, *extra,
                                   accum_out=stats[:, tile:tile + 1])
                else:
                    a = dve.do(lambda: V.tensor_tensor_reduce(
                        out=s.ap[:, 0:width], in0=src(tile), in1=src(tile), scale=1.0, scalar=0.0, op0=ALU.mult,
                        op1=ALU.add, accum_out=stats[:, tile:tile + 1]), *srcs_ready(tile), *s.free, *extra)
                s.free = (a,)
                made["var"] = vs(stats[:, 4 + tile:5 + tile], stats[:, tile:tile + 1], 1.0 / width, ALU.mult, a,
                                 s2=eps, op1=ALU.add)

            def root(tile, var):
                b = activation(stats[:, 4 + tile:5 + tile], stats[:, 4 + tile:5 + tile], ACT.Sqrt, var)
                return dve.do(lambda: V.reciprocal(stats[:, 8 + tile:9 + tile], stats[:, 4 + tile:5 + tile]), b)

            return square, root

        def norm_stages(src, width, eps, gain, chunk0, srcs_ready, dst_free=(), extra=()):
            square, root = rms_stages(src, width, eps, srcs_ready, extra)
            var, on_way, gained = {}, {}, {}

            def stats_of(tile):
                square(tile)
                var[tile] = made["var"]

            def scale(tile):
                inv = root(tile, var[tile])
                s = normed.next()
                on_way[tile] = s, activation(s.ap[:, 0:width], src(tile), ACT.Copy, inv, *s.free,
                                             scale=stats[:, 8 + tile:9 + tile])

            def turned(tile):
                s, n = on_way[tile]
                gained[tile] = []
                for half in range(width // 512):
                    bank = banks.next()
                    for c in range(4):
                        f = (half * 4 + c) * P
                        done = turn(bank.ap[:, c * P:(c + 1) * P], s.ap[:, f:f + P], n, *bank.free, small,
                                    tell=(c == 3))
                    c0 = col[gain].start + chunk0 + half * 4
                    where = (slice(None), slice(chunk0 + half * 4, chunk0 + half * 4 + 4),
                             slice(tile * P, (tile + 1) * P))
                    scaled = vv(xt_gained[where], bank.ap.rearrange("p (c t) -> p c t", c=4),
                                columns[:, c0:c0 + 4].unsqueeze(2).to_broadcast([P, 4, P]), ALU.mult, done, *dst_free)
                    bank.free = (scaled,)
                    gained[tile].append((where, scaled))
                s.free = (done,)

            def halves(tile):
                for where, scaled in gained[tile]:
                    made["normed"] = made["normed", tile] = split(xt_high[where], xt_low[where],
                                                                  xt_gained[where], scaled)

            return [stats_of, scale, turned, halves]

        made = {}

        steps = tile_steps(norm_stages(lambda n: resid[:, n, :], D, EPS1, "g_mix", 0, lambda n: (x_in[n],)), apart=1)
        for step, _ in enumerate(steps):
            if step == 4:
                first_split(0)
        first_split(1)
        first_split(2)
        x_ready = made["normed"]
        ns = vs(neg_sinks[:, :], sink_row, -1.0, ALU.mult, small)

        qt = place("qt", 0, [CHUNKS, SEQ])
        ot = (place("ot_high", 16384, [CHUNKS, SEQ], F32R), place("ot_low", 32768, [CHUNKS, SEQ], F32R))
        kt = place("kt", 49152, [SEQ])
        v_tok = place("v_tok", 53248, [TILES, KV_W])
        score = Ring([place(f"score_{n}", 55296 + n * 4096, [4, 256])[:, :, :] for n in range(3)])
        prob_t = Ring([place(f"prob_t_{n}", 67584 + n * 4096, [2, 512])[:, :, :] for n in range(2)])
        head_stat = Ring([place(f"head_stat_{n}", 75776 + n * 128, [5, 4])[:, :, :] for n in range(4)])
        padded = [place(f"padded_{n}", 76288 + n * 2112, [PAD + SEQ]) for n in range(4)]

        def q_finish(c, bank, done):
            made["q", c] = activation(qt[:, c, :], bank, ACT.Identity, done, bias=column("b_q", c))
            return made["q", c]

        feature_major(xt, 8, q_finish)
        n, w, there = take()
        bank = banks.next()
        for c in range(CHUNKS):
            done = mm3(bank.ap, tuple(h[:, c * P:(c + 1) * P] for h in w), tuple(h[:, c, :] for h in xt), c == 0,
                       c == CHUNKS - 1, *there, *bank.free, tell=(c == CHUNKS - 1))
        k_made = activation(kt[:, :], bank.ap, ACT.Identity, done, bias=column("b_k"))
        bank.free = (k_made,)
        bank = banks.next()
        for tile in range(TILES):
            for c in range(CHUNKS):
                done = mm3(bank.ap[:, tile * P:(tile + 1) * P], tuple(h[:, c, tile * P:(tile + 1) * P] for h in xt),
                           tuple(h[:, (8 + c) * P:(9 + c) * P] for h in w), c == 0, c == CHUNKS - 1, *bank.free,
                           tell=(c == CHUNKS - 1))
        give_back(n, done)
        v_made = vv(v_tok[:, :, :], bank.ap.rearrange("p (n f) -> p n f", n=TILES),
                    b_v_row.unsqueeze(1).to_broadcast([P, TILES, KV_W]), ALU.add, done)
        bank.free = (v_made,)

        units = [(blk, g, four) for blk in range(TILES) for g in range(KV_HEADS) for four in range(2)]
        state = {}

        def scores(u):
            blk, g, four = units[u]
            rows = slice(g * DH, (g + 1) * DH)
            keys = slice(max(blk - 1, 0) * P, (blk + 1) * P)
            n = keys.stop - keys.start
            pair_banks = []
            for b in range(2):
                bank = attn_banks.next()
                for e in range(2):
                    c = 4 * four + 2 * b + e
                    done = mm(bank.ap[:, e * 256:e * 256 + n], qt[rows, c, blk * P:(blk + 1) * P], kt[rows, keys],
                              True, True, *bank.free, made["q", c], k_made, tell=(e == 1))
                pair_banks.append((bank, done))
            state[u] = dict(s=score.next(), st=head_stat.next(), n=n, banks=pair_banks)

        def maximum(u):
            x = state[u]
            blk, g, four = units[u]
            s, st, n = x["s"], x["st"], x["n"]
            mask = table("window_mask")[:, 256 - n:256].unsqueeze(1).to_broadcast([P, 2, n])
            for b, (bank, done) in enumerate(x["banks"]):
                masked = stt(s.ap[:, 2 * b:2 * b + 2, 0:n],
                             bank.ap.rearrange("p (h k) -> p h k", h=2)[:, :, 0:n], SCALE, mask,
                             ALU.mult, ALU.add, done, *s.free)
                bank.free = (masked,)
            neg_max, sink_e = st.ap[:, 0, :], st.ap[:, 2, :]
            m = dve.do(lambda: V.tensor_reduce(neg_max, s.ap[:, :, 0:n], AX.X, ALU.max, negate=True), masked, *st.free)
            own = slice(8 * g + 4 * four, 8 * g + 4 * four + 4)
            x["m"] = vv(neg_max, neg_max, neg_sinks[:, own], ALU.min, m, ns)
            x["d"] = vv(sink_e, neg_max, sink_row[:, own], ALU.add, x["m"])

        def exponents(u):
            x = state[u]
            s, st, n = x["s"], x["st"], x["n"]
            neg_max, total, sink_e = (st.ap[:, k, :] for k in range(3))
            for h in range(4):
                activation(s.ap[:, h, 0:n], s.ap[:, h, 0:n], ACT.Exp, x["m"], bias=neg_max[:, h:h + 1],
                           accum_out=total[:, h:h + 1])
            x["e"] = activation(sink_e, sink_e, ACT.Exp, x["d"])

        def probabilities(u):
            x = state[u]
            s, st, n = x["s"], x["st"], x["n"]
            total, sink_e, inv = (st.ap[:, k, :] for k in (1, 2, 3))
            a = vv(total, total, sink_e, ALU.add, x["e"])
            a = dve.do(lambda: V.reciprocal(inv, total), a)
            for h in range(4):
                p = vs(s.ap[:, h, 0:n], s.ap[:, h, 0:n], inv[:, h:h + 1], ALU.mult, a)
            st.free = (p,)
            x["p"] = p

        def turn_probabilities(u):
            x = state[u]
            s, n = x["s"], x["n"]
            pt = x["pt"] = prob_t.next()
            for kb in range(n // P):
                bank = attn_banks.next()
                for h in range(4):
                    done = turn(bank.ap[:, h * P:(h + 1) * P], s.ap[:, h, kb * P:(kb + 1) * P], x["p"], *bank.free,
                                tell=(h == 3))
                x["c"] = activation(pt.ap[:, kb, :], bank.ap, ACT.Copy, done, *pt.free)
                bank.free = (x["c"],)
            s.free = (done,)

        def values(u):
            x = state.pop(u)
            blk, g, four = units[u]
            rows = slice(g * DH, (g + 1) * DH)
            nb = x["n"] // P
            bank = attn_banks.next()
            for kb in range(nb):
                done = mm(bank.ap[rows, :], v_tok[:, blk - nb + 1 + kb, g * DH:(g + 1) * DH], x["pt"].ap[:, kb, :],
                          kb == 0, kb == nb - 1, x["c"], v_made, *bank.free, tell=(kb == nb - 1))
            x["pt"].free = (done,)
            where = (rows, slice(4 * four, 4 * four + 4), slice(blk * P, (blk + 1) * P))
            bank.free = split(ot[0][where], ot[1][where], bank.ap[rows, :].rearrange("p (c t) -> p c t", c=4), done,
                              low_on=(dve, V))
            return bank.free

        def attend(count, scores, maximum, exponents, probabilities, turn_probabilities, values, fill, fills,
                   between=None):
            parts, filled = 3 * (count + 3), 0

            def some_fill(part):
                nonlocal filled
                while filled < part * fills // parts:
                    next(fill)
                    filled += 1

            for s in range(count + 3):
                if s < count:
                    scores(s)
                some_fill(3 * s + 1)
                if 0 <= s - 1 < count:
                    exponents(s - 1)
                if 0 <= s - 2 < count:
                    probabilities(s - 2)
                    turn_probabilities(s - 2)
                some_fill(3 * s + 2)
                if s < count:
                    maximum(s)
                if s >= 3:
                    last = values(s - 3)
                some_fill(3 * s + 3)
                if between:
                    between(s)
            return last

        zeroed = [dve.do(lambda p=p: V.memset(p[:, 0:PAD], 0.0), *x_ready) for p in padded]

        def padded_finish(g, bank, done):
            made["padded", g] = activation(padded[g][:, PAD:], bank, ACT.Identity, done, *x_ready,
                                           bias=column("b_pool", g))
            return made["padded", g]

        o_ready = attend(len(units), scores, maximum, exponents, probabilities, turn_probabilities, values,
                         feature_steps(xt, 4, padded_finish, fill_banks), 4 * CHUNKS)
        attended = (pe.sem, pe.count)

        POOL_AT = 49152
        sums = [place(f"sums_{n}", POOL_AT + n * 2112, [PAD + SEQ]) for n in range(2)]
        w_group = place("w_group", POOL_AT + 4224, [4, P])
        ypt = (place("ypt_high", POOL_AT + 6272, [4, SEQ], F32R), place("ypt_low", POOL_AT + 14464, [4, SEQ], F32R))
        y_groups = Ring([place(f"y_group_{n}", POOL_AT + 22656 + n * 2048, [SEQ])[:, :] for n in range(2)])
        group_sem = sem("group_matrices_loaded")
        w_group_in = act.start_dma(lambda: A.dma_start(w_group[:, :, :], t["w_pool_grp"]), group_sem, 16, attended,
                                   *o_ready)
        for g in range(4):
            p, reach, last = padded[g], 1, made["padded", g]
            src = p
            for k in range(g + 1):
                dst = sums[k % 2]
                lo = 2 * reach - 1
                last = vv(dst[:, lo:], src[:, lo:], src[:, lo - reach:PAD + SEQ - reach], ALU.add, last, *zeroed,
                          attended, (dve.sem, dve.count))
                src, reach = dst, 2 * reach
            inv = table("inv_count").rearrange("p (g k) -> p g k", g=4)[:, g, :]
            b = vv(src[:, PAD:2 * PAD], src[:, PAD:2 * PAD], inv, ALU.mult, last, small)
            stt(p[:, 2 * PAD:], src[:, 2 * PAD:], 1.0 / WINDOWS[g], p[:, 2 * PAD:], ALU.mult, ALU.subtract, last)
            made["pooled"] = vv(p[:, PAD:2 * PAD], src[:, PAD:2 * PAD], p[:, PAD:2 * PAD], ALU.subtract, b)

        ya = place("ya", 0, [CHUNKS, SEQ])
        x_ready_norm, x_ready = x_ready, o_ready

        def ya_finish(c, bank, done):
            made["ya", c] = activation(ya[:, c, :], bank, ACT.Copy, done, attended)
            return made["ya", c]

        feature_major(ot, 8, ya_finish)
        ot_read = (pe.sem, pe.count)
        x_ready = x_ready_norm
        for g in range(4):
            bank = banks.next()
            done = mm(bank.ap, w_group[:, g, :], padded[g][:, PAD:], True, True, made["pooled"], w_group_in, *bank.free,
                      tell=True)
            y = y_groups.next()
            a = vs(y.ap, bank.ap, column("pool_scale", g), ALU.mult, done, *y.free)
            bank.free = (a,)
            y.free = split(ypt[0][:, g, :], ypt[1][:, g, :], y.ap, a, low_on=(dve, V))
        y_ready = y.free

        merged = (place("merged_high", 16384, [CHUNKS, SEQ], F32R), place("merged_low", 32768, [CHUNKS, SEQ], F32R))
        gate = Ring([place(f"gate_{n}", 76288 + n * 2048, [SEQ])[:, :] for n in range(4)])
        for s in gate.slots:
            s.free = (*y_ready, done)

        for pair in range(4):
            a_items = take()
            halves = {}
            for kind, bias in (("a", "b_ga"), ("p", "b_gp")):
                n, w, there = a_items if kind == "a" else take()
                for e in range(2):
                    c = 2 * pair + e
                    bank = banks.next()
                    for k in range(CHUNKS):
                        done = mm3(bank.ap, tuple(h[:, k * 256 + e * P:k * 256 + (e + 1) * P] for h in w),
                                   tuple(h[:, k, :] for h in xt), k == 0, k == CHUNKS - 1, *there, *bank.free,
                                   tell=(k == CHUNKS - 1))
                    gt = gate.next()
                    s = activation(gt.ap, bank.ap, ACT.Sigmoid, done, *gt.free, bias=column(bias, c))
                    bank.free = (s,)
                    halves[kind, e] = (gt, s)
                give_back(n, done)
            n, w, there = take()
            for e in range(2):
                c = 2 * pair + e
                bank = banks.next()
                for k in range(4):
                    done = mm3(bank.ap, tuple(h[:, k * 256 + e * P:k * 256 + (e + 1) * P] for h in w),
                               tuple(h[:, k, :] for h in ypt), k == 0, k == 3, *there, *y_ready, *bank.free,
                               tell=(k == 3))
                (ga, sa), (gp, sg) = halves["a", e], halves["p", e]
                m1 = vv(ga.ap, ga.ap, ya[:, c, :], ALU.mult, sa, made["ya", c])
                m2 = vv(gp.ap, gp.ap, bank.ap, ALU.mult, sg, done)
                bank.free = (m2,)
                m3 = vv(ga.ap, ga.ap, gp.ap, ALU.add, m1, m2)
                gp.free = (m3,)
                ga.free = made["merged", c] = split(merged[0][:, c, :], merged[1][:, c, :], ga.ap, m3, ot_read, *y_ready)
            give_back(n, done)
        added = {}

        def residual_add(half):
            def finish(tile, bank, done):
                r = resid[:, tile, half * 512:(half + 1) * 512]
                added[tile] = vv(r, r, bank, ALU.add, done)
                return added[tile]
            return finish

        ffn_norm = tile_steps(norm_stages(lambda n: resid[:, n, :], D, EPS1, "g_ffn", 0, lambda n: (added[n],),
                                     extra=(*y_ready, *made["merged", CHUNKS - 1])))
        for half in range(2):
            token_major(merged, 2, residual_add(half), by_tile=(half == 1), steps=ffn_norm if half == 1 else None,
                        ready=lambda chunk, tile: made["merged", chunk])
        mixed_in = (pe.sem, pe.count)

        x_ready = made["normed"]

        hidden = Ring([place(f"hidden_{n}", n * 8192, [J, SEQ])[:, :, :] for n in range(AHEAD)])
        sub_keys = place("sub_keys", 24576, [2 * PHEADS, KEYS])
        query = Ring([place(f"query_{n}", 32768 + n * 2048, [SEQ])[:, :] for n in range(2)])
        key_score = Ring([place(f"key_score_{n}", 36864 + n * 2048, [TILES, KEYS])[:, :, :] for n in range(2)])
        top_v = place("top_v", 40960, [TILES, 2 * PHEADS, TOPK])
        top_i = place("top_i", 45056, [TILES, 2 * PHEADS, TOPK], U32)
        top_f = place("top_f", 49152, [TILES, 2 * PHEADS, TOPK])
        cand = place("cand", 53248, [PHEADS, TOPK * TOPK])
        same = place("same", 32768, [PAIRS, TOPK])
        names = ["best", "pos", "pos_a", "pos_b", "a_f", "b_f", "first", "second", "gate_w", "shifted"]
        small_at = {n: place(n, 61440 + 512 * k, [PHEADS, TOPK], U32 if n in ("pos", "pos_a", "pos_b") else F32)
                    for k, n in enumerate(names)}
        gate_sum = place("gate_sum", 61440 + 512 * len(names), [2, PHEADS])
        pair_t = place("pair_t", 79424, [3, SEQ])

        keys_sem = sem("sub_keys_loaded")
        keys_in = act.start_dma(lambda: A.dma_start(sub_keys[:, :, :], t["sub_keys"]), keys_sem, 16, mixed_in, *ga.free)

        dve_busy[0] = True
        def query_finish(c, bank, done):
            q = query.next()
            a = activation(q.ap, bank, ACT.Copy, done, *q.free)
            made["query"] = (q, a)
            return a

        def best_keys(c):
            q, a = made["query"]
            bank = banks.next()
            for tile in range(TILES):
                done = mm(bank.ap[:, tile * P:(tile + 1) * P], q.ap[:, tile * P:(tile + 1) * P], sub_keys[:, c, :],
                          True, True, a, keys_in, *bank.free, tell=(tile == TILES - 1))
            q.free = (done,)
            s = key_score.next()
            b = activation(s.ap, bank.ap.rearrange("p (n k) -> p n k", n=TILES), ACT.Copy, done, *s.free)
            bank.free = (b,)
            last = b
            for tile in range(TILES):
                v, i, x = top_v[:, tile, c, :], top_i[:, tile, c, :], s.ap[:, tile, :]
                last = top16(v, i, x, last)
            s.free = (last,)
            return last

        def top16(v, i, x, *after):
            a = dve.do(lambda: V.max(v[:, 0:8], x), *after)
            dve.do(lambda: V.max_index(i[:, 0:8], v[:, 0:8], x), a)
            b = dve.do(lambda: V.match_replace(x, v[:, 0:8], x, LOWEST), (dve.sem, dve.count))
            c = dve.do(lambda: V.max(v[:, 8:16], x), b)
            return dve.do(lambda: V.max_index(i[:, 8:16], v[:, 8:16], x), c)

        def chunk_of(n, w, there, e):
            bank = banks.next()
            for k in range(CHUNKS):
                done = mm3(bank.ap, tuple(h[:, k * 256 + e * P:k * 256 + (e + 1) * P] for h in w),
                           tuple(h[:, k, :] for h in xt), k == 0, k == CHUNKS - 1, *there, *x_ready, *bank.free,
                           tell=(k == CHUNKS - 1))
            if e == 1:
                give_back(n, done)
            return bank, done

        for c in range(2 * PHEADS):
            if c % 2 == 0:
                item = take()
            bank, done = chunk_of(*item, c % 2)
            if c:
                best_keys(c - 1)
            bank.free = (query_finish(c, bank.ap, done),)
        keys_done = best_keys(2 * PHEADS - 1)

        spill = nc.dram_tensor("spilled_hidden", [SPILLED, P, J * SEQ], F32, kind="Internal").ap()
        spill_sem = [sem(f"hidden_stored_{n}") for n in range(AHEAD)]
        reload_sem = [sem(f"hidden_loaded_{n}") for n in range(AHEAD)]
        spills, reloads = [0] * AHEAD, [0] * AHEAD
        held = {}

        def hidden_steps(g, j, ring):
            if j == 0:
                held["slot"] = hidden.next()
            if j % 2 == 0:
                held["item"] = take()
            slot, (n, w, there) = held["slot"], held["item"]
            bank = ring.next()
            for k in range(CHUNKS):
                at = (j % 2 * CHUNKS + k) * P
                done = mm3(bank.ap, tuple(h[:, at:at + P] for h in w), tuple(h[:, k, :] for h in xt),
                           k == 0, k == CHUNKS - 1, *there, *bank.free, tell=(k == CHUNKS - 1))
                if k < CHUNKS - 1:
                    yield
            if j % 2 == 1:
                give_back(n, done)
            a = activation(slot.ap[:, j, :], bank.ap, ACT.Gelu, done, *slot.free, *x_ready)
            bank.free = (a,)
            made["hidden", g] = (slot, (a,))
            if j == J - 1 and g < SPILLED:
                k = g % AHEAD
                spills[k] += 16
                src = slot.ap.rearrange("p j t -> p (j t)")
                st = act.start_dma(lambda: A.dma_start(spill[g], src), spill_sem[k], spills[k], a)
                slot.free = (st,)
                made["spilled", g] = st

        def expert_hidden(g, j):
            for _ in hidden_steps(g, j, banks):
                pass

        def reload_hidden(g):
            slot = hidden.next()
            k = (hidden.n - 1) % AHEAD
            reloads[k] += 16
            dst = slot.ap.rearrange("p j t -> p (j t)")
            there = act.start_dma(lambda: A.dma_start(dst, spill[g]), reload_sem[k], reloads[k], *slot.free,
                                  made["spilled", g])
            made["hidden", g] = (slot, (there,))

        early = [(g, j) for g in range(EARLY) for j in range(J)]

        as_float = dve.do(lambda: V.tensor_copy(top_f[:, :, :, :], top_i[:, :, :, :]), keys_done)
        free_small = ()

        def turn_choices(tile):
            for _ in range(LATE_BANKS):
                expert_hidden(*early.pop(0))
            bank = banks.next()
            for k, src in enumerate(("first", "second", "gate_w")):
                done = turn(bank.ap[:, k * P:(k + 1) * P], small_at[src][:, :, :].rearrange("p h k -> p (h k)"),
                            *chosen_of_tile, *bank.free, tell=(k == 2))
            turned = activation(pair_t[:, :, tile * P:(tile + 1) * P],
                                bank.ap[:, 0:3 * P].rearrange("p (k t) -> p k t", k=3), ACT.Copy, done)
            bank.free = (turned,)
            return (done,), turned

        for tile in range(TILES):
            if tile > 0:
                free_small, _ = turn_choices(tile - 1)

            def half(x, which):
                return x[:, tile, :, :].rearrange("p (h two) k -> p two h k", two=2)[:, which, :, :]
            a = vv(cand[:, :, :].rearrange("p h (a b) -> p h a b", a=TOPK),
                   half(top_v, 0).unsqueeze(3).to_broadcast([P, PHEADS, TOPK, TOPK]),
                   half(top_v, 1).unsqueeze(2).to_broadcast([P, PHEADS, TOPK, TOPK]), ALU.add, keys_done,
                   (dve.sem, dve.count))
            best, pos, pos_a, pos_b, a_f, b_f, first, second, gate_w, shifted = (small_at[n][:, :, :] for n in names)
            last = a
            for h in range(PHEADS):
                last = top16(best[:, h, :], pos[:, h, :], cand[:, h, :], last)
            ua = dve.do(lambda: V.tensor_scalar(pos_a, pos, 4, None, ALU.logical_shift_right), last)
            ub = dve.do(lambda: V.tensor_scalar(pos_b, pos, 15, None, ALU.bitwise_and), last)
            fa = dve.do(lambda: V.tensor_copy(a_f, pos_a), ua)
            fb = dve.do(lambda: V.tensor_copy(b_f, pos_b), ub)
            d = vv(shifted, best, best[:, :, 0:1].to_broadcast([P, PHEADS, TOPK]), ALU.subtract, last)
            iota_k = table("iota_k").unsqueeze(1).to_broadcast([P, PAIRS, TOPK])
            for which, at, dst, f in ((0, a_f, first, fa), (1, b_f, second, fb)):
                flat = at.rearrange("p h k -> p (h k)")
                x = vv(same[:, :, :], iota_k, flat.unsqueeze(2).to_broadcast([P, PAIRS, TOPK]), ALU.is_equal, f,
                       as_float, (dve.sem, dve.count))
                s4 = same[:, :, :].rearrange("p (h k) a -> p h k a", h=PHEADS)
                x = vv(s4, s4, half(top_f, which).unsqueeze(2).to_broadcast([P, PHEADS, TOPK, TOPK]), ALU.mult, x)
                looked = dve.do(lambda dst=dst: V.tensor_reduce(dst.rearrange("p h k -> p (h k)"), same[:, :, :], AX.X,
                                                                ALU.add), x, *free_small)
            for _ in range(CAND_BANKS - LATE_BANKS):
                expert_hidden(*early.pop(0))
            ex = activation(shifted, shifted, ACT.Exp, d)
            y = dve.do(lambda: V.tensor_reduce(gate_sum[:, 0, :], shifted, AX.X, ALU.add), ex)
            y = dve.do(lambda: V.reciprocal(gate_sum[:, 1, :], gate_sum[:, 0, :]), y)
            y = vv(gate_w, shifted, gate_sum[:, 1, :].unsqueeze(2).to_broadcast([P, PHEADS, TOPK]), ALU.mult, y)
            chosen_of_tile = (looked, y)
        free_small, pairs_ready = turn_choices(TILES - 1)
        chosen = (dve.sem, dve.count)
        dve_busy[0] = False

        gates = nc.dram_tensor("expert_gates", [GATE_CHUNKS, KEYS, KEYS, GATE_T], F32, kind="Internal").ap()
        staged = Ring([place(f"staged_{n}", 24576 + n * 16384, [KEYS, GATE_T])[:, :, :] for n in range(2)])
        hot_i, hot_high, hot_low = (
            Ring([place(f"{name}_{n}", 57344 + (at + n) * 2048, [4, KEYS], F32R)[:, :, :] for n in range(depth)])
            for name, at, depth in (("hot_i", 0, 4), ("hot_j_high", 4, 3), ("hot_j_low", 7, 3)))
        stored_sem = [sem(f"gates_stored_{n}") for n in range(2)]
        for s in hot_i.slots + hot_high.slots + hot_low.slots + staged.slots:
            s.free = (chosen, pairs_ready, *free_small)
        quads = SEQ // 4
        hot_banks, out_banks, hidden_banks = banks.part(0, 3), banks.part(3, 6), banks.part(6, 8)
        hot = {}

        def one_hots(quad):
            if quad >= quads:
                return
            tok = 4 * quad
            hi_, hj_ = hot_i.next(), hot_banks.next()
            for k in range(4):
                o, i = hi_.ap[:, k, :], pair_t[:, 0, tok + k:tok + k + 1]
                if k < 3:
                    a1 = pool.do(lambda o=o, i=i: G.tensor_scalar(o, table("iota"), i, None, ALU.is_equal),
                                 pairs_ready, *hi_.free)
                else:
                    a2 = vs(o, table("iota"), i, ALU.is_equal, pairs_ready, *hi_.free)
            for k in range(4):
                b = vs(hj_.ap[:, k * P:(k + 1) * P], table("iota"), pair_t[:, 1, tok + k:tok + k + 1], ALU.is_equal,
                       pairs_ready, *hj_.free, s2=pair_t[:, 2, tok + k:tok + k + 1], op1=ALU.mult)
            hot[quad] = hi_, hj_, (a1, a2), b

        def split_hots(quad):
            if quad >= quads:
                return
            hi_, hj_, i_ready, j_ready = hot.pop(quad)
            hh_, hl_ = hot_high.next(), hot_low.next()
            hj_.free = split(hh_.ap, hl_.ap, hj_.ap.rearrange("p (t j) -> p t j", t=4), j_ready, *hh_.free, *hl_.free, low_on=(dve, V))
            hots[quad] = hi_, hh_, hl_, (*i_ready, *hj_.free)

        hots = {}
        def early_steps():
            for g, j in early:
                yield from hidden_steps(g, j, hidden_banks)
                yield

        last_early = [early.pop() for _ in range(6)][::-1]
        ahead = 2 * CHUNKS
        steps, between = early_steps(), len(early) * CHUNKS - ahead
        one_hots(0)
        one_hots(1)
        split_hots(0)
        one_hots(2)
        split_hots(1)
        for _ in range(ahead):
            next(steps)
        for quad in range(quads):
            one_hots(quad + 3)
            split_hots(quad + 2)
            tok = 4 * quad
            chunk = tok // GATE_T
            if tok % GATE_T == 0:
                stage = staged.next()
            hi_, hh_, hl_, there = hots.pop(quad)
            bank = out_banks.next()
            for k in range(4):
                o = bank.ap[:, k * P:(k + 1) * P]
                mm(o, hi_.ap[:, k, :], hh_.ap[:, k, :], True, False, *there, *bank.free)
                done = mm(o, hi_.ap[:, k, :], hl_.ap[:, k, :], False, True, tell=(k == 3))
            hi_.free = hh_.free = hl_.free = (done,)
            t0 = tok % GATE_T
            e = activation(stage.ap[:, :, t0:t0 + 4].rearrange("p j t -> p t j"),
                           bank.ap.rearrange("p (t j) -> p t j", t=4), ACT.Copy, done, *stage.free)
            bank.free = (e,)
            if t0 == GATE_T - 4:
                total = 16 * (chunk // 2 + 1)
                st = act.start_dma(lambda stage=stage, chunk=chunk: A.dma_start(gates[chunk], stage.ap),
                                   stored_sem[chunk % 2], total, e)
                stage.free = (st,)
            for _ in range((quad + 1) * between // quads - quad * between // quads):
                next(steps)
        all_stored = [s.free[0] for s in staged.slots]
        gates_built = (pe.sem, pe.count)

        gate_in = Ring([place(f"gate_in_{n}", 24576 + n * 8192, [GATE_CHUNKS, J * GATE_T])[:, :, :] for n in range(2)])
        weight = Ring([(place(f"weight_high_{n}", 40960 + n * 16384, [J, SEQ], F32R),
                        place(f"weight_low_{n}", 40960 + n * 16384 + 8192, [J, SEQ], F32R)) for n in range(2)])
        gate_sem = [sem(f"gates_loaded_{n}") for n in range(2)]
        for s in weight.slots:
            s.free = (gates_built, *all_stored)
        gate_there, last_read = {}, {}

        def load_gates(at):
            if at >= GROUPS:
                return
            g = ORDER[at]
            s = gate_in.next()
            src = gates[:, :, g * J:(g + 1) * J, :].rearrange("c i j t -> i c (j t)")
            gate_there[g] = (s, act.start_dma(lambda: A.dma_start(s.ap, src), gate_sem[at % 2], 16 * (at // 2 + 1),
                                              *all_stored, *s.free))

        def weigh(at):
            if at >= GROUPS:
                return
            g = ORDER[at]
            slot, a = made["hidden", g]
            gs, there = gate_there[g]
            w = weight.next()
            h = slot.ap.rearrange("p j (c t) -> p j c t", t=GATE_T)
            m = vv(h, h, gs.ap.rearrange("p c (j t) -> p j c t", j=J), ALU.mult, *a, there)
            gs.free = (m,)
            load_gates(at + 2)
            done = split(w.ap[0][:, :, :], w.ap[1][:, :, :], slot.ap, m, *w.free, low_on=(dve, V))
            slot.free = done
            made["weight", g] = (w, done)

        row_sem = [sem(f"row_loaded_{n}") for n in range(4)]

        def load_row(name, first, last, at, k, *after):
            width = row[last].stop - row[first].start
            dst = place(name, at, [width])
            src = t["rows"][0:1, row[first].start:row[last].stop].to_broadcast([P, width])
            return dst, act.start_dma(lambda: A.dma_start(dst[:, :], src), row_sem[k], 16, *after)

        def start_final_norm(hidden_read):
            nonlocal normed, squared
            g_final, g_final_in = load_row("g_final_row", "g_final", "g_final", 0, 0, *hidden_read)
            normed, squared = norm_buffers("final", 4096)
            square, root = rms_stages(lambda n: resid[:, n, :], D, EPS1, lambda n: (added[n],), hidden_read,
                                      on_scalar=True)
            var = {}

            def final_square(tile):
                square(tile)
                var[tile] = made["var"]

            def final_scale(tile):
                r = resid[:, tile, :]
                added[tile] = stt(r, r, stats[:, 8 + tile:9 + tile], g_final[:, :], ALU.mult, ALU.mult,
                                  root(tile, var[tile]), g_final_in)

            return tile_steps([final_square, final_scale] + norm_stages(lambda n: resid[:, n, :], D, EPS2, "g_pre_mix", 0,
                                                                   lambda n: (added[n],)))

        load_gates(0)
        load_gates(1)
        for n, (g, j) in enumerate(last_early):
            if n == 4:
                weigh(0)
            expert_hidden(g, j)
        for at_group, g in enumerate(ORDER):
            weigh(at_group + 1)
            if at_group == GROUPS - 1:
                final_norm = start_final_norm(made["weight", g][1])
            w, w_ready = made["weight", g]
            pair = [take() for _ in range(2)]
            for two in range(0, TILES, 2):
                outs = [(tile, half, banks.next()) for tile in (two, two + 1) for half in range(2)]
                for e, (n, v, there) in enumerate(pair):
                    for tile, half, bank in outs:
                        for j in (2 * e, 2 * e + 1):
                            at = (j % 2) * D + half * 512
                            done = mm3(bank.ap, tuple(h[:, j, tile * P:(tile + 1) * P] for h in w.ap),
                                       tuple(h[:, at:at + 512] for h in v), j == 0, j == J - 1,
                                       *there, *w_ready, *bank.free, tell=(j % 2 == 1))
                        if e == 1:
                            r = resid[:, tile, half * 512:(half + 1) * 512]
                            added[tile] = vv(r, r, bank.ap, ALU.add, done)
                            bank.free = (added[tile],)
                    if two == TILES - 2:
                        last_read[n] = done
                        if at_group < GROUPS - 1:
                            give_back(n, done)
                if at_group == GROUPS - 1 and two == 0:
                    for _ in range(4):
                        next(final_norm)
            w.free = (done,)
            if at_group + AHEAD < GROUPS:
                then = ORDER[at_group + AHEAD]
                if then < SPILLED:
                    reload_hidden(then)
                else:
                    for j in range(J):
                        expert_hidden(then, j)
        experts_done = (pe.sem, pe.count)

        for _ in final_norm:
            pass
        for n, _, _ in pair:
            give_back(n, last_read[n])
        normed, squared = usual_buffers
        for s in normed.slots + squared.slots:
            s.free = made["normed"]
        x_ready = made["normed"]
        normed_tiles = [made["normed", tile] for tile in range(TILES)]
        scaled_all = added[TILES - 1]

        pos_i = place("pos_i", 65536, [TILES], I32)
        pos_f = place("pos_f", 65568, [TILES])
        angle = place("angle", 65600, [TILES, ROT_HALF])
        turns_i = place("turns_i", 65728, [TILES, ROT_HALF], I32)
        turns = place("turns", 65856, [TILES, ROT_HALF])
        over = place("over", 65984, [TILES, ROT_HALF])
        sin_a = place("sin_a", 66112, [TILES, ROT_HALF])
        cos_a = place("cos_a", 66240, [TILES, ROT_HALF])
        rot = place("rot", 66368, [4, 2 * HEADS2 * ROT_HALF])
        pos_sem = sem("positions_loaded")
        pos_in = act.start_dma(lambda: A.dma_start(pos_i[:, :], t["positions"]), pos_sem, 16, experts_done)
        times_never = place("times_never", 77952, [2 * SEQ])
        masks_sem = sem("dilated_masks_loaded")
        masks_in = act.start_dma(lambda: A.dma_start(times_never[:, :], t["dilated_masks"]), masks_sem, 16, *x_ready)
        times, never = times_never[:, 0:SEQ], times_never[:, SEQ:2 * SEQ]
        TWO_PI = 2 * np.pi
        part1 = 6.28125
        part2 = float(np.float32(np.round((TWO_PI - part1) * 2 ** 21) / 2 ** 21))
        part3 = float(np.float32(TWO_PI - part1 - part2))
        PI_IN = float(np.nextafter(np.float32(np.pi), np.float32(0)))
        a = dve.do(lambda: V.tensor_copy(pos_f[:, :], pos_i[:, :]), pos_in)
        a = vv(angle[:, :, :], pos_f[:, :].unsqueeze(2).to_broadcast([P, TILES, ROT_HALF]),
               table("inv_freq").unsqueeze(1).to_broadcast([P, TILES, ROT_HALF]), ALU.mult, a, small)
        a = vs(turns[:, :, :], angle[:, :, :], 1 / TWO_PI, ALU.mult, a)
        a = dve.do(lambda: V.tensor_copy(turns_i[:, :, :], turns[:, :, :]), a)
        a = dve.do(lambda: V.tensor_copy(turns[:, :, :], turns_i[:, :, :]), a)
        for part in (part1, part2, part3):
            a = stt(angle[:, :, :], turns[:, :, :], -part, angle[:, :, :], ALU.mult, ALU.add, a)

        def wrap(x, a):
            for limit, op, step in ((float(np.pi), ALU.is_gt, -TWO_PI), (-float(np.pi), ALU.is_lt, TWO_PI)):
                a = vs(over[:, :, :], x, limit, op, a, s2=step, op1=ALU.mult)
                a = vv(x, x, over[:, :, :], ALU.add, a)
            return vs(x, x, PI_IN, ALU.min, a, s2=-PI_IN, op1=ALU.max)

        a = vs(cos_a[:, :, :], angle[:, :, :], float(np.pi / 2), ALU.add, a)
        a = wrap(angle[:, :, :], a)
        b = activation(sin_a[:, :, :], angle[:, :, :], ACT.Sin, a)
        a = wrap(cos_a[:, :, :], a)
        rope_ready = activation(cos_a[:, :, :], cos_a[:, :, :], ACT.Sin, a)

        qk = place("qk", 0, [2, TILES, W2])
        v2 = place("v2", 16384, [TILES, W2])
        u_gate = place("u_gate", 24576, [TILES, W2])
        v_gate = place("v_gate", 32768, [TILES, W2])
        q2t = place("q2t", 40960, [4, SEQ])
        k2t = place("k2t", 49152, [4, SEQ])

        def qk_finish(which):
            def finish(tile, bank, done):
                made["qk", which, tile] = activation(qk[:, which, tile, :], bank, ACT.Copy, done, scaled_all, *x_ready)
                return made["qk", which, tile]
            return finish

        def v_finish(tile, bank, done):
            made["v2", tile] = activation(v2[:, tile, :], bank, ACT.Copy, done, *x_ready)
            return made["v2", tile]

        def gelu_finish(dst, sums):
            def finish(tile, bank, done):
                kw = dict(accum_out=sums[:, tile:tile + 1]) if sums is not None else {}
                made[id(dst), tile] = activation(dst[:, tile, :], bank, ACT.Gelu, done, *x_ready, **kw)
                return made[id(dst), tile]
            return finish

        token_major(xt, 2, qk_finish(0), ready=lambda chunk, tile: normed_tiles[tile])
        token_major(xt, 2, qk_finish(1))
        for tile in range(TILES):
            x = qk[:, :, tile, :].rearrange("p w (h f) -> p w h f", h=HEADS2)
            x1, x2 = x[:, :, :, 0:ROT_HALF], x[:, :, :, ROT_HALF:2 * ROT_HALF]
            cs, sn = (z[:, tile, :].unsqueeze(1).unsqueeze(1).to_broadcast([P, 2, HEADS2, ROT_HALF])
                      for z in (cos_a, sin_a))
            r = [rot[:, k, :].rearrange("p (w h f) -> p w h f", w=2, h=HEADS2) for k in range(4)]
            after = (made["qk", 0, tile], made["qk", 1, tile], rope_ready, (dve.sem, dve.count))
            m = [vv(r[k], y, z, ALU.mult, *after) for k, (y, z) in enumerate(((x1, cs), (x2, sn), (x2, cs), (x1, sn)))]
            vv(x1, r[0], r[1], ALU.subtract, *m)
            made["rot", tile] = vv(x2, r[2], r[3], ALU.add, *m)
        token_major(xt, 2, v_finish)
        for which, dst in ((0, q2t), (1, k2t)):
            for tile in range(TILES):
                bank = banks.next()
                for c in range(4):
                    done = turn(bank.ap[:, c * P:(c + 1) * P], qk[:, which, tile, c * P:(c + 1) * P],
                                made["rot", tile], *bank.free, tell=(c == 3))
                made["t", which, tile] = activation(dst[:, :, tile * P:(tile + 1) * P],
                                                    bank.ap.rearrange("p (c t) -> p c t", c=4), ACT.Copy, done)
                bank.free = (made["t", which, tile],)
        qk_turned = done
        v_mean = stats[:, 12:16]
        token_major(xt, 2, gelu_finish(u_gate, None))
        token_major(xt, 2, gelu_finish(v_gate, v_mean))
        projected = (pe.sem, pe.count)

        score2 = Ring([place(f"score2_{n}", 57344 + n * 4096, [2, SEQ])[:, :, :] for n in range(3)])
        prob2 = Ring([place(f"prob2_{n}", 69632 + n * 4096, [2, SEQ])[:, :, :] for n in range(2)])
        stat2 = Ring([place(f"stat2_{n}", 77824 + n * 32, [3, 2])[:, :, :] for n in range(4)])
        o2 = place("o2", 0, [TILES, W2])
        units2 = [(tile, c) for tile in range(TILES) for c in range(4)]
        for s in score2.slots + prob2.slots:
            s.free = (*x_ready, rope_ready, made["rot", TILES - 1])

        def scores2(u):
            tile, c = units2[u]
            n = (tile + 1) * P
            two = []
            for par in range(2):
                rows = slice(par * DH, (par + 1) * DH)
                bank = attn_banks.next()
                done = mm(bank.ap[:, 0:n], q2t[rows, c, tile * P:(tile + 1) * P], k2t[rows, c, 0:n], True, True,
                          made["t", 0, tile], *(made["t", 1, k] for k in range(tile + 1)), *bank.free, tell=True)
                two.append((bank, done))
            state[u] = dict(s=score2.next(), st=stat2.next(), n=n, banks=two)

        def maximum2(u):
            x = state[u]
            s, st, n = x["s"], x["st"], x["n"]
            for par, (bank, done) in enumerate(x["banks"]):
                masked = stt(s.ap[:, par, 0:n], bank.ap[:, 0:n], SCALE, never[:, SEQ - n:], ALU.mult, ALU.add,
                             done, masks_in, *s.free)
                bank.free = (masked,)
            x["m"] = dve.do(lambda: V.tensor_reduce(st.ap[:, 0, :], s.ap[:, :, 0:n], AX.X, ALU.max, negate=True),
                            masked, *st.free)

        def exponents2(u):
            x = state[u]
            s, n = x["s"], x["n"]
            for par in range(2):
                x["e"] = activation(s.ap[:, par, 0:n], s.ap[:, par, 0:n], ACT.Exp, x["m"],
                                    bias=x["st"].ap[:, 0, par:par + 1])

        def probabilities2(u):
            x = state[u]
            s, st, n = x["s"], x["st"], x["n"]
            for par in range(2):
                p = dve.do(lambda par=par: V.tensor_tensor_reduce(
                    out=s.ap[:, par, 0:n], in0=s.ap[:, par, 0:n], in1=times[:, SEQ - n:], scale=1.0,
                    scalar=0.0, op0=ALU.mult, op1=ALU.add, accum_out=st.ap[:, 1, par:par + 1]), x["e"])
            x["p"] = p
            x["inv"] = dve.do(lambda: V.reciprocal(st.ap[:, 2, :], st.ap[:, 1, :]), p)

        def turn_probabilities2(u):
            x = state[u]
            s, n = x["s"], x["n"]
            pt = x["pt"] = prob2.next()
            for par in range(2):
                bank = attn_banks.next()
                for kb in range(n // P):
                    done = turn(bank.ap[:, kb * P:(kb + 1) * P], s.ap[:, par, kb * P:(kb + 1) * P], x["p"],
                                *bank.free, tell=(kb == n // P - 1))
                x["c"] = activation(pt.ap[:, par, 0:n], bank.ap[:, 0:n], ACT.Copy, done, *pt.free)
                bank.free = (x["c"],)
            s.free = (done,)

        def values2(u):
            x = state.pop(u)
            tile, cc = units2[u]
            bank = attn_banks.next()
            for par in range(2):
                head = 2 * cc + par
                for kb in range(tile + 1):
                    done = mm(bank.ap[:, par * DH:(par + 1) * DH], x["pt"].ap[:, par, kb * P:(kb + 1) * P],
                              v2[:, kb, head * DH:(head + 1) * DH], kb == 0, kb == tile, x["c"],
                              made["v2", kb], *bank.free, tell=(kb == tile))
            x["pt"].free = (done,)
            o = vv(o2[:, tile, cc * P:(cc + 1) * P].rearrange("p (h f) -> p h f", h=2),
                   bank.ap[:, 0:P].rearrange("p (h f) -> p h f", h=2),
                   x["st"].ap[:, 2, :].unsqueeze(2).to_broadcast([P, 2, DH]), ALU.mult, done, x["inv"], qk_turned)
            bank.free = x["st"].free = (o,)
            made["o2", tile] = o

        ln_rows, ln_rows_in = load_row("ln_rows", "ln_gain", "ln_bias", 12288, 1, qk_turned)
        w_sp = place("w_sp", 8192, [8, P])
        sp_sem = sem("spatial_loaded")
        w_sp_in = act.start_dma(lambda: A.dma_start(w_sp[:, :, :], t["w_spatial"]), sp_sem, 16, qk_turned)
        causal = pool.do(lambda: G.affine_select(out=w_sp[:, :, :], in_=w_sp[:, :, :], compare_op=ALU.is_ge, fill=0.0,
                                                 base=0, pattern=[[0, 8], [1, P]], channel_multiplier=-1), w_sp_in)
        square_v = Ring([place(f"square_v_{n}", 82048 + n * 1024, [W2 // 2]).bitcast(BF16)[:, :] for n in range(2)])

        def centre(tile):
            if tile == 0:
                made["mean"] = vs(v_mean, v_mean, -1.0 / W2, ALU.mult, made[id(v_gate), TILES - 1])
            v, s = v_gate[:, tile, :], square_v.next()
            a = vs(v, v, v_mean[:, tile:tile + 1], ALU.add, made["mean"], made[id(v_gate), tile])
            a = dve.do(lambda: V.tensor_tensor_reduce(out=s.ap, in0=v, in1=v, scale=1.0, scalar=0.0, op0=ALU.mult,
                                                      op1=ALU.add, accum_out=stats[:, tile:tile + 1]), a, *s.free)
            s.free = (a,)
            made["squares"] = a

        def deviation():
            a = vs(stats[:, 4:8], stats[:, 0:4], 1.0 / W2, ALU.mult, made["squares"], s2=LN_EPS, op1=ALU.add)
            a = activation(stats[:, 4:8], stats[:, 4:8], ACT.Sqrt, a)
            made["deviation"] = dve.do(lambda: V.reciprocal(stats[:, 8:12], stats[:, 4:8]), a)

        def gain(tile):
            v = v_gate[:, tile, :]
            b = stt(v, v, stats[:, 8 + tile:9 + tile], ln_rows[:, 0:W2], ALU.mult, ALU.mult, made["deviation"],
                    ln_rows_in)
            made["v_normed"] = vv(v, v, ln_rows[:, W2:2 * W2], ALU.add, b)

        def mix(g):
            bank = attn_banks.next()
            done = mm(bank.ap[:, 0:256], w_sp[:, g, :], v_gate[:, :, g * DH:(g + 1) * DH], True, True,
                      made["v_normed"], causal, *bank.free, tell=True)
            u = u_gate[:, :, g * DH:(g + 1) * DH]
            made["gated"] = stt(u, bank.ap[:, 0:256].rearrange("p (n f) -> p n f", n=TILES), column("b_spatial", g), u,
                                ALU.add, ALU.mult, done, *(made[id(u_gate), k] for k in range(TILES)))
            bank.free = (made["gated"],)

        gating = [lambda: centre(0), lambda: centre(1), lambda: centre(2), lambda: centre(3), deviation,
                  lambda: gain(0), lambda: gain(1), lambda: gain(2), lambda: gain(3),
                  *((lambda g=g: (mix(g), mix(g + 1))) for g in range(0, 8, 2))]

        attend(len(units2), scores2, maximum2, exponents2, probabilities2, turn_probabilities2, values2,
               iter(()), 0, between=lambda s: gating[s]() if s < len(gating) else None)
        gated = made["gated"]
        attended2 = (pe.sem, pe.count)
        attended2_d = (dve.sem, dve.count)

        gate_norm = norm_stages(lambda n: u_gate[:, n, :], W2, EPS2, "g_out", 4, lambda n: (gated,),
                                dst_free=(projected,), extra=(attended2,))
        attn_norm = norm_stages(lambda n: o2[:, n, :], W2, EPS2, "g_out", 0, lambda n: (made["o2", n],),
                                dst_free=(projected,), extra=(attended2,))
        in_turn([lambda n, f=f, g=g: (f if n < TILES else g)(n % TILES) for f, g in zip(gate_norm, attn_norm)],
                2 * TILES)
        x_ready = made["normed"]
        normed_tiles = [made["normed", tile] for tile in range(TILES)]
        y2 = place("y2", 0, [TILES, D])
        turned_all = (pe.sem, pe.count)
        g_pm, g_pm_in = load_row("g_post_mix_row", "g_post_mix", "g_post_mix", 61440, 2, attended2, attended2_d,
                                 turned_all)

        y_in = {}

        def y_finish(half):
            def finish(tile, bank, done):
                y_in[tile] = activation(y2[:, tile, half * 512:(half + 1) * 512], bank, ACT.Copy, done)
                return y_in[tile]
            return finish

        token_major(xt, 2, y_finish(0), ready=lambda chunk, tile: normed_tiles[tile])

        def add_normed(y, gain, gain_in, tile, inv):
            a = stt(y, y, stats[:, 8 + tile:9 + tile], gain[:, :], ALU.mult, ALU.mult, inv, gain_in)
            return vv(resid[:, tile, :], resid[:, tile, :], y, ALU.add, a)

        def add_stages(y, gain, gain_in, srcs_ready):
            square, root = rms_stages(y, D, EPS2, srcs_ready, on_scalar=True)
            var = {}

            def stats_of(tile):
                square(tile)
                var[tile] = made["var"]

            def add(tile):
                added[tile] = add_normed(y(tile), gain, gain_in, tile, root(tile, var[tile]))

            return [stats_of, add]

        ffn_steps = tile_steps(add_stages(lambda n: y2[:, n, :], g_pm, g_pm_in, lambda n: (y_in[n],))
                          + norm_stages(lambda n: resid[:, n, :], D, EPS2, "g_pre_ffn", 0, lambda n: (added[n],)))
        token_major(xt, 2, y_finish(1), by_tile=True, ready=lambda chunk, tile: normed_tiles[tile], steps=ffn_steps)

        x_ready = made["normed"]
        ff = (place("ff_high", 0, [FF_PARTS[0], SEQ], F32R), place("ff_low", 24576, [FF_PARTS[0], SEQ], F32R))
        down = place("down", 49152, [TILES, D])
        act_g = Ring([place(f"act_g_{n}", 65536 + n * 2048, [SEQ])[:, :] for n in range(4)])
        normed_done = (*x_ready, (pe.sem, pe.count), (dve.sem, dve.count))
        g_pf, g_pf_in = load_row("g_post_ffn_row", "g_post_ffn", "g_post_ffn", 73728, 3, *normed_done)
        for s in act_g.slots:
            s.free = normed_done
        ff_free = normed_done
        out_sem = sem("out_stored")
        down_in = {}

        def store(tile):
            sp.start_dma(lambda: S.dma_start(out[tile * P:(tile + 1) * P, :], resid[:, tile, :]), out_sem, 0,
                         added[tile])

        last_steps = tile_steps(add_stages(lambda n: down[:, n, :], g_pf, g_pf_in, lambda n: (down_in[n],)) + [store])
        for part, chunks in enumerate(FF_PARTS):
            for pair in range(chunks // 2):
                silu = []
                for kind in range(2):
                    n, w, there = take()
                    for e in range(2):
                        bank = banks.next()
                        for k in range(CHUNKS):
                            done = mm3(bank.ap, tuple(h[:, k * 256 + e * P:k * 256 + (e + 1) * P] for h in w),
                                       tuple(h[:, k, :] for h in xt), k == 0, k == CHUNKS - 1, *there, *x_ready,
                                       *bank.free, tell=(k == CHUNKS - 1))
                        if e == 1:
                            give_back(n, done)
                        if kind == 0:
                            s = act_g.next()
                            a = activation(s.ap, bank.ap, ACT.Silu, done, *s.free)
                            bank.free = (a,)
                            silu.append((s, a))
                        else:
                            s, a = silu[e]
                            m = vv(s.ap, s.ap, bank.ap, ALU.mult, a, done)
                            bank.free = (m,)
                            c = 2 * pair + e
                            s.free = made["ff", c] = split(ff[0][:, c, :], ff[1][:, c, :], s.ap, m, *ff_free,
                                                      low_on=(dve, V))

            def down_finish(half, part=part):
                def finish(tile, bank, done):
                    d = down[:, tile, half * 512:(half + 1) * 512]
                    if part == 0:
                        down_in[tile] = activation(d, bank, ACT.Copy, done)
                    else:
                        down_in[tile] = vv(d, d, bank, ALU.add, done, down_in[tile])
                    return down_in[tile]
                return finish

            for half in range(2):
                token_major(ff, -(-chunks // 4), down_finish(half), k_last=(chunks - 1) % 4 + 1,
                            by_tile=(part == half == 1), ready=lambda chunk, tile: made["ff", chunk],
                            steps=last_steps if part == half == 1 else None)
            ff_free = ((pe.sem, pe.count),)

        sp.do(None, (out_sem, 16 * TILES), *all_stored, *(made["spilled", g] for g in range(SPILLED)), tell=False)
        assert taken[0] == len(items), (taken[0], len(items))

        block = ctx.enter_context(nc.Block())

        @block.sync
        def _(e):
            sp.run(e)

        @block.scalar
        def _(e):
            act.run(e)

        @block.vector
        def _(e):
            dve.run(e)

        @block.gpsimd
        def _(e):
            pool.run(e)

        @block.tensor
        def _(e):
            pe.run(e)


WEIGHTS_BEFORE_PEER = 4 + 1 + 4 + 2 + 12 + 4 + 8


def column_items(w, c0, c1, k=CHUNKS):
    return [w[:, c:c + 256].reshape(k, P, 256).transpose(1, 0, 2).reshape(P, k * 256) for c in range(c0, c1, 256)]


def row_items(w, c0, c1):
    out = []
    for c in range(c0, c1, 512):
        for r in range(0, w.shape[0], 4 * P):
            x = w[r:r + 4 * P, c:c + 512]
            out.append(x.reshape(-1, P, 512).transpose(1, 0, 2).reshape(P, -1))
    return out


def lay_out(i):
    w_in = i["w_in"][0]
    k0, v0 = Q_W, Q_W + KV_W
    p0 = v0 + KV_W
    ga0 = p0 + POOL_W
    gp0 = ga0 + D
    q_order = np.arange(Q_W).reshape(KV_HEADS, CHUNKS, DH).transpose(1, 0, 2).reshape(-1)
    items = column_items(w_in[:, q_order], 0, Q_W)
    items.append(np.concatenate([w_in[:, c:c + KV_W].reshape(CHUNKS, P, KV_W).transpose(1, 0, 2).reshape(P, -1)
                                 for c in (k0, v0)], axis=1))
    items += column_items(w_in, p0, ga0)
    items += column_items(i["w_attn_up"][0][q_order], 0, D)
    ga, gp, up = column_items(w_in, ga0, gp0), column_items(w_in, gp0, gp0 + D), column_items(i["w_pool_up"][0], 0, D, 4)
    for c in range(4):
        items += [ga[c], gp[c], up[c]]
    items += row_items(i["w_o"][0], 0, D)
    items += column_items(i["w_query"][0], 0, 2048)
    assert len(items) == WEIGHTS_BEFORE_PEER
    items += row_items(i["w_in_2"][0], 0, 5 * W2)
    items += row_items(i["w_out_2"][0], 0, D)
    gate, up = column_items(i["w_gate_2"][0], 0, FF), column_items(i["w_up_2"][0], 0, FF)
    at = 0
    for chunks in FF_PARTS:
        for c in range(at // 2, (at + chunks) // 2):
            items += [gate[c], up[c]]
        items += row_items(i["w_down_2"][0][at * P:(at + chunks) * P], 0, D)
        at += chunks
    weights = np.zeros((len(items), P, ITEM), np.float32)
    for n, x in enumerate(items):
        weights[n, :, :x.shape[1]] = x

    def cols(v):
        return v.reshape(-1, P).T

    b = i["b_in"][0]
    columns = [cols(b[:Q_W][q_order]), cols(b[k0:v0]), cols(b[p0:ga0]), cols(b[ga0:gp0]), cols(b[gp0:]),
               cols(i["ln_mix_g"][0]), cols(i["ln_ffn_g"][0]), cols(i["pool_scale"][0]), cols(i["pre_mix_norm_2"][0]),
               cols(i["attn_out_norm_2"][0]), cols(i["sgu_out_norm_2"][0]), cols(i["pre_ffn_norm_2"][0]),
               i["sgu_b_spatial_2"][0].T]
    rows = [b[v0:p0], i["attn_sinks"][0], i["ln_final_g"], i["post_mix_norm_2"][0], i["sgu_ln_gain_2"][0],
            i["sgu_ln_bias_2"][0], i["post_ffn_norm_2"][0]]
    u = i["u_experts"][0].reshape(KEYS, KEYS // 2, 2, CHUNKS, P)
    return {
        "x": i["x"][0],
        "positions": np.ascontiguousarray(i["positions_2"][0].reshape(TILES, P).T),
        "weights": weights,
        "u_tiles": np.ascontiguousarray(u.transpose(1, 4, 2, 3, 0)).reshape(KEYS // 2, P, ITEM),
        "v_experts": i["v_experts"][0],
        "columns": np.ascontiguousarray(np.concatenate(columns, axis=1)),
        "rows": np.ascontiguousarray(np.concatenate(rows)[None]),
        "tables": shape_tables()[0],
        "dilated_masks": shape_tables()[1],
        "w_pool_grp": np.ascontiguousarray(i["w_pool_grp"][0].transpose(1, 0, 2)),
        "sub_keys": np.ascontiguousarray(i["sub_keys"][0].reshape(2 * PHEADS, KEYS, P).transpose(2, 0, 1)),
        "w_spatial": np.ascontiguousarray(i["sgu_w_spatial_2"][0].transpose(2, 0, 1)),
    }


def shape_tables():
    q, k = np.arange(P)[:, None], np.arange(2 * P)[None, :] - P
    near = (q - k >= 0) & (q - k < P)
    dist = q - (np.arange(SEQ)[None, :] - (SEQ - P))
    times = ((dist >= 0) & (dist <= 128)) * 1.0 + ((dist >= 0) & (dist % 4 == 0)) + ((dist >= 0) & (dist % 16 == 0))
    count = np.minimum(np.arange(1, PAD + 1)[None, :], np.array(WINDOWS)[:, None]).astype(np.float32)
    freq = np.float32(500000.0) ** (-np.arange(0, 16, 2, dtype=np.float32) / np.float32(16))
    every = lambda r: np.broadcast_to(np.asarray(r, np.float32).reshape(1, -1), (P, np.size(r)))
    parts = [np.eye(P), every(np.arange(P)), every(np.arange(TOPK)), np.where(near, 0.0, MASKED), every(1 / count),
             every(freq)]
    masks = [times, np.where(times > 0, 0.0, MASKED)]
    return tuple(np.ascontiguousarray(np.concatenate(x, axis=1).astype(np.float32)) for x in (parts, masks))


def kernel(**inputs):
    import concourse.bacc as bacc
    from concourse.bass_utils import run_bass_kernel_spmd as run

    nc = bacc.Bacc("TRN2", target_bir_lowering=False, num_devices=1)
    arrays, t = {}, {}
    for name, a in lay_out({k: np.asarray(v) for k, v in inputs.items()}).items():
        arrays[f"in_{name}"] = a
        t[name] = nc.dram_tensor(f"in_{name}", a.shape, mybir.dt.from_np(a.dtype), kind="ExternalInput").ap()
    out = nc.dram_tensor("out_x", (SEQ, D), F32, kind="ExternalOutput").ap()
    build(nc, t, out)
    r = run(nc, [arrays], core_ids=[0])
    return r.results[0]["out_x"].reshape(1, SEQ, D)
```
